# Optimizing a Trainium2 kernel written in Bass

```python
import math
import jax
import jax.numpy as jnp
from jax import lax
import numpy as np

D_MODEL = 1024
BATCH = 1
SEQ = 512
DEPTH = 2

N_EVEN = (DEPTH + 1) // 2
N_ODD = DEPTH // 2

HGRN_HEADS = 4
HGRN_DK = 128
HGRN_DV = 128
HGRN_QK_WIDTH = HGRN_HEADS * HGRN_DK
HGRN_V_WIDTH = HGRN_HEADS * HGRN_DV
HGRN_CHUNK = 32
S5_WIDTH = D_MODEL // 2
S5_GROUP = 16
S5_GROUPS = S5_WIDTH // S5_GROUP
S5_STATE = 64
EVEN_PROJ = 2 * HGRN_QK_WIDTH + 2 * HGRN_V_WIDTH + S5_WIDTH
EVEN_MIX = HGRN_V_WIDTH + S5_WIDTH
GDN_HEADS = 8
GDN_DK = 128
GDN_DV = 128
GDN_QK = GDN_HEADS * GDN_DK
GDN_V = GDN_HEADS * GDN_DV
GDN_CONV = 4
GDN_CHUNK = 64
ODD_PROJ = 2 * GDN_QK + 2 * GDN_V + 2 * GDN_HEADS
PEER_HEADS = 8
PEER_NKEYS = 128
PEER_EXPERTS = PEER_NKEYS * PEER_NKEYS
PEER_DKEY = 256
PEER_DHALF = PEER_DKEY // 2
PEER_TOPK = 16
PEER_BLOCK = 128

RMS_EPS = 1e-6
L2_EPS = 1e-6

kernel_name = 'hybrid_hgrn2_s5_gdn_peer'

def rmsnorm(x, w):
    x32 = x.astype(jnp.float32)
    y = x32 * lax.rsqrt(jnp.mean(x32 * x32, axis=-1, keepdims=True) + RMS_EPS)
    return (y * w.astype(jnp.float32)).astype(x.dtype)

def l2norm(x):
    return x * lax.rsqrt(jnp.sum(x * x, axis=-1, keepdims=True) + L2_EPS)

def to_chunks(t, c):
    b, s, h, d = t.shape
    return t.reshape(b, s // c, c, h, d).transpose(1, 0, 3, 2, 4)

def from_chunks(t):
    n, b, h, c, d = t.shape
    return t.transpose(1, 0, 3, 2, 4).reshape(b, n * c, h, d)

def scalar_chunks(t, c):
    b, s, h = t.shape
    return t.reshape(b, s // c, c, h).transpose(1, 0, 3, 2)

def hgrn2_mixer(q_raw, f_raw, i_raw, g_raw, lower_bound, gn_w):
    bsz, s, _ = q_raw.shape
    c = HGRN_CHUNK
    hk = (bsz, s, HGRN_HEADS, HGRN_DK)
    hv = (bsz, s, HGRN_HEADS, HGRN_DV)
    lb = lower_bound.astype(jnp.float32).reshape(HGRN_HEADS, HGRN_DK)
    q = jax.nn.silu(q_raw.reshape(hk)) * (HGRN_DK ** -0.5)
    f = lb + (1.0 - lb) * jax.nn.sigmoid(f_raw.reshape(hk))
    qc = to_chunks(q, c)
    kc = to_chunks(1.0 - f, c)
    vc = to_chunks(i_raw.reshape(hv), c)
    cum = jnp.cumsum(to_chunks(jnp.log(f), c), axis=3)
    cum_last = cum[:, :, :, -1:, :]
    q_e = qc * jnp.exp(cum)
    k_e = kc * jnp.exp(-cum)
    k_dec = kc * jnp.exp(cum_last - cum)
    tot = jnp.exp(cum_last[:, :, :, 0, :])
    causal = jnp.tril(jnp.ones((c, c), dtype=bool))
    att = jnp.where(causal, jnp.einsum('nbhtd,nbhsd->nbhts', q_e, k_e), 0.0)
    o_intra = jnp.einsum('nbhts,nbhse->nbhte', att, vc)

    def step(state, inp):
        q_n, k_n, v_n, tot_n = inp
        o_n = jnp.einsum('bhtd,bhde->bhte', q_n, state)
        state = tot_n[..., None] * state + jnp.einsum('bhtd,bhte->bhde', k_n, v_n)
        return state, o_n

    s0 = jnp.zeros((bsz, HGRN_HEADS, HGRN_DK, HGRN_DV), jnp.float32)
    _, o_inter = lax.scan(step, s0, (q_e, k_dec, vc, tot))
    o = from_chunks(o_intra + o_inter)
    o = rmsnorm(o, gn_w) * jax.nn.silu(g_raw.reshape(hv))
    return o.reshape(bsz, s, HGRN_V_WIDTH)

def _complex_affine_combine(e1, e2):
    a1r, a1i, b1r, b1i = e1
    a2r, a2i, b2r, b2i = e2
    ar = a1r * a2r - a1i * a2i
    ai = a1r * a2i + a1i * a2r
    br = a2r * b1r - a2i * b1i + b2r
    bi = a2r * b1i + a2i * b1r + b2i
    return (ar, ai, br, bi)

def s5_mixer(u, a_re, a_im, log_dt, b_re, b_im, c_re, c_im, d_skip, glu_w):
    f32 = jnp.float32
    bsz, s, _ = u.shape
    a_re, a_im, b_re, b_im, c_re, c_im = (t.astype(f32) for t in (a_re, a_im, b_re, b_im, c_re, c_im))
    ug = u.reshape(bsz, s, S5_GROUPS, S5_GROUP)
    dt = jnp.exp(log_dt.astype(f32))[:, None]
    mag = jnp.exp(a_re * dt)
    abar_re = mag * jnp.cos(a_im * dt)
    abar_im = mag * jnp.sin(a_im * dt)
    den = a_re * a_re + a_im * a_im
    coef_re = ((abar_re - 1.0) * a_re + abar_im * a_im) / den
    coef_im = (abar_im * a_re - (abar_re - 1.0) * a_im) / den
    bb_re = coef_re[..., None] * b_re - coef_im[..., None] * b_im
    bb_im = coef_re[..., None] * b_im + coef_im[..., None] * b_re
    bu_re = jnp.einsum('bsgp,gnp->bsgn', ug, bb_re)
    bu_im = jnp.einsum('bsgp,gnp->bsgn', ug, bb_im)
    shape = (1, s, S5_GROUPS, S5_STATE)
    elems = (jnp.broadcast_to(abar_re, shape), jnp.broadcast_to(abar_im, shape), bu_re, bu_im)
    _, _, x_re, x_im = lax.associative_scan(_complex_affine_combine, elems, axis=1)
    y = (jnp.einsum('bsgn,gpn->bsgp', x_re, c_re) - jnp.einsum('bsgn,gpn->bsgp', x_im, c_im)
         + d_skip.astype(f32) * ug)
    y = jax.nn.gelu(y.reshape(bsz, s, S5_WIDTH), approximate=False)
    return y * jax.nn.sigmoid(y @ glu_w.astype(f32))

def gated_deltanet_mixer(qkv_raw, z_raw, beta_raw, a_raw, conv_w, a_log, dt_bias, gn_w):
    f32 = jnp.float32
    bsz, s, ch = qkv_raw.shape
    c = GDN_CHUNK
    qkv = lax.conv_general_dilated(qkv_raw, conv_w.astype(f32)[:, None, :], window_strides=(1,),
                                   padding=[(GDN_CONV - 1, 0)], dimension_numbers=('NWC', 'WIO', 'NWC'),
                                   feature_group_count=ch)
    qkv = jax.nn.silu(qkv)
    q, k, v = jnp.split(qkv, [GDN_QK, 2 * GDN_QK], axis=-1)
    q = l2norm(q.reshape(bsz, s, GDN_HEADS, GDN_DK)) * (GDN_DK ** -0.5)
    k = l2norm(k.reshape(bsz, s, GDN_HEADS, GDN_DK))
    v = v.reshape(bsz, s, GDN_HEADS, GDN_DV)
    beta = jax.nn.sigmoid(beta_raw)
    g = -jnp.exp(a_log.astype(f32)) * jax.nn.softplus(a_raw + dt_bias.astype(f32))
    qc, kc, vc = to_chunks(q, c), to_chunks(k, c), to_chunks(v, c)
    bc = scalar_chunks(beta, c)[..., None]
    decay = jnp.cumsum(scalar_chunks(g, c), axis=-1)
    incl = jnp.tril(jnp.ones((c, c), dtype=bool))
    strict = jnp.tril(jnp.ones((c, c), dtype=bool), -1)
    diff = decay[..., :, None] - decay[..., None, :]
    lmask = jnp.where(incl, jnp.exp(jnp.where(incl, diff, 0.0)), 0.0)
    kb = kc * bc
    a_mat = jnp.where(strict, jnp.einsum('nbhtd,nbhsd->nbhts', kb, kc) * lmask, 0.0)
    eye = jnp.eye(c, dtype=a_mat.dtype)
    t_inv = lax.linalg.triangular_solve(a_mat + eye, jnp.broadcast_to(eye, a_mat.shape),
                                        left_side=True, lower=True)
    value = jnp.einsum('nbhts,nbhse->nbhte', t_inv, vc * bc)
    k_cum = jnp.einsum('nbhts,nbhsd->nbhtd', t_inv, kb * jnp.exp(decay)[..., None])
    attn = jnp.einsum('nbhtd,nbhsd->nbhts', qc, kc) * lmask
    q_dec = qc * jnp.exp(decay)[..., None]
    k_tail = kc * jnp.exp(decay[..., -1:] - decay)[..., None]
    tot = jnp.exp(decay[..., -1])

    def step(state, inp):
        value_n, kcum_n, attn_n, qdec_n, ktail_n, tot_n = inp
        v_new = value_n - jnp.einsum('bhtd,bhde->bhte', kcum_n, state)
        o_n = jnp.einsum('bhtd,bhde->bhte', qdec_n, state) + jnp.einsum('bhts,bhse->bhte', attn_n, v_new)
        state = tot_n[..., None, None] * state + jnp.einsum('bhtd,bhte->bhde', ktail_n, v_new)
        return state, o_n

    s0 = jnp.zeros((bsz, GDN_HEADS, GDN_DK, GDN_DV), f32)
    _, o = lax.scan(step, s0, (value, k_cum, attn, q_dec, k_tail, tot))
    o = from_chunks(o)
    o = rmsnorm(o, gn_w) * jax.nn.silu(z_raw.reshape(bsz, s, GDN_HEADS, GDN_DV))
    return o.reshape(bsz, s, GDN_V)

def peer_ffn(xn, w_q, sub_keys, u_tab, v_tab):
    bsz, s, d = xn.shape
    n_tok = bsz * s
    xt = xn.reshape(n_tok, d)
    q = (xt @ w_q).astype(jnp.float32).reshape(n_tok, PEER_HEADS, 2, PEER_DHALF)
    scores = jnp.einsum('thcd,ckd->thck', q, sub_keys.astype(jnp.float32))
    top_s, top_i = lax.top_k(scores, PEER_TOPK)
    n_cand = PEER_TOPK * PEER_TOPK
    cand_s = (top_s[:, :, 0, :, None] + top_s[:, :, 1, None, :]).reshape(n_tok, PEER_HEADS, n_cand)
    cand_e = (top_i[:, :, 0, :, None] * PEER_NKEYS + top_i[:, :, 1, None, :]).reshape(n_tok, PEER_HEADS, n_cand)
    sel_s, sel_pos = lax.top_k(cand_s, PEER_TOPK)
    expert_id = jnp.take_along_axis(cand_e, sel_pos, axis=-1).reshape(n_tok, PEER_HEADS * PEER_TOPK)
    gate = jax.nn.softmax(sel_s, axis=-1).reshape(n_tok, PEER_HEADS * PEER_TOPK)
    nb = n_tok // PEER_BLOCK

    def block(args):
        xb, eb, gb = args
        act = jax.nn.gelu(jnp.einsum('td,tkd->tk', xb, u_tab[eb]).astype(jnp.float32), approximate=False)
        return jnp.einsum('tk,tkd->td', (gb * act).astype(xb.dtype), v_tab[eb])

    out = lax.map(block, (xt.reshape(nb, PEER_BLOCK, d),
                          expert_id.reshape(nb, PEER_BLOCK, PEER_HEADS * PEER_TOPK),
                          gate.reshape(nb, PEER_BLOCK, PEER_HEADS * PEER_TOPK)))
    return out.reshape(bsz, s, d)

def setup_inputs(seed: int = 0) -> dict:
    key = jax.random.key(seed)
    k = jax.random.split(key, 27)
    f32 = jnp.float32

    def nrm(kk, shape, scale):
        return scale * jax.random.normal(kk, shape, f32)

    state_idx = jnp.arange(S5_STATE, dtype=f32)
    dt_gdn = jnp.exp(jax.random.uniform(k[21], (N_ODD, GDN_HEADS), f32, math.log(1e-3), math.log(1e-1)))
    return {
        'x': nrm(k[0], (BATCH, SEQ, D_MODEL), 1.0),
        'norm_mix_w': 1.0 + nrm(k[1], (DEPTH, D_MODEL), 0.02),
        'norm_ffn_w': 1.0 + nrm(k[2], (DEPTH, D_MODEL), 0.02),
        'norm_out_w': 1.0 + nrm(k[3], (D_MODEL,), 0.02),
        'ev_in_w': nrm(k[4], (N_EVEN, D_MODEL, EVEN_PROJ), D_MODEL ** -0.5),
        'ev_out_w': nrm(k[5], (N_EVEN, EVEN_MIX, D_MODEL), EVEN_MIX ** -0.5),
        'hgrn_lb': nrm(k[6], (N_EVEN + 1, HGRN_QK_WIDTH), 0.1),
        'hgrn_gn_w': 1.0 + nrm(k[7], (N_EVEN, HGRN_DV), 0.02),
        's5_a_re': -0.5 + nrm(k[8], (N_EVEN, S5_GROUPS, S5_STATE), 0.01),
        's5_a_im': jnp.pi * state_idx + nrm(k[9], (N_EVEN, S5_GROUPS, S5_STATE), 0.01),
        's5_log_dt': jax.random.uniform(k[10], (N_EVEN, S5_GROUPS), f32, math.log(1e-3), math.log(1e-1)),
        's5_b_re': nrm(k[11], (N_EVEN, S5_GROUPS, S5_STATE, S5_GROUP), (2 * S5_GROUP) ** -0.5),
        's5_b_im': nrm(k[12], (N_EVEN, S5_GROUPS, S5_STATE, S5_GROUP), (2 * S5_GROUP) ** -0.5),
        's5_c_re': nrm(k[13], (N_EVEN, S5_GROUPS, S5_GROUP, S5_STATE), 0.5),
        's5_c_im': nrm(k[14], (N_EVEN, S5_GROUPS, S5_GROUP, S5_STATE), 0.5),
        's5_d': nrm(k[15], (N_EVEN, S5_GROUPS, S5_GROUP), 1.0),
        's5_glu_w': nrm(k[16], (N_EVEN, S5_WIDTH, S5_WIDTH), S5_WIDTH ** -0.5),
        'od_in_w': nrm(k[17], (N_ODD, D_MODEL, ODD_PROJ), D_MODEL ** -0.5),
        'od_out_w': nrm(k[18], (N_ODD, GDN_V, D_MODEL), GDN_V ** -0.5),
        'gdn_conv_w': nrm(k[19], (N_ODD, GDN_CONV, 2 * GDN_QK + GDN_V), GDN_CONV ** -0.5),
        'gdn_a_log': jnp.log(jax.random.uniform(k[20], (N_ODD, GDN_HEADS), f32, 1.0, 16.0)),
        'gdn_dt_bias': dt_gdn + jnp.log(-jnp.expm1(-dt_gdn)),
        'gdn_gn_w': 1.0 + nrm(k[22], (N_ODD, GDN_DV), 0.02),
        'peer_wq': nrm(k[23], (DEPTH, D_MODEL, PEER_HEADS * PEER_DKEY), D_MODEL ** -0.5),
        'peer_sub_keys': nrm(k[24], (DEPTH, 2, PEER_NKEYS, PEER_DHALF), PEER_DHALF ** -0.5),
        'peer_u': nrm(k[25], (DEPTH, PEER_EXPERTS, D_MODEL), D_MODEL ** -0.5),
        'peer_v': nrm(k[26], (DEPTH, PEER_EXPERTS, D_MODEL), PEER_HEADS ** -0.5),
    }

def reference(x, norm_mix_w, norm_ffn_w, norm_out_w, ev_in_w, ev_out_w, hgrn_lb, hgrn_gn_w,
              s5_a_re, s5_a_im, s5_log_dt, s5_b_re, s5_b_im, s5_c_re, s5_c_im, s5_d, s5_glu_w,
              od_in_w, od_out_w, gdn_conv_w, gdn_a_log, gdn_dt_bias, gdn_gn_w,
              peer_wq, peer_sub_keys, peer_u, peer_v):
    lb_all = jnp.cumsum(jax.nn.softmax(hgrn_lb.astype(jnp.float32), axis=0), axis=0)
    even_splits = [HGRN_QK_WIDTH, 2 * HGRN_QK_WIDTH, 2 * HGRN_QK_WIDTH + HGRN_V_WIDTH,
                   2 * HGRN_QK_WIDTH + 2 * HGRN_V_WIDTH]
    odd_splits = [2 * GDN_QK + GDN_V, 2 * GDN_QK + 2 * GDN_V, 2 * GDN_QK + 2 * GDN_V + GDN_HEADS]
    h = x
    for layer in range(DEPTH):
        j = layer // 2
        hn = rmsnorm(h, norm_mix_w[layer])
        if layer % 2 == 0:
            proj = (hn @ ev_in_w[j]).astype(jnp.float32)
            q_raw, f_raw, i_raw, g_raw, u_raw = jnp.split(proj, even_splits, axis=-1)
            o_a = hgrn2_mixer(q_raw, f_raw, i_raw, g_raw, lb_all[j], hgrn_gn_w[j])
            o_b = s5_mixer(u_raw, s5_a_re[j], s5_a_im[j], s5_log_dt[j], s5_b_re[j], s5_b_im[j],
                           s5_c_re[j], s5_c_im[j], s5_d[j], s5_glu_w[j])
            mixed = jnp.concatenate([o_a, o_b], axis=-1).astype(h.dtype) @ ev_out_w[j]
        else:
            proj = (hn @ od_in_w[j]).astype(jnp.float32)
            qkv_raw, z_raw, beta_raw, a_raw = jnp.split(proj, odd_splits, axis=-1)
            o_c = gated_deltanet_mixer(qkv_raw, z_raw, beta_raw, a_raw, gdn_conv_w[j], gdn_a_log[j],
                                       gdn_dt_bias[j], gdn_gn_w[j])
            mixed = o_c.astype(h.dtype) @ od_out_w[j]
        h = h + mixed
        h = h + peer_ffn(rmsnorm(h, norm_ffn_w[layer]), peer_wq[layer], peer_sub_keys[layer],
                         peer_u[layer], peer_v[layer])
    return rmsnorm(h, norm_out_w)


_drawn_inputs = setup_inputs


def setup_inputs(seed=0):
    import zlib

    import numpy as np

    out = dict(_drawn_inputs(seed))
    spreads = {}
    factors = {}
    for name, (base, spread) in spreads.items():
        noise = np.random.default_rng([zlib.crc32(name.encode()), seed]).standard_normal(out[name].shape)
        drawn = base * np.exp(spread * noise) if base else spread * noise
        out[name] = jnp.asarray(drawn.astype(out[name].dtype))
    for name, factor in factors.items():
        out[name] = (out[name] * factor).astype(out[name].dtype)
    return out
```

```python
from contextlib import ExitStack

import concourse.bass as bass
from concourse import mybir

F32 = mybir.dt.float32
I32 = mybir.dt.int32
U32 = mybir.dt.uint32
ALU = mybir.AluOpType
ACT = mybir.ActivationFunctionType
AX = mybir.AxisListType

P = 128
D = 1024
T = 512
DC = D // P
TT = T // P
HG = 4
HC = 32
NCH = T // HC
ST = 16
GH = 8
PH = 8
NK = 128
TOPK = 16
E = NK * NK
EPS = 1e-6
HGRN_SCALE = 128 ** -0.5
GDN_SCALE = 128 ** -0.5
TWO_PI_HI = 6.28125
TWO_PI_LO = 6.283185307179586 - 6.28125
ROUND = 12582912.0
LOWEST = -3.0e38
NU = 8
NV = 16
ROUTE_LINKS = 21
HEADS = PH * TT

STREAMS = {"ev_in": (0, 20), "ev_out": (20, 8), "wq0": (28, 16),
           "od_in": (44, 32), "od_out": (76, 8), "wq1": (84, 16)}
NSLOT = 4

SMALL = [("norm_w", 5 * DC), ("s5_are", ST), ("s5_aim", ST), ("s5_ldt", ST), ("s5_d", 4),
         ("lb", 8), ("gn", 2), ("conv", 96), ("ab", 2), ("ba_w", DC * 16), ("keys", 4 * NK)]
SMALL_AT = {}
_at = 0
for _n, _w in SMALL:
    SMALL_AT[_n] = (_at, _w)
    _at += _w
NSMALL = _at

ARENA = 40064


class Chain:

    def __init__(self, eng, sem):
        self.eng, self.sem, self.base, self.k = eng, sem, 0, 0

    def link(self, ins):
        self.k += 1
        ins.then_inc(self.sem, 1)
        self.eng.wait_ge(self.sem, self.base + self.k)


def trunk(nc, xT, wall, glu_w, s5_b, s5_c, small, u_tab, v_tab, out, stop_after=None, probe=None):
    ctx = ExitStack()
    with ctx:
        def sb(name, shape, dt=F32):
            return ctx.enter_context(nc.sbuf_tensor(name, shape, dt))

        def sem(name):
            return ctx.enter_context(nc.semaphore(name))

        h = sb("h", [P, DC, T])
        wring = sb("wring", [P, NSLOT, DC, P])
        scr = sb("scr", [P, 4, T])
        consts = sb("consts", [P, NSMALL])
        ident = sb("ident", [P, P])
        mean_d = sb("mean_d", [P, P])
        mean_h = sb("mean_h", [P, P])
        ones = sb("ones", [P, P])
        maskc = sb("maskc", [P, P])
        mask32 = sb("mask32", [P, P])
        iota16 = sb("iota16", [P, TOPK])
        cols = sb("cols", [P, 640])
        rt = sb("rt", [P, T])
        arena = sb("arena", [P, ARENA])
        ps = [ctx.enter_context(nc.psum_tensor(f"ps{i}", [P, T], F32)) for i in range(8)]

        def region(at, *shape):
            n = 1
            for x in shape:
                n *= x
            assert at + n <= ARENA, (at, n)
            v = arena[:, at:at + n]
            if len(shape) == 2:
                return v.rearrange("p (a b) -> p a b", a=shape[0])
            if len(shape) == 3:
                return v.rearrange("p (a b c) -> p a b c", a=shape[0], b=shape[1])
            return v

        def small_in(name):
            a, w = SMALL_AT[name]
            return consts[:, a:a + w]

        norm_w = small_in("norm_w").rearrange("p (n k) -> p n k", k=DC)
        conv_w = small_in("conv").rearrange("p (c j) -> p c j", j=4)
        ba_w = small_in("ba_w").rearrange("p (k m) -> p k m", m=16)
        keys = small_in("keys").rearrange("p (l c k) -> p l c k", l=2, c=2)
        gn_col = small_in("gn")
        eps_col = cols[:, 0:1]

        maskl = region(32768, 2, 7, P)

        hn = region(0, DC, T)
        proj = region(4096, 20, T)
        uT, qT, fT, vT0, gT = (proj[:, 4 * i:4 * i + 4, :] for i in range(5))
        tab_c = region(14336, ST, T)
        tab_s = region(22528, ST, T)
        bw = region(30720, 2, 4, P)
        cw = region(31744, 2, ST, 32)
        s5w = region(32768, 2, 6, T)
        tab_t = region(32768, 2, 2048)
        kA = region(14336, HG, T)
        eC = region(16384, HG, T)
        kE = region(18432, HG, T)
        kD = region(20480, HG, T)
        kTok = region(22528, HG, TT, P)
        vTok = region(24576, HG, TT, P)
        states = region(26624, NCH, P)
        glu_sb = region(36864, 4, T)
        totH = cols[:, 64:128].rearrange("p (h c) -> p h c", h=HG)
        mix0 = [qT[:, j, :] for j in range(4)] + [uT[:, j, :] for j in range(4)]
        statesA = [region(26624, NCH, P), region(28672, NCH, P), region(32768, NCH, P), region(34816, NCH, P)]

        raw = region(4096, 24, T)
        zT = region(16384, GH, T)
        conv = region(20480, 24, T)
        beta_r = region(34560, T)[0:GH]
        dec_r = region(35072, T)[0:GH]
        soft_r = [region(37632 + T * i, T)[0:GH] for i in range(4)]
        dec_c = cols[:, 64:96].rearrange("p (t h) -> p t h", h=GH)
        beta_c = cols[:, 96:128].rearrange("p (t h) -> p t h", h=GH)
        last_c = cols[:, 128:160].rearrange("p (h t) -> p h t", t=TT)
        kbe_c = cols[:, 160:192].rearrange("p (t h) -> p t h", h=GH)
        tail_c = cols[:, 192:224].rearrange("p (t h) -> p t h", h=GH)
        tot_c = cols[:, 224:256].rearrange("p (h t) -> p h t", t=TT)
        kbT = region(0, 4, T)
        qdT = region(2048, 4, T)
        vb = region(4096, 4, TT, P)
        kbe = region(6144, 4, TT, P)
        ktail = region(8192, 4, TT, P)
        invT = region(10240, 4, T)
        inv = region(12288, 4, T)
        negA = region(14336, 4, T)
        lmT = region(35584, 4, T)
        xs = region(37632, 4, T)
        gstate = region(37632, 4, P)
        vnew = region(38144, 4, P)
        mcur = region(39680, 2, P)
        mix1 = [zT[:, j, :] for j in range(GH)]

        sc = region(0, PH * TT + 1, 2 * NK)
        xtok = region(8448, TT, D)
        xcur = region(12544, D)
        yacc = region(13568, D)
        uring = region(14592, NU, D)
        vring = region(22784, NV, D)
        sct = region(39168, 2, 2, NK)
        phn = region(14592, DC, T)
        pq = region(18688, 2 * PH, T)
        cand = rt[:, 0:TOPK * TOPK]
        hot = rt[:, TOPK * TOPK:2 * TOPK * TOPK].rearrange("p (a b) -> p a b", a=TOPK)
        diag = scr[:, :, :].rearrange("p a (b c) -> p (a b) c", c=P)

        def rcol(i, n, dt=F32):
            return cols[:, i:i + n].bitcast(dt) if dt is not F32 else cols[:, i:i + n]

        top_v = rcol(64, 32).rearrange("p (c k) -> p c k", c=2)
        top_i = rcol(96, 32, U32).rearrange("p (c k) -> p c k", c=2)
        top_f = rcol(128, 32).rearrange("p (c k) -> p c k", c=2)
        sel_v, sel_p = rcol(160, TOPK), rcol(176, TOPK, U32)
        sel_a, sel_b = rcol(192, TOPK, U32), rcol(208, TOPK, U32)
        pos_a, pos_b = rcol(224, TOPK), rcol(240, TOPK)
        exp_a, exp_b = rcol(256, TOPK), rcol(272, TOPK)
        soft_e, soft_m, soft_s = rcol(288, TOPK), rcol(304, 1), rcol(305, 1)
        ids = [rcol(320 + 16 * i, TOPK, U32) for i in range(2)]
        gate = [rcol(352 + 16 * i, TOPK) for i in range(2)]
        dots = [rcol(384 + 16 * i, TOPK) for i in range(2)]
        gelu = [rcol(416 + 16 * i, TOPK) for i in range(2)]
        wgt = [rcol(448 + 16 * i, TOPK) for i in range(2)]

        s = {n: sem(n) for n in (
            "lm_iota", "lm_built", "conv_done", "silu", "l2_sq", "l2_sum", "l2_root", "l2_done",
            "ba_mm", "a_raw", "a_abs", "a_exp", "a_one", "a_ln", "beta_ready", "dec_ready", "col_tr", "cols_ready",
            "bc_mm", "last_ready", "kb_ready", "lm_min", "gq_exp", "lm_exp", "small_exp", "scale_cols", "qd_ready",
            "kk_mm", "negA_ready", "ktr_mm", "kbe_ready", "ktail_ready", "vtr_mm", "vb_ready",
            "wt_done", "x_mm", "xs_copied", "y_mm", "kc_mm", "kc_ready", "qk_mm", "att_raw", "att_ready",
            "vn_mm", "vn_ready", "gds_mm", "gs_ready", "go_done", "g_sq", "g_sum", "g_root",
            "xt_tr", "xt_copied", "sc_mm", "sc_ready", "sct_ready", "soft_in", "soft_exp", "ids_ready",
            "u_free", "v_free", "gelu_ready", "w_ready", "diag_ready", "y_added", "yT_ready", "peer_done", "mix1_free",
            "x_loaded", "small_loaded", "bc_loaded", "glu_loaded", "out_stored",
            "const_pool", "masks_built",
            "sq_ready", "sum_ready", "root_ready", "rt_ready", "hn_ready",
            "acc_ready", "acc_free",
            "dve_own", "act_own", "pool_own", "dve_passed", "pool_passed",
            "s5_theta", "s5_trig", "s5_trig_exp", "s5_wc", "tab_dve", "tab_pool", "s5_ctab", "s5_bu", "s5_bcopy",
            "s5_wr", "s5_wi", "s5_scan", "s5_pr", "s5_pi", "s5_y", "s5_ysum", "s5_gelu", "s5_glu", "s5_sig",
            "lb_e", "lb_d", "hg_sig", "hg_f", "hg_ln", "hg_k", "hg_cum", "hg_dif", "hg_exp", "hg_ke", "hg_kd",
            "hg_att", "hg_attm", "hg_tr", "hg_trc", "hg_ds", "hg_st", "hg_o", "hg_sq", "hg_sum", "hg_root",
            "mix_ready")}
        u_arrived = [sem(f"u_arrived{i}") for i in range(NU)]
        v_arrived = [sem(f"v_arrived{i}") for i in range(NV)]
        w_arrived = [sem(f"w_arrived{i}") for i in range(NSLOT)]

        block = ctx.enter_context(nc.Block())

        def probe_sp(sp):
            sp.wait_ge(s["mix_ready"], 8)
            for j in range(8):
                sp.dma_start(out[:, j, :], mix0[j]).then_inc(s["out_stored"], 16)
            sp.wait_ge(s["out_stored"], 16 * 8)

        def s5t(i, w):
            return tab_t[:, i, 0:ST * w].rearrange("p (a b) -> p a b", a=ST)

        @block.sync
        def _(sp):
            sp.dma_start(h[:, :, :], xT).then_inc(s["x_loaded"], 16)
            sp.dma_start(consts[:, :], small).then_inc(s["small_loaded"], 16)
            sp.dma_start(bw, s5_b).then_inc(s["bc_loaded"], 16)
            sp.dma_start(cw, s5_c).then_inc(s["bc_loaded"], 16)

            def load_stream(name, first=False):
                c0, n = STREAMS[name]
                start = 0
                if first:
                    for j in range(NSLOT):
                        sp.dma_start(wring[:, j, :, :], wall[c0 + j]).then_inc(w_arrived[j], 16)
                    start = NSLOT
                with sp.Fori(start // NSLOT, n // NSLOT) as i:
                    for j in range(NSLOT):
                        sp.wait_ge(s["acc_ready"], i * NSLOT + (c0 + j - NSLOT + 1))
                        sp.dma_start(wring[:, j, :, :],
                                     wall[bass.ds(i * NSLOT + (c0 + j), 1)].rearrange("a p k n -> (a p) k n")
                                     ).then_inc(w_arrived[j], 16)

            load_stream("ev_in", first=True)
            sp.wait_ge(s["s5_y"], ST)
            sp.dma_start(glu_sb, glu_w).then_inc(s["glu_loaded"], 16)
            if stop_after == "mix0":
                return probe_sp(sp)
            load_stream("ev_out")
            load_stream("wq0")
            if stop_after == "h1":
                sp.wait_ge(s["peer_done"], TT)
                sp.dma_start(out, h[:, :, :]).then_inc(s["out_stored"], 16)
                sp.wait_ge(s["out_stored"], 16)
                return
            load_stream("od_in")
            if stop_after == "mix1":
                for j in range(8):
                    sp.wait_ge(s["mix_ready"], 9 + j)
                    sp.dma_start(out[:, j, :], mix1[j]).then_inc(s["out_stored"], 16)
                sp.wait_ge(s["out_stored"], 16 * 8)
                return
            load_stream("od_out")
            load_stream("wq1")
            for k in range(DC):
                sp.wait_ge(s["hn_ready"], 4 * DC + k + 1)
                sp.dma_start(out[:, k, :], hn[:, k, :]).then_inc(s["out_stored"], 16)
            sp.wait_ge(s["out_stored"], 16 * DC)

        @block.gpsimd
        def _(pool):
            own = Chain(pool, s["pool_own"])
            pool.memset(ident[:, :], 0.0)
            pool.memset(mean_d[:, :], 1.0 / D)
            pool.memset(mean_h[:, :], 1.0 / P)
            pool.memset(maskc[:, :], 1.0)
            own.link(pool.memset(ones[:, :], 1.0))
            pool.affine_select(out=ident[:, :], in_=ident[:, :], compare_op=ALU.not_equal, fill=1.0, base=0,
                               pattern=[[-1, P]], channel_multiplier=1)
            pool.affine_select(out=maskc[:, :], in_=maskc[:, :], compare_op=ALU.is_ge, fill=0.0, base=0,
                               pattern=[[1, P]], channel_multiplier=-1)
            pool.iota(iota16[:, :], [[1, TOPK]], base=0, channel_multiplier=0,
                      allow_small_or_imprecise_dtypes=True)
            row = scr[:, 0, 0:P].bitcast(I32)
            col = scr[:, 0, P:2 * P].bitcast(I32)
            pool.iota(row, [[0, P]], base=0, channel_multiplier=1)
            pool.iota(scr[:, 1, :].bitcast(I32), [[1, T]], base=0, channel_multiplier=0)
            pool.iota(col, [[1, P]], base=0, channel_multiplier=0).then_inc(s["const_pool"], 1)

            for m in range(9):
                w = 1 << m
                pool.wait_ge(s["s5_ctab"], m + 1)
                if m:
                    pool.wait_ge(s["tab_dve"], m)
                step = min(w, 128)
                for a in range(0, w, step):
                    tmp = s5t(1, step)
                    cmb = cols[:, 128 + 32 * m:144 + 32 * m].unsqueeze(2).to_broadcast([P, ST, step])
                    smb = cols[:, 144 + 32 * m:160 + 32 * m].unsqueeze(2).to_broadcast([P, ST, step])
                    pool.tensor_tensor(tab_s[:, :, w + a:w + a + step], tab_s[:, :, a:a + step], cmb, ALU.mult)
                    own.link(pool.tensor_tensor(tmp, tab_c[:, :, a:a + step], smb, ALU.mult))
                    last = pool.tensor_tensor(tab_s[:, :, w + a:w + a + step], tab_s[:, :, w + a:w + a + step], tmp,
                                              ALU.add)
                    if a + step < w:
                        own.link(last)
                last.then_inc(s["tab_pool"], 1)
                pool.wait_ge(s["tab_pool"], m + 1)

            for st in range(ST):
                W = s5w[:, st % 2]
                pool.wait_ge(s["s5_bcopy"], 2 * st + 2)
                if st == 0:
                    pool.wait_ge(s["tab_dve"], 9)
                if st >= 2:
                    pool.wait_ge(s["s5_y"], st - 1)
                pool.tensor_tensor(W[:, 5, :], W[:, 1, :], tab_c[:, st, :], ALU.mult)
                own.link(pool.tensor_tensor(W[:, 3, :], W[:, 0, :], tab_s[:, st, :], ALU.mult))
                pool.tensor_tensor(W[:, 3, :], W[:, 5, :], W[:, 3, :], ALU.subtract).then_inc(s["s5_wi"], 1)
                pool.wait_ge(s["s5_scan"], 2 * st + 2)
                pool.tensor_tensor(W[:, 1, :], W[:, 2, :], tab_s[:, st, :], ALU.mult)
                pool.tensor_tensor(W[:, 5, :], W[:, 3, :], tab_c[:, st, :], ALU.mult).then_inc(s["s5_pi"], 1)

            pool.wait_ge(s["hg_f"], 4)
            pool.wait_ge(s["s5_y"], ST)
            pool.tensor_scalar(kA, fT, -1.0, 1.0, ALU.mult, ALU.add).then_inc(s["hg_k"], 1)
            pool.wait_ge(s["hg_exp"], 3)
            pool.tensor_tensor(kD, kA, kD, ALU.mult).then_inc(s["hg_kd"], 1)

            def peer(layer):
                def head(g, par):
                    pool.wait_ge(s["ids_ready"], g + ((HEADS + 1) * layer + 1))
                    for ring, tab, n, free, arrived in ((uring, u_tab, NU, "u_free", u_arrived),
                                                        (vring, v_tab, NV, "v_free", v_arrived)):
                        for k in range(TOPK):
                            pool.wait_ge(s[free], g * TOPK + (TOPK * HEADS * layer + k + 1))
                            pool.sem_inc(s["pool_passed"], 1)
                            pool.indirect_dma_start(
                                out=ring[:, k % n, :], out_offset=None, in_=tab,
                                in_offset=bass.IndirectOffsetOnAxis(ap=ids[par][:, k:k + 1], axis=0)
                            ).then_inc(arrived[k % n], 16)

                with pool.Fori(0, HEADS // 2) as p:
                    for par in range(2):
                        head(p * 2 + par, par)

            if stop_after == "mix0":
                return
            peer(0)
            if stop_after == "h1":
                return

            pool.wait_ge(s["peer_done"], TT)
            row = lmT[:, 0, 0:P].bitcast(I32)
            col = lmT[:, 0, P:2 * P].bitcast(I32)
            pool.iota(row, [[0, P]], base=0, channel_multiplier=1)
            pool.iota(col, [[1, P]], base=0, channel_multiplier=0).then_inc(s["lm_iota"], 1)

            for grp in range(2):
                for hh in range(4):
                    pool.wait_ge(s["att_raw"], 4 * grp + hh + 1)
                    pool.tensor_tensor(negA[:, hh, :].rearrange("p (t x) -> p t x", t=TT),
                                       negA[:, hh, :].rearrange("p (t x) -> p t x", t=TT),
                                       maskc[:, :].unsqueeze(1).to_broadcast([P, TT, P]),
                                       ALU.mult).then_inc(s["att_ready"], 1)
            if stop_after == "mix1":
                return
            peer(1)

        @block.tensor
        def _(pe):
            def norm_sum(n):
                for k in range(DC):
                    pe.wait_ge(s["sq_ready"], DC * n + k + 1)
                    mm = pe.matmul(ps[2][:, :], mean_d[:, :], scr[:, k % 4, :], start=(k == 0), stop=(k == DC - 1))
                    mm.then_inc(s["sum_ready"], 1)

            def stream(name, rhs):
                c0, n = STREAMS[name]
                with pe.Fori(0, n // NSLOT) as i:
                    for j in range(NSLOT):
                        chunk(c0, i * NSLOT + j, j, rhs)

            def chunk(c0, c, j, rhs):
                pe.wait_ge(w_arrived[j], (c - j) * 4 + (4 * c0 + 16))
                pe.wait_ge(s["acc_free"], c + (c0 + 1))
                for k in range(DC):
                    mm = pe.matmul(ps[j % 2][:, :], wring[:, j, k, :], rhs(k), start=(k == 0), stop=(k == DC - 1))
                mm.then_inc(s["acc_ready"], 1)

            pe.wait_ge(s["const_pool"], 1)
            norm_sum(0)
            pe.wait_ge(s["hn_ready"], DC)

            def s5_in(st):
                q, jj = st // 4, st % 4
                if st >= 2:
                    pe.wait_ge(s["s5_bcopy"], 2 * (st - 2) + 2)
                for i in range(2):
                    mm = pe.matmul(ps[3 + 2 * (st % 2) + i][:, :], bw[32 * jj:32 * jj + 32, i, q, :],
                                   uT[32 * jj:32 * jj + 32, q, :], start=True, stop=True)
                mm.then_inc(s["s5_bu"], 1)

            def s5_out(st):
                q, jj = st // 4, st % 4
                W = s5w[:, st % 2]
                pe.wait_ge(s["s5_pr"], st + 1)
                pe.wait_ge(s["s5_pi"], st + 1)
                if jj == 0 and q:
                    pe.wait_ge(s["s5_ysum"], q)
                o = ps[7][32 * jj:32 * jj + 32, :]
                for n, (w, x) in enumerate(((0, 0), (0, 4), (1, 1), (1, 5))):
                    mm = pe.matmul(o, cw[:, w, st, :], W[:, x, :], start=(n == 0), stop=(n == 3))
                mm.then_inc(s["s5_y"], 1)

            for c in range(20):
                chunk(0, c, c % 4, lambda k: hn[:, k, :])
                if c == 3:
                    pe.wait_ge(s["bc_loaded"], 32)
                    pe.wait_ge(s["acc_free"], 4 + 2)
                    s5_in(0)
                if c >= 4:
                    st = c - 4
                    if st + 1 < ST:
                        s5_in(st + 1)
                    if st == 0:
                        pe.wait_ge(s["s5_wc"], 1)
                    s5_out(st)

            pe.wait_ge(s["s5_gelu"], 1)
            pe.wait_ge(s["glu_loaded"], 16)
            for n in range(4):
                for k in range(4):
                    mm = pe.matmul(ps[3 + n][:, :], glu_sb[:, k, P * n:P * n + P], uT[:, k, :],
                                   start=(k == 0), stop=(k == 3))
                mm.then_inc(s["s5_glu"], 1)

            BA = (0, 1, 2, 7)
            pe.wait_ge(s["hg_ke"], 2)
            for hd in range(HG):
                for t in range(TT):
                    c = slice(P * t, P * t + P)
                    mm = pe.matmul(ps[BA[hd]][:, c], kE[:, hd, c], qT[:, hd, c], start=(t == 0), stop=(t == TT - 1),
                                   skip_group_check=True)
                mm.then_inc(s["hg_att"], 1)
            pe.wait_ge(s["s5_sig"], 4)
            pe.wait_ge(s["hg_kd"], 1)
            for i in range(8):
                hd = i % 4
                src = kD if i < 4 else vT0
                if i >= 4:
                    pe.wait_ge(s["hg_trc"], i - 3)
                for t in range(TT):
                    c = slice(P * t, P * t + P)
                    mm = pe.transpose(ps[3 + hd][:, c], src[:, hd, c], ident[:, :])
                mm.then_inc(s["hg_tr"], 1)
            for hd in range(HG):
                if hd == 0:
                    pe.wait_ge(s["hg_trc"], 8)
                else:
                    pe.wait_ge(s["hg_st"], 15 * hd)
                for j in range(4):
                    for t in range(TT):
                        r = slice(HC * j, HC * j + HC)
                        mm = pe.matmul(ps[3 + j][:, P * t:P * t + P], kTok[r, hd, t, :], vTok[r, hd, t, :],
                                       start=True, stop=True, skip_group_check=True)
                mm.then_inc(s["hg_ds"], 1)
            for hd in range(HG):
                pe.wait_ge(s["hg_attm"], 4)
                pe.wait_ge(s["hg_st"], 15 * hd + 15)
                for t in range(TT):
                    c = slice(P * t, P * t + P)
                    pe.matmul(ps[BA[hd]][:, c], vTok[:, hd, t, :], eC[:, hd, c], start=(t == 0), stop=False,
                              skip_group_check=True)
                for n in range(1, NCH):
                    c = slice(HC * n, HC * n + HC)
                    mm = pe.matmul(ps[BA[hd]][:, c], statesA[hd][:, n, :], qT[:, hd, c], start=False,
                                   stop=(n == NCH - 1), skip_group_check=True)
                mm.then_inc(s["hg_o"], 1)
            for hd in range(HG):
                pe.wait_ge(s["hg_sq"], hd + 1)
                pe.matmul(ps[3 + hd][:, :], mean_h[:, :], scr[:, hd, :], start=True, stop=True).then_inc(s["hg_sum"], 1)

            def peer(layer):
                norm_sum(2 * layer + 1)
                pe.wait_ge(s["hn_ready"], DC * (2 * layer + 2))
                for n in range(2 * TT):
                    t, half = n // 2, n % 2
                    if n >= 2 or layer:
                        pe.wait_ge(s["xt_copied"], 2 * TT * layer + n - 1)
                    for k in range(4):
                        mm = pe.transpose(ps[3 + n % 2][:, P * k:P * k + P], phn[:, 4 * half + k, P * t:P * t + P],
                                          ident[:, :])
                    mm.then_inc(s["xt_tr"], 1)
                stream(f"wq{layer}", lambda k: phn[:, k, :])
                pe.wait_ge(s["acc_free"], STREAMS[f"wq{layer}"][0] + 16 + 2)
                for n in range(4 * TT):
                    t, g = n // 4, n % 4
                    if n >= 4 or layer:
                        pe.wait_ge(s["sc_ready"], 4 * TT * layer + n - 3)
                    if n < 4:
                        pe.wait_ge(s["xt_copied"], 2 * TT * (layer + 1))
                    for k in range(4):
                        hc = 4 * g + k
                        mm = pe.matmul(ps[3 + n % 4][:, P * k:P * k + P], pq[:, hc, P * t:P * t + P],
                                       keys[:, layer, hc % 2, :], start=(k == 0), stop=(k == 3), skip_group_check=True)
                    mm.then_inc(s["sc_mm"], 1)
                pe.wait_ge(s["sc_ready"], 4 * TT * (layer + 1))

                def head(g, par):
                    pe.wait_ge(s["y_added"], g + (HEADS * layer + 1))
                    for k in range(TOPK):
                        pe.wait_ge(s["diag_ready"], g * TOPK + (TOPK * HEADS * layer + k + 1))
                        pe.wait_ge(v_arrived[k % NV], (g * (TOPK // NV) + (HEADS * layer * (TOPK // NV) + k // NV + 1)) * 16)
                        for i in range(2):
                            mm = pe.matmul(ps[4 + 2 * par + i][:, :], diag[:, k, :], vring[:, k % NV, T * i:T * i + T],
                                           start=(k == 0), stop=(k == TOPK - 1))
                        mm.then_inc(s["v_free"], 1)

                with pe.Fori(0, TT) as t:
                    with pe.Fori(0, PH // 2) as p:
                        for par in range(2):
                            head(t * PH + p * 2 + par, par)
                    pe.wait_ge(s["y_added"], t * PH + (HEADS * layer + PH + 2))
                    for k in range(DC):
                        mm = pe.transpose(ps[2 + k // 4][:, P * (k % 4):P * (k % 4) + P], yacc[:, P * k:P * k + P],
                                          ident[:, :])
                    mm.then_inc(s["yT_ready"], 1)

            if stop_after == "mix0":
                return
            pe.wait_ge(s["mix_ready"], DC)
            stream("ev_out", lambda k: mix0[k])
            peer(0)
            if stop_after == "h1":
                return

            norm_sum(2)
            pe.wait_ge(s["hn_ready"], 3 * DC)
            stream("od_in", lambda k: hn[:, k, :])
            for i, bank in enumerate((7, 2)):
                for k in range(DC):
                    mm = pe.matmul(ps[bank][0:GH, :], ba_w[:, k, GH * i:GH * i + GH], hn[:, k, :], start=(k == 0),
                                   stop=(k == DC - 1))
                mm.then_inc(s["ba_mm"], 1)
            for c in range(16):
                pe.wait_ge(s["l2_sq"], c + 1)
                pe.matmul(ps[3 + c % 4][:, :], ones[:, :], scr[:, c % 4, :], start=True,
                          stop=True).then_inc(s["l2_sum"], 1)
            pe.wait_ge(s["beta_ready"], 1)
            pe.wait_ge(s["dec_ready"], 1)
            for i, r in enumerate((dec_r, beta_r)):
                for t in range(TT):
                    mm = pe.transpose(ps[0][:, 32 * i + GH * t:32 * i + GH * t + GH], r[:, P * t:P * t + P],
                                      ident[0:GH, 0:GH])
            mm.then_inc(s["col_tr"], 1)

            def tile(t):
                return slice(P * t, P * t + P)

            for grp in range(2):
                hs = range(4 * grp, 4 * grp + 4)
                if grp:
                    pe.wait_ge(s["mix_ready"], 8 + 4 * grp)
                pe.wait_ge(s["cols_ready"], 1)
                pe.wait_ge(s["l2_done"], 16)
                for hh, hd in enumerate(hs):
                    pick = ident[0:GH, hd:hd + 1].to_broadcast([GH, P])
                    pe.matmul(ps[BA[hh]][:, :], pick, beta_r, start=True, stop=True)
                    pe.matmul(ps[3 + hh][:, :], pick, dec_r, start=True, stop=True).then_inc(s["bc_mm"], 1)
                for hh, hd in enumerate(hs):
                    pe.wait_ge(s["kb_ready"], 4 * grp + hh + 1)
                    for t in range(TT):
                        mm = pe.matmul(ps[BA[hh]][:, tile(t)], conv[:, GH + hd, tile(t)], kbT[:, hh, tile(t)],
                                       start=(t == 0), stop=(t == TT - 1), skip_group_check=True)
                    mm.then_inc(s["kk_mm"], 1)
                for hh, hd in enumerate(hs):
                    pe.wait_ge(s["lm_min"], 4 * grp + hh + 1)
                    pe.wait_ge(s["gq_exp"], 4 * grp + hh + 1)
                    for t in range(TT):
                        mm = pe.transpose(ps[3 + hh][:, tile(t)], conv[:, GH + hd, tile(t)], ident[:, :])
                    mm.then_inc(s["ktr_mm"], 1)
                pe.wait_ge(s["silu"], 6)
                for hh, hd in enumerate(hs):
                    pe.wait_ge(s["negA_ready"], 4 * grp + hh + 1)
                    for t in range(TT):
                        mm = pe.transpose(ps[BA[hh]][:, tile(t)], conv[:, 2 * GH + hd, tile(t)], ident[:, :])
                    mm.then_inc(s["vtr_mm"], 1)
                pe.wait_ge(s["vb_ready"], 4 * grp + 4)
                pe.wait_ge(s["kbe_ready"], 4 * grp + 4)
                pe.wait_ge(s["ktail_ready"], 4 * grp + 4)
                with pe.Fori(0, 7) as l:
                    for hh in range(4):
                        pe.wait_ge(s["wt_done"], l * 4 + (32 * grp + hh + 1))
                        for t in range(TT):
                            mm = pe.matmul(ps[BA[hh]][:, tile(t)], negA[:, hh, tile(t)], inv[:, hh, tile(t)],
                                           start=(t == 0), stop=(t == TT - 1), skip_group_check=True)
                        mm.then_inc(s["x_mm"], 1)
                    for hh in range(4):
                        pe.wait_ge(s["xs_copied"], l * 4 + (28 * grp + hh + 1))
                        if hh >= 2:
                            pe.wait_ge(s["wt_done"], l * 4 + (32 * grp + 4 + hh - 1))
                        for t in range(TT):
                            pe.matmul(ps[3 + hh % 2][:, tile(t)], invT[:, hh, tile(t)], xs[:, hh, tile(t)],
                                      start=(t == 0), stop=(t == TT - 1), skip_group_check=True)
                        for t in range(TT):
                            mm = pe.matmul(ps[5 + hh % 2][:, tile(t)], xs[:, hh, tile(t)], invT[:, hh, tile(t)],
                                           start=(t == 0), stop=(t == TT - 1), skip_group_check=True)
                        mm.then_inc(s["y_mm"], 1)
                pe.wait_ge(s["wt_done"], 32 * grp + 32)
                for hh in range(4):
                    for t in range(TT):
                        mm = pe.matmul(ps[BA[hh]][:, tile(t)], kbe[:, hh, t, :], invT[:, hh, tile(t)],
                                       start=(t == 0), stop=(t == TT - 1), skip_group_check=True)
                    mm.then_inc(s["kc_mm"], 1)
                for hh, hd in enumerate(hs):
                    for t in range(TT):
                        mm = pe.matmul(ps[3 + hh][:, tile(t)], conv[:, GH + hd, tile(t)], conv[:, hd, tile(t)],
                                       start=(t == 0), stop=(t == TT - 1), skip_group_check=True)
                    mm.then_inc(s["qk_mm"], 1)
                pe.wait_ge(s["kc_ready"], 4 * grp + 4)
                pe.wait_ge(s["att_ready"], 4 * grp + 4)
                for t in range(TT):
                    n = (grp * TT + t) * 4
                    for hh in range(4):
                        if t:
                            pe.wait_ge(s["gs_ready"], (grp * 3 + t - 1) * 4 + hh + 1)
                        mm = pe.matmul(ps[BA[hh]][:, 0:P], invT[:, hh, tile(t)], vb[:, hh, t, :], start=True,
                                       stop=(t == 0), skip_group_check=True)
                        if t:
                            mm = pe.matmul(ps[BA[hh]][:, 0:P], kbT[:, hh, tile(t)], gstate[:, hh, :], start=False,
                                           stop=True, skip_group_check=True)
                        mm.then_inc(s["vn_mm"], 1)
                    if t:
                        for hh in range(4):
                            pe.matmul(ps[3 + hh][:, tile(t)], gstate[:, hh, :], qdT[:, hh, tile(t)], start=False,
                                      stop=False, skip_group_check=True)
                    for hh in range(4):
                        pe.wait_ge(s["vn_ready"], n + hh + 1)
                        mm = pe.matmul(ps[3 + hh][:, tile(t)], vnew[:, hh, :], negA[:, hh, tile(t)], start=(t == 0),
                                       stop=(t == TT - 1), skip_group_check=True)
                        if t < TT - 1:
                            pe.matmul(ps[BA[hh]][:, P:2 * P], ktail[:, hh, t, :], vnew[:, hh, :], start=True,
                                      stop=True, skip_group_check=True).then_inc(s["gds_mm"], 1)
                        else:
                            mm.then_inc(s["go_done"], 1)
                for hh in range(4):
                    pe.wait_ge(s["g_sq"], 4 * grp + hh + 1)
                    pe.matmul(ps[BA[hh]][:, :], mean_h[:, :], scr[:, hh, :], start=True,
                              stop=True).then_inc(s["g_sum"], 1)
            if stop_after == "mix1":
                return
            pe.wait_ge(s["mix_ready"], 2 * DC)
            stream("od_out", lambda k: mix1[k])
            peer(1)
            norm_sum(4)

        @block.scalar
        def _(act):
            own = Chain(act, s["act_own"])

            def norm_squares(n):
                for k in range(DC):
                    if n == 0 and k == 0:
                        act.wait_ge(s["x_loaded"], 16)
                        act.wait_ge(s["masks_built"], 1)
                    if n in (1, 3):
                        act.wait_ge(s["acc_free"], STREAMS["ev_out" if n == 1 else "od_out"][0] + 2 + k + 1)
                    if n in (2, 4) and k == 0:
                        act.wait_ge(s["peer_done"], TT * (n // 2))
                    if k >= 4:
                        act.wait_ge(s["sum_ready"], DC * n + k - 3)
                    act.activation(scr[:, k % 4, :], h[:, k, :], ACT.Square).then_inc(s["sq_ready"], 1)
                act.wait_ge(s["sum_ready"], DC * n + DC)
                act.activation(rt[:, :], ps[2][:, :], ACT.Sqrt, bias=eps_col).then_inc(s["root_ready"], 1)

            norm_squares(0)
            act.wait_ge(s["small_loaded"], 16)
            act.activation(cols[:, 16:32], small_in("s5_ldt"), ACT.Exp).then_inc(s["s5_trig_exp"], 1)
            act.wait_ge(s["s5_theta"], 1)
            act.activation(cols[:, 32:48], cols[:, 32:48], ACT.Exp).then_inc(s["s5_trig_exp"], 1)
            act.wait_ge(s["s5_theta"], 2)
            act.activation(cols[:, 416:432], cols[:, 416:432], ACT.Sin)
            act.activation(cols[:, 432:448], cols[:, 432:448], ACT.Sin).then_inc(s["s5_trig"], 1)

            def evac(c0, c, dst):
                act.wait_ge(s["acc_ready"], c0 + c + 1)
                act.activation(dst, ps[c % 2][:, :], ACT.Copy).then_inc(s["acc_free"], 1)

            def s5_copy(st):
                act.wait_ge(s["s5_bu"], st + 1)
                if st >= 2:
                    act.wait_ge(s["s5_y"], st - 1)
                else:
                    act.wait_ge(s["s5_wc"], 1)
                    act.wait_ge(s["tab_pool"], 9)
                for i in range(2):
                    act.activation(s5w[:, st % 2, i, :], ps[3 + 2 * (st % 2) + i][:, :],
                                   ACT.Copy).then_inc(s["s5_bcopy"], 1)

            for c in range(20):
                evac(0, c, proj[:, c, :])
                if c >= 4:
                    s5_copy(c - 4)

            act.wait_ge(s["s5_ysum"], 4)
            act.activation(uT, uT, ACT.Gelu).then_inc(s["s5_gelu"], 1)
            for n in range(4):
                act.wait_ge(s["s5_glu"], n + 1)
                act.activation(scr[:, n, :], ps[3 + n][:, :], ACT.Sigmoid).then_inc(s["s5_sig"], 1)
            act.wait_ge(s["acc_free"], 22)
            act.activation(fT, fT, ACT.Sigmoid).then_inc(s["hg_sig"], 1)
            act.activation(qT, qT, ACT.Silu).then_inc(s["hg_sig"], 1)
            act.activation(gT, gT, ACT.Silu).then_inc(s["hg_sig"], 1)
            act.wait_ge(s["small_loaded"], 16)
            act.wait_ge(s["lb_d"], 1)
            act.activation(cols[:, 4:12], cols[:, 4:12], ACT.Exp).then_inc(s["lb_e"], 1)
            act.wait_ge(s["hg_f"], 4)
            act.wait_ge(s["hg_k"], 1)
            act.activation(fT, fT, ACT.Ln).then_inc(s["hg_ln"], 1)
            act.wait_ge(s["hg_cum"], 1)
            act.activation(eC, fT, ACT.Exp).then_inc(s["hg_exp"], 1)
            act.activation(kE, fT, ACT.Exp, scale=-1.0).then_inc(s["hg_exp"], 1)
            act.wait_ge(s["hg_dif"], 1)
            act.activation(kD, kD, ACT.Exp).then_inc(s["hg_exp"], 1)
            act.activation(totH, fT.rearrange("p h (c l) -> p h c l", l=HC)[:, :, :, HC - 1],
                           ACT.Exp).then_inc(s["hg_exp"], 1)
            for i in range(8):
                act.wait_ge(s["hg_tr"], i + 1)
                dst = (kTok if i < 4 else vTok)[:, i % 4]
                act.activation(dst, ps[3 + i % 4][:, :].rearrange("p (t d) -> p t d", t=TT),
                               ACT.Copy).then_inc(s["hg_trc"], 1)
            BA = (0, 1, 2, 7)
            act.wait_ge(s["mix_ready"], 4)
            for hd in range(HG):
                act.wait_ge(s["hg_o"], hd + 1)
                act.activation(scr[:, hd, :], ps[BA[hd]][:, :], ACT.Square).then_inc(s["hg_sq"], 1)
            for hd in range(HG):
                act.wait_ge(s["hg_sum"], hd + 1)
                act.activation(kE[:, hd, :], ps[3 + hd][:, :], ACT.Sqrt, bias=eps_col).then_inc(s["hg_root"], 1)

            def peer(layer):
                norm_squares(2 * layer + 1)
                for n in range(2 * TT):
                    act.wait_ge(s["xt_tr"], 2 * TT * layer + n + 1)
                    act.activation(xtok[:, n // 2, T * (n % 2):T * (n % 2) + T], ps[3 + n % 2][:, :],
                                   ACT.Copy).then_inc(s["xt_copied"], 1)
                c0, n = STREAMS[f"wq{layer}"]
                with act.Fori(0, n // NSLOT) as i:
                    for j in range(NSLOT):
                        act.wait_ge(s["acc_ready"], i * NSLOT + (c0 + j + 1))
                        act.activation(pq[:, bass.ds(i * NSLOT + j, 1), :].rearrange("p a t -> p (a t)"), ps[j % 2][:, :],
                                       ACT.Copy).then_inc(s["acc_free"], 1)
                for n in range(4 * TT):
                    act.wait_ge(s["sc_mm"], 4 * TT * layer + n + 1)
                    act.activation(sc[:, 2 * n:2 * n + 2, :], ps[3 + n % 4][:, :].rearrange("p (a k) -> p a k", a=2),
                                   ACT.Copy).then_inc(s["sc_ready"], 1)
                act.wait_ge(s["sc_ready"], 4 * TT * (layer + 1))

                own.link(act.activation(sc[:, HEADS, :], sc[:, 0, :], ACT.Copy))

                def route(g, par):
                    if layer or not isinstance(g, int):
                        act.wait_ge(s["ids_ready"], g + (HEADS + 1) * layer)
                    act.activation(sct[:, par, :, :].rearrange("p c k -> p (c k)"),
                                   sc[:, bass.ds(g, 1), :].rearrange("p a k -> p (a k)"),
                                   ACT.Copy).then_inc(s["sct_ready"], 1)
                    act.wait_ge(s["soft_in"], g + ((HEADS + 1) * layer + 1))
                    act.activation(soft_e, sel_v, ACT.Exp, bias=soft_m, accum_out=soft_s).then_inc(s["soft_exp"], 1)

                def head(g, par):
                    act.wait_ge(s["u_free"], g * TOPK + (TOPK * HEADS * layer + TOPK + NU))
                    act.activation(gelu[par], dots[par], ACT.Gelu).then_inc(s["gelu_ready"], 1)
                    act.wait_ge(s["w_ready"], g + (HEADS * layer + 1))
                    for k in range(TOPK):
                        act.wait_ge(s["v_free"], g * TOPK + (TOPK * HEADS * layer + k + 1 + NV - TOPK))
                        act.activation(diag[:, k, :], ident[:, :], ACT.Copy,
                                       scale=wgt[par][:, k:k + 1]).then_inc(s["diag_ready"], 1)

                route(0, 0)
                with act.Fori(0, TT) as t:
                    with act.Fori(0, PH // 2) as p:
                        for par in range(2):
                            g = t * PH + p * 2 + par
                            route(g + 1, 1 - par)
                            head(g, par)

            if stop_after == "mix0":
                return
            peer(0)
            if stop_after == "h1":
                return

            norm_squares(2)
            c0, n = STREAMS["od_in"]
            raw_z = region(4096, 32, T)
            with act.Fori(0, n // NSLOT) as i:
                for j in range(NSLOT):
                    act.wait_ge(s["acc_ready"], i * NSLOT + (c0 + j + 1))
                    act.activation(raw_z[:, bass.ds(i * NSLOT + j, 1), :].rearrange("p a t -> p (a t)"),
                                   ps[j % 2][:, :], ACT.Copy).then_inc(s["acc_free"], 1)
            ab = small_in("ab")
            act.wait_ge(s["ba_mm"], 2)
            act.activation(beta_r, ps[7][0:GH, :], ACT.Sigmoid).then_inc(s["beta_ready"], 1)
            act.wait_ge(s["a_abs"], 1)
            act.activation(soft_r[1], soft_r[1], ACT.Exp, scale=-1.0)
            act.activation(cols[0:GH, 2:3], ab[0:GH, 0:1], ACT.Exp).then_inc(s["a_exp"], 1)
            act.wait_ge(s["a_one"], 1)
            act.activation(soft_r[1], soft_r[1], ACT.Ln).then_inc(s["a_ln"], 1)
            for b in range(6):
                act.wait_ge(s["conv_done"], 4 * b + 4)
                act.activation(conv[:, 4 * b:4 * b + 4, :], conv[:, 4 * b:4 * b + 4, :], ACT.Silu).then_inc(s["silu"], 1)
            act.wait_ge(s["acc_free"], c0 + n + 2)
            act.activation(zT, zT, ACT.Silu).then_inc(s["silu"], 1)
            act.wait_ge(s["silu"], 7)
            for c in range(17):
                if c < 16:
                    if c >= 4:
                        act.wait_ge(s["l2_done"], c - 3)
                    act.activation(scr[:, c % 4, :], conv[:, c, :], ACT.Square).then_inc(s["l2_sq"], 1)
                if c:
                    act.wait_ge(s["l2_sum"], c)
                    act.activation(scr[:, (c - 1) % 4, :], ps[3 + (c - 1) % 4][:, :], ACT.Sqrt,
                                   bias=eps_col).then_inc(s["l2_root"], 1)
            act.wait_ge(s["col_tr"], 1)
            act.activation(cols[:, 64:128], ps[0][:, 0:64], ACT.Copy).then_inc(s["cols_ready"], 1)
            BA = (0, 1, 2, 7)
            for grp in range(2):
                hs = range(4 * grp, 4 * grp + 4)
                for hh in range(4):
                    act.wait_ge(s["bc_mm"], 4 * grp + hh + 1)
                    act.activation(qdT[:, hh, :], ps[3 + hh][:, :], ACT.Exp).then_inc(s["gq_exp"], 1)
                for hh in range(4):
                    act.wait_ge(s["lm_min"], 4 * grp + hh + 1)
                    act.activation(lmT[:, hh, :], lmT[:, hh, :], ACT.Exp).then_inc(s["lm_exp"], 1)
                hsl = slice(4 * grp, 4 * grp + 4)
                act.wait_ge(s["last_ready"], grp + 1)
                act.activation(kbe_c[:, :, hsl], dec_c[:, :, hsl], ACT.Exp)
                act.activation(tail_c[:, :, hsl], tail_c[:, :, hsl], ACT.Exp)
                act.activation(tot_c[:, hsl, :], last_c[:, hsl, :], ACT.Exp).then_inc(s["small_exp"], 1)
                act.wait_ge(s["scale_cols"], grp + 1)
                for hh, hd in enumerate(hs):
                    act.wait_ge(s["ktr_mm"], 4 * grp + hh + 1)
                    for t in range(TT):
                        m = act.activation(kbe[:, hh, t, :], ps[3 + hh][:, P * t:P * t + P], ACT.Copy,
                                           scale=kbe_c[:, t, hd:hd + 1])
                    m.then_inc(s["kbe_ready"], 1)
                for hh, hd in enumerate(hs):
                    act.wait_ge(s["vtr_mm"], 4 * grp + hh + 1)
                    for t in range(TT):
                        m = act.activation(vb[:, hh, t, :], ps[BA[hh]][:, P * t:P * t + P], ACT.Copy,
                                           scale=beta_c[:, t, hd:hd + 1])
                    m.then_inc(s["vb_ready"], 1)
                with act.Fori(0, 7) as l:
                    for hh in range(4):
                        act.wait_ge(s["x_mm"], l * 4 + (28 * grp + hh + 1))
                        act.activation(xs[:, hh, :], ps[BA[hh]][:, :], ACT.Copy).then_inc(s["xs_copied"], 1)
                for hh in range(4):
                    act.wait_ge(s["kc_mm"], 4 * grp + hh + 1)
                    act.activation(kbT[:, hh, :], ps[BA[hh]][:, :], ACT.Copy, scale=-1.0).then_inc(s["kc_ready"], 1)
                for t in range(TT):
                    for hh in range(4):
                        act.wait_ge(s["vn_mm"], (grp * TT + t) * 4 + hh + 1)
                        act.activation(vnew[:, hh, :], ps[BA[hh]][:, 0:P], ACT.Copy).then_inc(s["vn_ready"], 1)
                for hh in range(4):
                    act.wait_ge(s["go_done"], 4 * grp + hh + 1)
                    act.activation(scr[:, hh, :], ps[3 + hh][:, :], ACT.Square).then_inc(s["g_sq"], 1)
                for hh in range(4):
                    act.wait_ge(s["g_sum"], 4 * grp + hh + 1)
                    act.activation(lmT[:, hh, :], ps[BA[hh]][:, :], ACT.Sqrt, bias=eps_col).then_inc(s["g_root"], 1)
            if stop_after == "mix1":
                return
            peer(1)
            norm_squares(4)

        @block.vector
        def _(dve):
            own = Chain(dve, s["dve_own"])
            link = own.link

            def alone():
                dve.sem_inc(s["dve_passed"], 1)

            tt, ts = dve.tensor_tensor, dve.tensor_scalar
            stt = dve.scalar_tensor_tensor

            dve.memset(eps_col, EPS).then_inc(s["acc_free"], 2)
            dve.wait_ge(s["const_pool"], 1)
            row = scr[:, 0, 0:P].bitcast(U32)
            col = scr[:, 0, P:2 * P].bitcast(U32)
            xr = scr[:, 0, 2 * P:3 * P].bitcast(U32)
            sh = scr[:, 0, 3 * P:4 * P].bitcast(U32)
            up = scr[:, 2, 0:P]
            dn = scr[:, 2, P:2 * P]
            tok = scr[:, 1, :].bitcast(U32)
            m32row = scr[:, 3, :]
            tt(xr, row, col, ALU.bitwise_xor)
            tt(up, row, col, ALU.is_lt)
            link(tt(dn, row, col, ALU.is_gt))
            link(ts(sh, xr, 5, None, ALU.logical_shift_right))
            link(ts(sh.bitcast(F32), sh, 0, None, ALU.is_equal))
            link(tt(mask32[:, :], sh.bitcast(F32), maskc[:, :], ALU.mult))
            dve.memset(rt[:, :], 0.0).then_inc(s["masks_built"], 1)
            dve.wait_ge(s["masks_built"], 1)

            def norm_apply(n, dst):
                dve.wait_ge(s["root_ready"], n + 1)
                link(dve.reciprocal(rt[:, :], rt[:, :]))
                for k in range(DC):
                    stt(dst[:, k, :], h[:, k, :], norm_w[:, n, k:k + 1], rt[:, :], ALU.mult,
                        ALU.mult).then_inc(s["hn_ready"], 1)

            dve.wait_ge(s["small_loaded"], 16)
            norm_apply(0, hn)
            are, aim = small_in("s5_are"), small_in("s5_aim")
            dt_, mag, th = cols[:, 16:32], cols[:, 32:48], cols[:, 48:64]
            c1, s1 = cols[:, 128:144], cols[:, 144:160]
            sn_h, sn = cols[:, 416:432], cols[:, 432:448]
            t0, t1, t2, den = (cols[:, 448 + 16 * i:464 + 16 * i] for i in range(4))
            dve.wait_ge(s["s5_trig_exp"], 1)
            tt(mag, are, dt_, ALU.mult).then_inc(s["s5_theta"], 1)
            link(tt(th, aim, dt_, ALU.mult))
            link(ts(t0, th, 1.0 / 6.283185307179586, ROUND, ALU.mult, ALU.add))
            link(ts(t0, t0, -ROUND, None, ALU.add))
            link(stt(t1, t0, -TWO_PI_HI, th, ALU.mult, ALU.add))
            link(stt(t1, t0, -TWO_PI_LO, t1, ALU.mult, ALU.add))
            link(ts(t1, t1, -3.1415925, 3.1415925, ALU.max, ALU.min))
            ts(sn_h, t1, 0.5, None, ALU.mult)
            dve.tensor_copy(sn, t1).then_inc(s["s5_theta"], 1)
            dve.wait_ge(s["s5_trig"], 1)
            link(stt(t0, sn_h, -2.0, sn_h, ALU.mult, ALU.mult))
            dve.tensor_copy(s1, sn)
            link(ts(c1, t0, 1.0, None, ALU.add))
            for m in range(9):
                if m:
                    pc, psn = cols[:, 96 + 32 * m:112 + 32 * m], cols[:, 112 + 32 * m:128 + 32 * m]
                    nco, nsn = cols[:, 128 + 32 * m:144 + 32 * m], cols[:, 144 + 32 * m:160 + 32 * m]
                    tt(t0, pc, pc, ALU.mult)
                    tt(t1, psn, psn, ALU.mult)
                    link(stt(nsn, pc, 2.0, psn, ALU.mult, ALU.mult))
                    link(tt(nco, t0, t1, ALU.subtract))
                    tt(t0, nco, nco, ALU.mult)
                    link(tt(t1, nsn, nsn, ALU.mult))
                    link(tt(t0, t0, t1, ALU.add))
                    link(ts(t0, t0, -0.5, 1.5, ALU.mult, ALU.add))
                    tt(nco, nco, t0, ALU.mult)
                    link(tt(nsn, nsn, t0, ALU.mult))
            dve.memset(tab_c[:, :, 0:1], 1.0)
            link(dve.memset(tab_s[:, :, 0:1], 0.0))
            dve.memset(t2, 0.0).then_inc(s["s5_ctab"], 9)
            dve.wait_ge(s["s5_ctab"], 9)
            for m in range(9):
                w = 1 << m
                if m:
                    dve.wait_ge(s["tab_pool"], m)
                step = min(w, 128)
                cmb = cols[:, 128 + 32 * m:144 + 32 * m].unsqueeze(2).to_broadcast([P, ST, step])
                smb = cols[:, 144 + 32 * m:160 + 32 * m].unsqueeze(2).to_broadcast([P, ST, step])
                for a in range(0, w, step):
                    tmp = s5t(0, step)
                    tt(tab_c[:, :, w + a:w + a + step], tab_c[:, :, a:a + step], cmb, ALU.mult)
                    link(tt(tmp, tab_s[:, :, a:a + step], smb, ALU.mult))
                    last = tt(tab_c[:, :, w + a:w + a + step], tab_c[:, :, w + a:w + a + step], tmp, ALU.subtract)
                    if a + step < w:
                        link(last)
                last.then_inc(s["tab_dve"], 1)
                dve.wait_ge(s["tab_dve"], m + 1)
            dve.wait_ge(s["s5_trig_exp"], 2)
            cr, ci = cols[:, 512:528], cols[:, 528:544]
            tt(t0, mag, c1, ALU.mult)
            tt(t1, mag, s1, ALU.mult)
            tt(t2, are, are, ALU.mult)
            link(tt(den, aim, aim, ALU.mult))
            ts(t0, t0, -1.0, None, ALU.add)
            link(tt(den, den, t2, ALU.add))
            link(dve.reciprocal(den, den))
            tt(cr, t0, are, ALU.mult)
            link(tt(t2, t1, aim, ALU.mult))
            link(tt(cr, cr, t2, ALU.add))
            tt(cr, cr, den, ALU.mult)
            tt(ci, t1, are, ALU.mult)
            link(tt(t2, t0, aim, ALU.mult))
            link(tt(ci, ci, t2, ALU.subtract))
            link(tt(ci, ci, den, ALU.mult))
            dve.wait_ge(s["bc_loaded"], 32)
            dve.wait_ge(s["tab_pool"], 9)
            crb = cr.unsqueeze(2).to_broadcast([P, ST, 32])
            cib = ci.unsqueeze(2).to_broadcast([P, ST, 32])
            pr = [tab_t[:, 0, 512 * i:512 * i + 512].rearrange("p (a b) -> p a b", a=ST) for i in range(4)]
            tt(pr[0], cw[:, 0], crb, ALU.mult)
            tt(pr[1], cw[:, 1], cib, ALU.mult)
            tt(pr[2], cw[:, 0], cib, ALU.mult)
            link(tt(pr[3], cw[:, 1], crb, ALU.mult))
            tt(cw[:, 0], pr[0], pr[1], ALU.subtract)
            link(tt(cw[:, 1], pr[2], pr[3], ALU.add))
            link(ts(cw[:, 1], cw[:, 1], -1.0, None, ALU.mult))
            dve.memset(t0, 0.0).then_inc(s["s5_wc"], 1)

            for st in range(ST):
                W = s5w[:, st % 2]
                dve.wait_ge(s["s5_bcopy"], 2 * st + 2)
                if st >= 2:
                    dve.wait_ge(s["s5_y"], st - 1)
                tt(W[:, 4, :], W[:, 0, :], tab_c[:, st, :], ALU.mult)
                link(tt(W[:, 2, :], W[:, 1, :], tab_s[:, st, :], ALU.mult))
                link(tt(W[:, 2, :], W[:, 4, :], W[:, 2, :], ALU.add))
                magb = mag[:, st:st + 1].to_broadcast([P, T])
                dve.tensor_tensor_scan(W[:, 2, :], magb, W[:, 2, :], 0.0, ALU.mult, ALU.add).then_inc(s["s5_scan"], 1)
                dve.wait_ge(s["s5_wi"], st + 1)
                dve.tensor_tensor_scan(W[:, 3, :], magb, W[:, 3, :], 0.0, ALU.mult, ALU.add).then_inc(s["s5_scan"], 1)
                dve.wait_ge(s["s5_scan"], 2 * st + 2)
                tt(W[:, 0, :], W[:, 2, :], tab_c[:, st, :], ALU.mult)
                stt(W[:, 4, :], W[:, 3, :], -1.0, tab_s[:, st, :], ALU.mult, ALU.mult).then_inc(s["s5_pr"], 1)
                if st % 4 == 3:
                    q = st // 4
                    dve.wait_ge(s["s5_y"], st + 1)
                    stt(uT[:, q, :], uT[:, q, :], small_in("s5_d")[:, q:q + 1], ps[7][:, :], ALU.mult,
                        ALU.add).then_inc(s["s5_ysum"], 1)
            dve.wait_ge(s["s5_gelu"], 1)
            for n in range(4):
                dve.wait_ge(s["s5_sig"], n + 1)
                if n == 0:
                    dve.wait_ge(s["s5_glu"], 4)
                tt(uT[:, n, :], uT[:, n, :], scr[:, n, :], ALU.mult).then_inc(s["mix_ready"], 1)

            lb = small_in("lb").rearrange("p (r c) -> p r c", r=2)
            le = cols[:, 4:12].rearrange("p (r c) -> p r c", r=2)
            lbm = cols[:, 448:452]
            lbv, oml = cols[:, 452:456], cols[:, 456:460]
            link(tt(lbm, lb[:, 0], lb[:, 1], ALU.max))
            tt(le[:, 0], lb[:, 0], lbm, ALU.subtract)
            link(tt(le[:, 1], lb[:, 1], lbm, ALU.subtract))
            dve.memset(cols[:, 1:2], 0.0).then_inc(s["lb_d"], 1)
            dve.wait_ge(s["lb_e"], 1)
            link(tt(lbm, le[:, 0], le[:, 1], ALU.add))
            link(dve.reciprocal(lbm, lbm))
            link(tt(lbv, le[:, 0], lbm, ALU.mult))
            link(ts(oml, lbv, -1.0, 1.0, ALU.mult, ALU.add))
            dve.wait_ge(s["hg_sig"], 3)
            for hd in range(HG):
                ts(fT[:, hd, :], fT[:, hd, :], oml[:, hd:hd + 1], lbv[:, hd:hd + 1], ALU.mult,
                   ALU.add).then_inc(s["hg_f"], 1)
            m32 = rt[:, :]
            link(dve.memset(m32, 1.0))
            link(dve.memset(m32.rearrange("p (c l) -> p c l", l=HC)[:, :, 0:1], 0.0))
            dve.wait_ge(s["hg_ln"], 1)
            for hd in range(HG):
                link(dve.tensor_tensor_scan(fT[:, hd, :], m32, fT[:, hd, :], 0.0, ALU.mult, ALU.add))
            f4 = fT.rearrange("p h (c l) -> p (h c) l", l=HC)
            d4 = kD.rearrange("p h (c l) -> p (h c) l", l=HC)
            tt(d4, f4[:, :, HC - 1:HC].to_broadcast([P, HG * NCH, HC]), f4, ALU.subtract).then_inc(s["hg_dif"], 1)
            dve.memset(cols[:, 1:2], 0.0).then_inc(s["hg_cum"], 1)
            dve.wait_ge(s["hg_exp"], 1)
            stt(qT, qT, HGRN_SCALE, eC, ALU.mult, ALU.mult).then_inc(s["hg_ke"], 1)
            dve.wait_ge(s["hg_exp"], 2)
            dve.wait_ge(s["hg_k"], 1)
            tt(kE, kA, kE, ALU.mult).then_inc(s["hg_ke"], 1)
            dve.wait_ge(s["hg_ke"], 2)
            BA = (0, 1, 2, 7)
            for hd in range(HG):
                dve.wait_ge(s["hg_att"], hd + 1)
                tt(eC[:, hd, :].rearrange("p (t x) -> p t x", t=TT), ps[BA[hd]][:, :].rearrange("p (t x) -> p t x", t=TT),
                   mask32[:, :].unsqueeze(1).to_broadcast([P, TT, P]), ALU.mult).then_inc(s["hg_attm"], 1)
            dve.wait_ge(s["hg_exp"], 4)
            for hd in range(HG):
                dve.wait_ge(s["hg_ds"], hd + 1)
                for n in range(NCH - 1):
                    t, j = n // 4, n % 4
                    ds = ps[3 + j][:, P * t:P * t + P]
                    if n == 0:
                        dve.tensor_copy(statesA[hd][:, 1, :], ds).then_inc(s["hg_st"], 1)
                    else:
                        stt(statesA[hd][:, n + 1, :], statesA[hd][:, n, :], totH[:, hd, n:n + 1], ds, ALU.mult,
                            ALU.add).then_inc(s["hg_st"], 1)
                    dve.wait_ge(s["hg_st"], 15 * hd + n + 1)
            for hd in range(HG):
                dve.wait_ge(s["hg_root"], hd + 1)
                link(dve.reciprocal(kE[:, hd, :], kE[:, hd, :]))
                link(stt(kA[:, hd, :], ps[BA[hd]][:, :], gn_col[:, 0:1], kE[:, hd, :], ALU.mult, ALU.mult))
                tt(qT[:, hd, :], kA[:, hd, :], gT[:, hd, :], ALU.mult).then_inc(s["mix_ready"], 1)

            def add_stream(name):
                c0, n = STREAMS[name]
                with dve.Fori(0, n // NSLOT) as i:
                    for j in range(NSLOT):
                        dve.wait_ge(s["acc_ready"], i * NSLOT + (c0 + j + 1))
                        hc = h[:, bass.ds(i * NSLOT + j, 1), :].rearrange("p a t -> p (a t)")
                        tt(hc, hc, ps[j % 2][:, :], ALU.add).then_inc(s["acc_free"], 1)

            def peer(layer):
                norm_apply(2 * layer + 1, phn)
                dve.wait_ge(s["sc_ready"], 4 * TT * (layer + 1))

                def route(g, par):
                    dve.wait_ge(s["sct_ready"], g + ((HEADS + 1) * layer + 1))
                    alone()
                    for lo in (0, 8):
                        for c in range(2):
                            m = dve.max(top_v[:, c, lo:lo + 8], sct[:, par, c, :])
                        link(m)
                        alone()
                        for c in range(2):
                            m = dve.max_index(top_i[:, c, lo:lo + 8], top_v[:, c, lo:lo + 8], sct[:, par, c, :])
                        if lo == 0:
                            link(m)
                            alone()
                            for c in range(2):
                                m = dve.match_replace(sct[:, par, c, :], top_v[:, c, 0:8], sct[:, par, c, :], LOWEST)
                        link(m)
                        if lo == 0:
                            alone()
                    dve.tensor_copy(top_f, top_i)
                    link(tt(cand.rearrange("p (a b) -> p a b", a=TOPK),
                            top_v[:, 0, :].unsqueeze(2).to_broadcast([P, TOPK, TOPK]),
                            top_v[:, 1, :].unsqueeze(1).to_broadcast([P, TOPK, TOPK]), ALU.add))
                    alone()
                    link(dve.max(sel_v[:, 0:8], cand))
                    alone()
                    link(dve.max_index(sel_p[:, 0:8], sel_v[:, 0:8], cand))
                    ts(soft_m, sel_v[:, 0:1], -1.0, None, ALU.mult)
                    link(dve.match_replace(cand, sel_v[:, 0:8], cand, LOWEST))
                    alone()
                    dve.max(sel_v[:, 8:16], cand).then_inc(s["soft_in"], 1)
                    dve.wait_ge(s["soft_in"], g + ((HEADS + 1) * layer + 1))
                    alone()
                    link(dve.max_index(sel_p[:, 8:16], sel_v[:, 8:16], cand))
                    ts(sel_a, sel_p, 4, None, ALU.logical_shift_right)
                    link(ts(sel_b, sel_p, TOPK - 1, None, ALU.bitwise_and))
                    dve.tensor_copy(pos_a, sel_a)
                    link(dve.tensor_copy(pos_b, sel_b))
                    for pos, dst, c in ((pos_a, exp_a, 0), (pos_b, exp_b, 1)):
                        link(tt(hot, pos.unsqueeze(2).to_broadcast([P, TOPK, TOPK]),
                                iota16[:, :].unsqueeze(1).to_broadcast([P, TOPK, TOPK]), ALU.is_equal))
                        link(tt(hot, hot, top_f[:, c, :].unsqueeze(1).to_broadcast([P, TOPK, TOPK]), ALU.mult))
                        link(dve.tensor_reduce(dst, hot, AX.X, ALU.add))
                    link(stt(exp_a, exp_a, float(NK), exp_b, ALU.mult, ALU.add))
                    link(ts(ids[par], exp_a, float(layer * E), None, ALU.add))
                    dve.wait_ge(s["soft_exp"], g + ((HEADS + 1) * layer + 1))
                    link(dve.reciprocal(soft_s, soft_s))
                    ts(gate[par], soft_e, soft_s, None, ALU.mult).then_inc(s["ids_ready"], 1)

                def head(g, par):
                    for k in range(TOPK):
                        dve.wait_ge(u_arrived[k % NU],
                                    (g * (TOPK // NU) + (HEADS * layer * (TOPK // NU) + k // NU + 1)) * 16)
                        dve.tensor_tensor_reduce(uring[:, k % NU, :], uring[:, k % NU, :], xcur, 1.0, 0.0, ALU.mult,
                                                 ALU.add, dots[par][:, k:k + 1]).then_inc(s["u_free"], 1)
                    dve.wait_ge(s["gelu_ready"], g + (HEADS * layer + 1))
                    dve.wait_ge(s["ids_ready"], g + ((HEADS + 1) * layer + 1))
                    tt(wgt[par], gelu[par], gate[par], ALU.mult).then_inc(s["w_ready"], 1)
                    dve.wait_ge(s["v_free"], g * TOPK + (TOPK * HEADS * layer + TOPK + NV))
                    for i in range(2):
                        m = tt(yacc[:, T * i:T * i + T], yacc[:, T * i:T * i + T], ps[4 + 2 * par + i][:, :], ALU.add)
                    m.then_inc(s["y_added"], 1)
                    dve.wait_ge(s["y_added"], g + (HEADS * layer + 3))
                    alone()

                route(0, 0)
                tile_links, pair_links = 1, 2 * ROUTE_LINKS
                per_tile = tile_links + (PH // 2) * pair_links
                start = own.base + own.k
                with dve.Fori(0, TT) as t:
                    own.base, own.k = t * per_tile + start, 0
                    dve.tensor_copy(xcur, xtok[:, bass.ds(t, 1), :].rearrange("p a d -> p (a d)"))
                    link(dve.memset(yacc, 0.0))
                    alone()
                    with dve.Fori(0, PH // 2) as p:
                        own.base, own.k = t * per_tile + p * pair_links + (start + tile_links), 0
                        for par in range(2):
                            g = t * PH + p * 2 + par
                            route(g + 1, 1 - par)
                            head(g, par)
                        assert own.k == pair_links, own.k
                    dve.wait_ge(s["yT_ready"], t + (TT * layer + 1))
                    for i in range(2):
                        hc = h[:, 4 * i:4 * i + 4, bass.ds(t * P, P)]
                        m = tt(hc, hc, ps[2 + i][:, :].rearrange("p (k t) -> p k t", k=4), ALU.add)
                    m.then_inc(s["peer_done"], 1)
                    dve.wait_ge(s["peer_done"], t + (TT * layer + 1))
                    alone()
                own.base, own.k = start + TT * per_tile, 0

            if stop_after == "mix0":
                return
            dve.memset(cols[:, 1:2], 0.0).then_inc(s["u_free"], NU)
            dve.memset(cols[:, 2:3], 0.0).then_inc(s["v_free"], NV)
            dve.memset(cols[:, 3:4], 0.0).then_inc(s["y_added"], 2)
            add_stream("ev_out")
            peer(0)
            if stop_after == "h1":
                return

            norm_apply(2, hn)
            row = lmT[:, 0, 0:P].bitcast(U32)
            col = lmT[:, 0, P:2 * P].bitcast(U32)
            xr = lmT[:, 0, 2 * P:3 * P].bitcast(U32)
            sh = lmT[:, 0, 3 * P:4 * P].bitcast(U32)
            up, dn, shf = lmT[:, 1, 0:P], lmT[:, 1, P:2 * P], lmT[:, 1, 2 * P:3 * P]
            dve.wait_ge(s["lm_iota"], 1)
            tt(xr, row, col, ALU.bitwise_xor)
            tt(up, row, col, ALU.is_lt)
            link(tt(dn, row, col, ALU.is_gt))
            for l in range(7):
                link(ts(sh, xr, l, None, ALU.logical_shift_right))
                link(ts(shf, sh, 1, None, ALU.is_equal))
                tt(maskl[:, 0, l, :], shf, dn, ALU.mult)
                link(tt(maskl[:, 1, l, :], shf, up, ALU.mult))

            conv_links = 3
            start = own.base + own.k
            with dve.Fori(0, 12) as i:
                own.base, own.k = i * conv_links + start, 0
                dve.wait_ge(s["acc_free"], i * 2 + (STREAMS["od_in"][0] + 2 + 2))
                for j in (3, 2, 1, 0):
                    d = 3 - j
                    for e in range(2):
                        c = bass.ds(i * 2 + e, 1)
                        w = conv_w[:, c, j:j + 1].rearrange("p a b -> p (a b)")
                        src = raw[:, c, 0:T - d].rearrange("p a t -> p (a t)")
                        dst = conv[:, c, d:T].rearrange("p a t -> p (a t)")
                        m = ts(dst, src, w, None, ALU.mult) if d == 0 else stt(dst, src, w, dst, ALU.mult, ALU.add)
                    if j:
                        link(m)
                m.then_inc(s["conv_done"], 2)
            own.base, own.k = start + 12 * conv_links, 0

            ab = small_in("ab")
            dve.wait_ge(s["ba_mm"], 2)
            link(ts(soft_r[0], ps[2][0:GH, :], ab[0:GH, 1:2], None, ALU.add))
            stt(soft_r[1], soft_r[0], -1.0, soft_r[0], ALU.mult, ALU.max).then_inc(s["a_abs"], 1)
            dve.memset(soft_r[3], 1.0)
            link(ts(soft_r[0], soft_r[0], 0.0, None, ALU.max))
            dve.memset(soft_r[3].rearrange("p (t x) -> p t x", t=TT)[:, :, 0:1], 0.0)
            dve.wait_ge(s["a_exp"], 1)
            ts(soft_r[1], soft_r[1], 1.0, None, ALU.add).then_inc(s["a_one"], 1)
            link(ts(cols[0:GH, 2:3], cols[0:GH, 2:3], -1.0, None, ALU.mult))
            dve.wait_ge(s["a_ln"], 1)
            link(tt(soft_r[0], soft_r[0], soft_r[1], ALU.add))
            link(ts(soft_r[0], soft_r[0], cols[0:GH, 2:3], None, ALU.mult))
            dve.tensor_tensor_scan(dec_r, soft_r[3], soft_r[0], 0.0, ALU.mult, ALU.add).then_inc(s["dec_ready"], 1)

            for c in range(16):
                dve.wait_ge(s["l2_root"], c + 1)
                r = scr[:, c % 4, :]
                link(dve.reciprocal(r, r))
                stt(conv[:, c, :], conv[:, c, :], GDN_SCALE if c < GH else 1.0, r, ALU.mult,
                    ALU.mult).then_inc(s["l2_done"], 1)

            for grp in range(2):
                hs = range(4 * grp, 4 * grp + 4)
                dve.wait_ge(s["cols_ready"], 1)
                dve.wait_ge(s["l2_done"], 16)
                for hh, hd in enumerate(hs):
                    dve.wait_ge(s["bc_mm"], 4 * grp + hh + 1)
                    tt(kbT[:, hh, :], conv[:, GH + hd, :], ps[BA[hh]][:, :], ALU.mult).then_inc(s["kb_ready"], 1)
                    dve.wait_ge(s["gq_exp"], 4 * grp + hh + 1)
                    dve.tensor_copy(last_c[:, hd, :], ps[3 + hh][:, :].rearrange("p (t x) -> p t x", t=TT)[:, :, P - 1])
                    for t in range(TT):
                        m = ts(lmT[:, hh, P * t:P * t + P], ps[3 + hh][:, P * t:P * t + P], dec_c[:, t, hd:hd + 1], 0.0,
                               ALU.subtract, ALU.min)
                    m.then_inc(s["lm_min"], 1)
                dve.wait_ge(s["lm_min"], 4 * grp + 4)
                hsl = slice(4 * grp, 4 * grp + 4)
                tt(tail_c[:, :, hsl], last_c[:, hsl, :].rearrange("p h t -> p t h"), dec_c[:, :, hsl],
                   ALU.subtract).then_inc(s["last_ready"], 1)
                dve.wait_ge(s["small_exp"], grp + 1)
                tt(kbe_c[:, :, hsl], kbe_c[:, :, hsl], beta_c[:, :, hsl], ALU.mult).then_inc(s["scale_cols"], 1)
                for hh, hd in enumerate(hs):
                    dve.wait_ge(s["gq_exp"], 4 * grp + hh + 1)
                    tt(qdT[:, hh, :], conv[:, hd, :], qdT[:, hh, :], ALU.mult).then_inc(s["qd_ready"], 1)
                for hh in range(4):
                    dve.wait_ge(s["kk_mm"], 4 * grp + hh + 1)
                    dve.wait_ge(s["lm_exp"], 4 * grp + hh + 1)
                    stt(negA[:, hh, :], ps[BA[hh]][:, :], -1.0, lmT[:, hh, :], ALU.mult,
                        ALU.mult).then_inc(s["negA_ready"], 1)
                for hh, hd in enumerate(hs):
                    dve.wait_ge(s["kbe_ready"], 4 * grp + hh + 1)
                    for t in range(TT):
                        m = ts(ktail[:, hh, t, :], ps[3 + hh][:, P * t:P * t + P], tail_c[:, t, hd:hd + 1], None,
                               ALU.mult)
                    m.then_inc(s["ktail_ready"], 1)
                eye = ident[:, :].unsqueeze(1).to_broadcast([P, TT, P])
                for hh in range(4):
                    dve.tensor_copy(inv[:, hh, :].rearrange("p (t x) -> p t x", t=TT), eye)
                    dve.tensor_copy(invT[:, hh, :].rearrange("p (t x) -> p t x", t=TT), eye).then_inc(s["wt_done"], 1)
                dve.wait_ge(s["wt_done"], 32 * grp + 4)
                start = own.base + own.k
                with dve.Fori(0, 7) as l:
                    own.base, own.k = l + start, 0
                    link(dve.tensor_copy(mcur, maskl[:, :, bass.ds(l, 1), :].rearrange("p a b x -> p a (b x)")))
                    for hh in range(4):
                        dve.wait_ge(s["y_mm"], l * 4 + (28 * grp + hh + 1))
                        alone()
                        for m, (dst, bank) in enumerate(((inv, 3), (invT, 5))):
                            q = dve.copy_predicated(dst[:, hh, :].rearrange("p (t x) -> p t x", t=TT),
                                                    mcur[:, m, :].bitcast(U32).unsqueeze(1).to_broadcast([P, TT, P]),
                                                    ps[bank + hh % 2][:, :].rearrange("p (t x) -> p t x", t=TT))
                        q.then_inc(s["wt_done"], 1)
                    dve.wait_ge(s["wt_done"], l * 4 + (32 * grp + 8))
                    alone()
                own.base, own.k = start + 7, 0
                for hh in range(4):
                    dve.wait_ge(s["qk_mm"], 4 * grp + hh + 1)
                    tt(negA[:, hh, :], ps[3 + hh][:, :], lmT[:, hh, :], ALU.mult).then_inc(s["att_raw"], 1)
                for t in range(TT - 1):
                    for hh, hd in enumerate(hs):
                        n = (grp * 3 + t) * 4 + hh + 1
                        dve.wait_ge(s["gds_mm"], n)
                        ds = ps[BA[hh]][:, P:2 * P]
                        if t:
                            m = stt(gstate[:, hh, :], gstate[:, hh, :], tot_c[:, hd, t:t + 1], ds, ALU.mult, ALU.add)
                        else:
                            m = dve.tensor_copy(gstate[:, hh, :], ds)
                        m.then_inc(s["gs_ready"], 1)
                    dve.wait_ge(s["gs_ready"], (grp * 3 + t) * 4 + 4)
                for hh, hd in enumerate(hs):
                    dve.wait_ge(s["g_root"], 4 * grp + hh + 1)
                    link(dve.reciprocal(lmT[:, hh, :], lmT[:, hh, :]))
                    link(stt(xs[:, 2, :], ps[3 + hh][:, :], gn_col[:, 1:2], lmT[:, hh, :], ALU.mult, ALU.mult))
                    tt(zT[:, hd, :], xs[:, 2, :], zT[:, hd, :], ALU.mult).then_inc(s["mix_ready"], 1)
                    dve.wait_ge(s["mix_ready"], 8 + 4 * grp + hh + 1)
            if stop_after == "mix1":
                return
            add_stream("od_out")
            peer(1)
            norm_apply(4, hn)


def host_layout(i):
    import numpy as np
    f = {k: np.asarray(v) for k, v in i.items()}

    def chunks(w):
        k, n = w.shape
        return w.reshape(k // P, P, n // P, P).transpose(2, 1, 0, 3)

    def rows(w, c):
        return np.moveaxis(w.reshape((c, P) + w.shape[1:]), 0, 1)

    ev = f["ev_in_w"][0]
    ev = np.concatenate([ev[:, 2048:2560], ev[:, 0:2048]], axis=1)
    od = f["od_in_w"][0]
    wall = np.concatenate([chunks(w) for w in (ev, f["ev_out_w"][0], f["peer_wq"][0], od[:, 0:4096],
                                               f["od_out_w"][0], f["peer_wq"][1])])
    norm = np.concatenate([f["norm_mix_w"][0:1], f["norm_ffn_w"][0:1], f["norm_mix_w"][1:2],
                           f["norm_ffn_w"][1:2], f["norm_out_w"][None]])
    b = np.zeros((4, 2, 16, 2, 4, 2, 64), np.float32)
    c = np.zeros((2, 64, 2, ST, 2, 16), np.float32)
    for n, (bn, cn) in enumerate((("s5_b_re", "s5_c_re"), ("s5_b_im", "s5_c_im"))):
        bb = f[bn][0].reshape(4, 4, 2, 64, 16)
        cc = f[cn][0].reshape(ST, 2, 16, 64)
        for g in range(2):
            b[:, g, :, n, :, g, :] = bb[:, :, g].transpose(1, 3, 0, 2)
            c[g, :, n, :, g, :] = cc[:, g].transpose(2, 0, 1)
    ab = np.zeros((P, 2), np.float32)
    ab[0:GH, 0], ab[0:GH, 1] = f["gdn_a_log"][0], f["gdn_dt_bias"][0]
    parts = {
        "norm_w": norm.reshape(5, DC, P).transpose(2, 0, 1),
        "s5_are": f["s5_a_re"][0].reshape(ST, P).T,
        "s5_aim": f["s5_a_im"][0].reshape(ST, P).T,
        "s5_ldt": np.repeat(f["s5_log_dt"][0], 64).reshape(ST, P).T,
        "s5_d": f["s5_d"][0].reshape(4, P).T,
        "lb": f["hgrn_lb"].reshape(2, 4, P).transpose(2, 0, 1),
        "gn": np.stack([f["hgrn_gn_w"][0], f["gdn_gn_w"][0]], axis=1),
        "conv": f["gdn_conv_w"][0].reshape(4, 24, P).transpose(2, 1, 0),
        "ab": ab,
        "ba_w": rows(od[:, 4096:4112], DC),
        "keys": f["peer_sub_keys"].transpose(3, 0, 1, 2),
    }
    small = np.concatenate([parts[n].reshape(P, w) for n, w in SMALL], axis=1)
    return {
        "xT": rows(f["x"][0].T, DC), "wall": wall, "glu_w": rows(f["s5_glu_w"][0], 4),
        "s5_b": b.reshape(P, 2, 4, P), "s5_c": c.reshape(P, 2, ST, 32), "small": small,
        "u_tab": f["peer_u"].reshape(2 * E, D), "v_tab": f["peer_v"].reshape(2 * E, D),
    }


def kernel(**inputs):
    import numpy as np
    import concourse.bacc as bacc
    from concourse.bass_utils import run_bass_kernel_spmd

    nc = bacc.Bacc("TRN2", target_bir_lowering=False, num_devices=1)
    arrays = {n: np.ascontiguousarray(a) for n, a in host_layout(inputs).items()}
    args = [nc.dram_tensor(n, a.shape, mybir.dt.from_np(a.dtype), kind="ExternalInput").ap()
            for n, a in arrays.items()]
    out = nc.dram_tensor("out", (P, DC, T), F32, kind="ExternalOutput").ap()
    trunk(nc, *args, out)
    r = run_bass_kernel_spmd(nc, [arrays], core_ids=[0])
    got = r.results[0]["out"]
    return got.transpose(2, 1, 0).reshape(1, T, D)
```

```python
from contextlib import ExitStack

import concourse.bass as bass
from concourse import mybir

F32 = mybir.dt.float32
I32 = mybir.dt.int32
U32 = mybir.dt.uint32
ALU = mybir.AluOpType
ACT = mybir.ActivationFunctionType
AX = mybir.AxisListType

P = 128
D = 1024
T = 512
DC = D // P
TT = T // P
HG = 4
HC = 32
NCH = T // HC
ST = 16
GH = 8
PH = 8
NK = 128
TOPK = 16
E = NK * NK
EPS = 1e-6
HGRN_SCALE = 128 ** -0.5
GDN_SCALE = 128 ** -0.5
TWO_PI_HI = 6.28125
TWO_PI_LO = 6.283185307179586 - 6.28125
ROUND = 12582912.0
LOWEST = -3.0e38
NU = 8
NV = 8
ROUTE_LINKS = 21
HEADS = PH * TT

STREAMS = {"ev_in": (0, 20), "ev_out": (20, 8), "wq0": (28, 16),
           "od_in": (44, 32), "od_out": (76, 8), "wq1": (84, 16)}
EARLY = 12
NSLOT = 4

SMALL = [("norm_w", 5 * DC), ("s5_are", ST), ("s5_aim", ST), ("s5_ldt", ST), ("s5_d", 4),
         ("lb", 8), ("gn", 2), ("conv", 96), ("ab", 2), ("ba_w", DC * 16), ("keys", 4 * NK)]
SMALL_AT = {}
_at = 0
for _n, _w in SMALL:
    SMALL_AT[_n] = (_at, _w)
    _at += _w
NSMALL = _at

ARENA = 40064


class Chain:

    def __init__(self, eng, sem):
        self.eng, self.sem, self.base, self.k = eng, sem, 0, 0

    def link(self, ins):
        self.k += 1
        ins.then_inc(self.sem, 1)
        self.eng.wait_ge(self.sem, self.base + self.k)


def trunk(nc, xT, wall, glu_w, s5_b, s5_c, small, u_tab, v_tab, out, stop_after=None, probe=None):
    ctx = ExitStack()
    with ctx:
        def sb(name, shape, dt=F32):
            return ctx.enter_context(nc.sbuf_tensor(name, shape, dt))

        def sem(name):
            return ctx.enter_context(nc.semaphore(name))

        h = sb("h", [P, DC, T])
        wring = sb("wring", [P, NSLOT, DC, P])
        scr = sb("scr", [P, 4, T])
        consts = sb("consts", [P, NSMALL])
        ident = sb("ident", [P, P])
        mean_d = sb("mean_d", [P, P])
        mean_h = sb("mean_h", [P, P])
        ones = sb("ones", [P, P])
        maskc = sb("maskc", [P, P])
        mask32 = sb("mask32", [P, P])
        iota16 = sb("iota16", [P, TOPK])
        cols = sb("cols", [P, 640])
        rt = sb("rt", [P, T])
        arena = sb("arena", [P, ARENA])
        ps = [ctx.enter_context(nc.psum_tensor(f"ps{i}", [P, T], F32)) for i in range(8)]

        def region(at, *shape):
            n = 1
            for x in shape:
                n *= x
            assert at + n <= ARENA, (at, n)
            v = arena[:, at:at + n]
            if len(shape) == 2:
                return v.rearrange("p (a b) -> p a b", a=shape[0])
            if len(shape) == 3:
                return v.rearrange("p (a b c) -> p a b c", a=shape[0], b=shape[1])
            return v

        def small_in(name):
            a, w = SMALL_AT[name]
            return consts[:, a:a + w]

        norm_w = small_in("norm_w").rearrange("p (n k) -> p n k", k=DC)
        conv_w = small_in("conv").rearrange("p (c j) -> p c j", j=4)
        ba_w = small_in("ba_w").rearrange("p (k m) -> p k m", m=16)
        keys = small_in("keys").rearrange("p (l c k) -> p l c k", l=2, c=2)
        gn_col = small_in("gn")
        eps_col = cols[:, 0:1]

        maskl = region(32768, 2, 7, P)

        hn = region(0, DC, T)
        proj = region(4096, 20, T)
        uT, qT, fT, vT0, gT = (proj[:, 4 * i:4 * i + 4, :] for i in range(5))
        tab_c = region(14336, ST, T)
        tab_s = region(22528, ST, T)
        bw = region(30720, 2, 4, P)
        cw = region(31744, 2, ST, 32)
        s5w = [[region(32768 + T * i, T) for i in range(6)], [region(35840 + T * i, T) for i in range(6)],
               [scr[:, 0, :], scr[:, 1, :], scr[:, 2, :], scr[:, 3, :], rt[:, :], region(38912, T)]]
        tab_t = region(32768, 2, 2048)
        kA = region(14336, HG, T)
        eC = region(16384, HG, T)
        kE = region(18432, HG, T)
        kD = region(20480, HG, T)
        kTok = region(22528, HG, TT, P)
        vTok = region(24576, HG, TT, P)
        states = region(26624, NCH, P)
        glu_sb = region(36864, 4, T)
        totH = cols[:, 64:128].rearrange("p (h c) -> p h c", h=HG)
        mix0 = [qT[:, j, :] for j in range(4)] + [uT[:, j, :] for j in range(4)]
        statesA = [region(26624, NCH, P), region(28672, NCH, P), region(32768, NCH, P), region(34816, NCH, P)]

        raw = region(4096, 24, T)
        zT = region(16384, GH, T)
        conv = region(20480, 24, T)
        beta_r = region(34560, T)[0:GH]
        dec_r = region(35072, T)[0:GH]
        soft_r = [region(37632 + T * i, T)[0:GH] for i in range(4)]
        dec_c = cols[:, 64:96].rearrange("p (t h) -> p t h", h=GH)
        beta_c = cols[:, 96:128].rearrange("p (t h) -> p t h", h=GH)
        last_c = cols[:, 128:160].rearrange("p (h t) -> p h t", t=TT)
        kbe_c = cols[:, 160:192].rearrange("p (t h) -> p t h", h=GH)
        tail_c = cols[:, 192:224].rearrange("p (t h) -> p t h", h=GH)
        tot_c = cols[:, 224:256].rearrange("p (h t) -> p h t", t=TT)
        kbT = region(0, 4, T)
        qdT = region(2048, 4, T)
        vb = region(4096, 4, TT, P)
        kbe = region(6144, 4, TT, P)
        ktail = region(8192, 4, TT, P)
        invT = region(10240, 4, T)
        inv = region(12288, 4, T)
        negA = region(14336, 4, T)
        lmT = region(35584, 4, T)
        xs = region(37632, 4, T)
        gstate = region(37632, 4, P)
        vnew = region(38144, 4, P)
        mcur = region(39680, 2, P)
        mix1 = [zT[:, j, :] for j in range(GH)]

        sc = region(0, HEADS + 1, 2 * NK)
        xtok = region(8448, TT, D)
        xcur = region(12544, D)
        ycur = region(13568, D)
        uring = region(14592, NU, D)
        vring = region(22784, NV, D)
        sct = region(39168, 2, 2, NK)
        phn = region(30976, DC, T)
        pq = region(35072, 2, 2, T)
        cand = rt[:, 0:TOPK * TOPK]
        hot = rt[:, TOPK * TOPK:2 * TOPK * TOPK].rearrange("p (a b) -> p a b", a=TOPK)
        diag = scr[:, :, :].rearrange("p a (b c) -> p (a b) c", c=P)

        def rcol(i, n, dt=F32):
            return cols[:, i:i + n].bitcast(dt) if dt is not F32 else cols[:, i:i + n]

        top_v = rcol(64, 32).rearrange("p (c k) -> p c k", c=2)
        top_i = rcol(96, 32, U32).rearrange("p (c k) -> p c k", c=2)
        top_f = rcol(128, 32).rearrange("p (c k) -> p c k", c=2)
        sel_v, sel_p = rcol(160, TOPK), rcol(176, TOPK, U32)
        sel_a, sel_b = rcol(192, TOPK, U32), rcol(208, TOPK, U32)
        pos_a, pos_b = rcol(224, TOPK), rcol(240, TOPK)
        exp_a, exp_b = rcol(256, TOPK), rcol(272, TOPK)
        soft_e, soft_m, soft_s = rcol(288, TOPK), rcol(304, 1), rcol(305, 1)
        ids = [rcol(320 + 16 * i, TOPK, U32) for i in range(2)]
        gate = [rcol(352 + 16 * i, TOPK) for i in range(2)]
        dots = [rcol(384 + 16 * i, TOPK) for i in range(2)]
        gelu = [rcol(416 + 16 * i, TOPK) for i in range(2)]
        wgt = [rcol(448 + 16 * i, TOPK) for i in range(2)]

        s = {n: sem(n) for n in (
            "lm_iota", "lm_built", "conv_done", "silu", "l2_sq", "l2_sum", "l2_root", "l2_done",
            "ba_mm", "a_raw", "a_abs", "a_exp", "a_one", "a_ln", "beta_ready", "dec_ready", "col_tr", "cols_ready",
            "bc_mm", "last_ready", "kb_ready", "lm_min", "gq_exp", "lm_exp", "small_exp", "scale_cols", "qd_ready",
            "kk_mm", "negA_ready", "ktr_mm", "kbe_ready", "ktail_ready", "vtr_mm", "vb_ready",
            "wt_done", "x_mm", "xs_copied", "y_mm", "kc_mm", "kc_ready", "qk_mm", "att_raw", "att_ready",
            "vn_mm", "vn_ready", "gds_mm", "gs_ready", "go_done", "g_sq", "g_sum", "g_root",
            "xt_tr", "xt_copied", "sc_mm", "sc_ready", "sct_ready", "soft_in", "soft_exp", "ids_ready",
            "u_free", "v_free", "gelu_ready", "w_ready", "diag_ready", "y_copied", "hy_ready", "peer_done",
            "x_loaded", "small_loaded", "bc_loaded", "glu_loaded", "out_stored",
            "const_pool", "masks_built",
            "sq_ready", "sum_ready", "root_ready", "rt_ready", "hn_ready",
            "acc_ready", "acc_free",
            "dve_own", "act_own", "pool_own", "dve_passed", "act_passed", "pool_passed",
            "s5_theta", "s5_trig", "s5_trig_exp", "s5_wc", "tab_dve", "tab_pool", "s5_ctab", "s5_bu", "s5_bcopy",
            "s5_wr", "s5_wi", "s5_scan", "s5_pr", "s5_pi", "s5_y", "s5_ysum", "s5_gelu", "s5_glu", "s5_sig",
            "lb_e", "lb_d", "hg_f", "hg_ln", "hg_k", "hg_cum", "hg_dif", "hg_exp", "hg_ke", "hg_kd",
            "hg_att", "hg_attm", "hg_tr", "hg_trc", "hg_ds", "hg_st", "hg_o", "hg_sq", "hg_sum", "hg_root",
            "mix_ready")}
        u_arrived = [sem(f"u_arrived{i}") for i in range(NU)]
        v_arrived = [sem(f"v_arrived{i}") for i in range(NV)]
        w_arrived = [sem(f"w_arrived{i}") for i in range(NSLOT)]

        block = ctx.enter_context(nc.Block())

        def probe_sp(sp):
            sp.wait_ge(s["mix_ready"], 8)
            for j in range(8):
                sp.dma_start(out[:, j, :], mix0[j]).then_inc(s["out_stored"], 16)
            sp.wait_ge(s["out_stored"], 16 * 8)

        def s5t(i, w):
            return tab_t[:, i, 0:ST * w].rearrange("p (a b) -> p a b", a=ST)

        @block.sync
        def _(sp):
            sp.dma_start(h[:, :, :], xT).then_inc(s["x_loaded"], 16)
            sp.dma_start(consts[:, :], small).then_inc(s["small_loaded"], 16)
            sp.dma_start(bw, s5_b).then_inc(s["bc_loaded"], 16)
            sp.dma_start(cw, s5_c).then_inc(s["bc_loaded"], 16)

            def load_stream(name, first=False):
                c0, n = STREAMS[name]
                start = 0
                if first:
                    for j in range(NSLOT):
                        sp.dma_start(wring[:, j, :, :], wall[c0 + j]).then_inc(w_arrived[j], 16)
                    start = NSLOT
                with sp.Fori(start // NSLOT, n // NSLOT) as i:
                    for j in range(NSLOT):
                        sp.wait_ge(s["acc_ready"], i * NSLOT + (c0 + j - NSLOT + 1))
                        sp.dma_start(wring[:, j, :, :],
                                     wall[bass.ds(i * NSLOT + (c0 + j), 1)].rearrange("a p k n -> (a p) k n")
                                     ).then_inc(w_arrived[j], 16)

            load_stream("ev_in", first=True)
            sp.wait_ge(s["s5_y"], ST)
            sp.dma_start(glu_sb, glu_w).then_inc(s["glu_loaded"], 16)
            if stop_after == "mix0":
                return probe_sp(sp)
            load_stream("ev_out")
            load_stream("wq0")
            if stop_after == "h1":
                sp.wait_ge(s["peer_done"], TT)
                sp.dma_start(out, h[:, :, :]).then_inc(s["out_stored"], 16)
                sp.wait_ge(s["out_stored"], 16)
                return
            load_stream("od_in")
            if stop_after == "mix1":
                for j in range(8):
                    sp.wait_ge(s["mix_ready"], 9 + j)
                    sp.dma_start(out[:, j, :], mix1[j]).then_inc(s["out_stored"], 16)
                sp.wait_ge(s["out_stored"], 16 * 8)
                return
            load_stream("od_out")
            load_stream("wq1")
            for k in range(DC):
                sp.wait_ge(s["hn_ready"], 4 * DC + k + 1)
                sp.dma_start(out[:, k, :], hn[:, k, :]).then_inc(s["out_stored"], 16)
            sp.wait_ge(s["out_stored"], 16 * DC)

        @block.gpsimd
        def _(pool):
            own = Chain(pool, s["pool_own"])
            pool.memset(ident[:, :], 0.0)
            pool.memset(mean_d[:, :], 1.0 / D)
            pool.memset(mean_h[:, :], 1.0 / P)
            pool.memset(maskc[:, :], 1.0)
            own.link(pool.memset(ones[:, :], 1.0))
            pool.affine_select(out=ident[:, :], in_=ident[:, :], compare_op=ALU.not_equal, fill=1.0, base=0,
                               pattern=[[-1, P]], channel_multiplier=1)
            pool.affine_select(out=maskc[:, :], in_=maskc[:, :], compare_op=ALU.is_ge, fill=0.0, base=0,
                               pattern=[[1, P]], channel_multiplier=-1)
            pool.iota(iota16[:, :], [[1, TOPK]], base=0, channel_multiplier=0,
                      allow_small_or_imprecise_dtypes=True)
            row = scr[:, 0, 0:P].bitcast(I32)
            col = scr[:, 0, P:2 * P].bitcast(I32)
            pool.iota(row, [[0, P]], base=0, channel_multiplier=1)
            pool.iota(scr[:, 1, :].bitcast(I32), [[1, T]], base=0, channel_multiplier=0)
            pool.iota(col, [[1, P]], base=0, channel_multiplier=0).then_inc(s["const_pool"], 1)

            for m in range(9):
                w = 1 << m
                pool.wait_ge(s["s5_ctab"], m + 1)
                if m:
                    pool.wait_ge(s["tab_dve"], m)
                step = min(w, 128)
                for a in range(0, w, step):
                    tmp = s5t(1, step)
                    cmb = cols[:, 128 + 32 * m:144 + 32 * m].unsqueeze(2).to_broadcast([P, ST, step])
                    smb = cols[:, 144 + 32 * m:160 + 32 * m].unsqueeze(2).to_broadcast([P, ST, step])
                    pool.tensor_tensor(tab_s[:, :, w + a:w + a + step], tab_s[:, :, a:a + step], cmb, ALU.mult)
                    own.link(pool.tensor_tensor(tmp, tab_c[:, :, a:a + step], smb, ALU.mult))
                    last = pool.tensor_tensor(tab_s[:, :, w + a:w + a + step], tab_s[:, :, w + a:w + a + step], tmp,
                                              ALU.add)
                    if a + step < w:
                        own.link(last)
                last.then_inc(s["tab_pool"], 1)
                pool.wait_ge(s["tab_pool"], m + 1)

            def s5_wi(st):
                W = s5w[st % 3]
                pool.wait_ge(s["s5_bcopy"], 2 * st + 2)
                if st == 0:
                    pool.wait_ge(s["tab_dve"], 9)
                if st >= 3:
                    pool.wait_ge(s["s5_y"], st - 2)
                pool.tensor_tensor(W[5], W[1], tab_c[:, st, :], ALU.mult)
                own.link(pool.tensor_tensor(W[3], W[0], tab_s[:, st, :], ALU.mult))
                pool.tensor_tensor(W[3], W[5], W[3], ALU.subtract).then_inc(s["s5_wi"], 1)

            s5_wi(0)
            for st in range(ST):
                if st + 1 < ST:
                    s5_wi(st + 1)
                W = s5w[st % 3]
                pool.wait_ge(s["s5_scan"], 2 * st + 2)
                pool.tensor_tensor(W[1], W[2], tab_s[:, st, :], ALU.mult)
                pool.tensor_tensor(W[5], W[3], tab_c[:, st, :], ALU.mult).then_inc(s["s5_pi"], 1)

            pool.wait_ge(s["hg_f"], 4)
            pool.wait_ge(s["s5_y"], ST)
            pool.tensor_scalar(kA, fT, -1.0, 1.0, ALU.mult, ALU.add).then_inc(s["hg_k"], 1)
            pool.wait_ge(s["hg_exp"], 3)
            pool.tensor_tensor(kD, kA, kD, ALU.mult).then_inc(s["hg_kd"], 1)

            def peer(layer):
                def head(g, par):
                    pool.wait_ge(s["ids_ready"], g + ((HEADS + 1) * layer + 1))
                    for ring, tab, n, free, extra, arrived in ((uring, u_tab, NU, "u_free", 0, u_arrived),
                                                               (vring, v_tab, NV, "v_free", TOPK - NV, v_arrived)):
                        for k in range(TOPK):
                            pool.wait_ge(s[free], g * TOPK + (TOPK * HEADS * layer + extra + k + 1))
                            pool.sem_inc(s["pool_passed"], 1)
                            pool.indirect_dma_start(
                                out=ring[:, k % n, :], out_offset=None, in_=tab,
                                in_offset=bass.IndirectOffsetOnAxis(ap=ids[par][:, k:k + 1], axis=0)
                            ).then_inc(arrived[k % n], 16)

                with pool.Fori(0, HEADS // 2) as p:
                    for par in range(2):
                        head(p * 2 + par, par)

            if stop_after == "mix0":
                return
            peer(0)
            if stop_after == "h1":
                return

            pool.wait_ge(s["peer_done"], TT)
            row = lmT[:, 0, 0:P].bitcast(I32)
            col = lmT[:, 0, P:2 * P].bitcast(I32)
            pool.iota(row, [[0, P]], base=0, channel_multiplier=1)
            pool.iota(col, [[1, P]], base=0, channel_multiplier=0).then_inc(s["lm_iota"], 1)

            for grp in range(2):
                for hh in range(4):
                    pool.wait_ge(s["att_raw"], 4 * grp + hh + 1)
                    pool.tensor_tensor(negA[:, hh, :].rearrange("p (t x) -> p t x", t=TT),
                                       negA[:, hh, :].rearrange("p (t x) -> p t x", t=TT),
                                       maskc[:, :].unsqueeze(1).to_broadcast([P, TT, P]),
                                       ALU.mult).then_inc(s["att_ready"], 1)
            if stop_after == "mix1":
                return
            peer(1)

        @block.tensor
        def _(pe):
            def norm_sum(n):
                for k in range(DC):
                    pe.wait_ge(s["sq_ready"], DC * n + k + 1)
                    mm = pe.matmul(ps[2][:, :], mean_d[:, :], scr[:, k % 4, :], start=(k == 0), stop=(k == DC - 1))
                    mm.then_inc(s["sum_ready"], 1)

            def stream(name, rhs, upto=None):
                c0, n = STREAMS[name]
                n = upto or n
                with pe.Fori(0, n // NSLOT) as i:
                    for j in range(NSLOT):
                        chunk(c0, i * NSLOT + j, j, rhs)

            def chunk(c0, c, j, rhs):
                pe.wait_ge(w_arrived[j], (c - j) * 4 + (4 * c0 + 16))
                pe.wait_ge(s["acc_free"], c + (c0 + 1))
                for k in range(DC):
                    mm = pe.matmul(ps[j % 2][:, :], wring[:, j, k, :], rhs(k), start=(k == 0), stop=(k == DC - 1))
                mm.then_inc(s["acc_ready"], 1)

            pe.wait_ge(s["const_pool"], 1)
            norm_sum(0)
            pe.wait_ge(s["hn_ready"], DC)

            def s5_in(st):
                q, jj = st // 4, st % 4
                if st >= 2:
                    pe.wait_ge(s["s5_bcopy"], 2 * (st - 2) + 2)
                for i in range(2):
                    mm = pe.matmul(ps[3 + 2 * (st % 2) + i][:, :], bw[32 * jj:32 * jj + 32, i, q, :],
                                   uT[32 * jj:32 * jj + 32, q, :], start=True, stop=True)
                mm.then_inc(s["s5_bu"], 1)

            def s5_out(st):
                q, jj = st // 4, st % 4
                W = s5w[st % 3]
                pe.wait_ge(s["s5_pr"], st + 1)
                pe.wait_ge(s["s5_pi"], st + 1)
                if jj == 0 and q:
                    pe.wait_ge(s["s5_ysum"], q)
                o = ps[7][32 * jj:32 * jj + 32, :]
                for n, (w, x) in enumerate(((0, 0), (0, 4), (1, 1), (1, 5))):
                    mm = pe.matmul(o, cw[:, w, st, :], W[x], start=(n == 0), stop=(n == 3))
                mm.then_inc(s["s5_y"], 1)

            stream("ev_in", lambda k: hn[:, k, :], upto=EARLY)
            pe.wait_ge(s["bc_loaded"], 32)
            late = iter(range(EARLY, 20))
            s5_in(0)
            for st in range(ST + 1):
                if st + 1 < ST:
                    s5_in(st + 1)
                c = next(late, None)
                if c is not None:
                    chunk(0, c, c % 4, lambda k: hn[:, k, :])
                if st:
                    s5_out(st - 1)

            pe.wait_ge(s["s5_gelu"], 1)
            pe.wait_ge(s["glu_loaded"], 16)
            for n in range(4):
                for k in range(4):
                    mm = pe.matmul(ps[3 + n][:, :], glu_sb[:, k, P * n:P * n + P], uT[:, k, :],
                                   start=(k == 0), stop=(k == 3))
                mm.then_inc(s["s5_glu"], 1)

            BA = (0, 1, 2, 7)
            pe.wait_ge(s["hg_ke"], 2)
            for hd in range(HG):
                for t in range(TT):
                    c = slice(P * t, P * t + P)
                    mm = pe.matmul(ps[BA[hd]][:, c], kE[:, hd, c], qT[:, hd, c], start=(t == 0), stop=(t == TT - 1),
                                   skip_group_check=True)
                mm.then_inc(s["hg_att"], 1)
            pe.wait_ge(s["s5_sig"], 4)
            pe.wait_ge(s["hg_kd"], 1)
            for i in range(8):
                hd = i % 4
                src = kD if i < 4 else vT0
                if i >= 4:
                    pe.wait_ge(s["hg_trc"], i - 3)
                for t in range(TT):
                    c = slice(P * t, P * t + P)
                    mm = pe.transpose(ps[3 + hd][:, c], src[:, hd, c], ident[:, :])
                mm.then_inc(s["hg_tr"], 1)
            pe.wait_ge(s["hg_trc"], 8)
            pe.wait_ge(s["hg_attm"], 4)
            for t in range(TT):
                if t >= 2:
                    pe.wait_ge(s["hg_st"], 16 * (t - 1))
                for j in range(4):
                    bank = (BA if t % 2 else (3, 4, 5, 6))[j]
                    for hd in range(HG):
                        r = slice(HC * j, HC * j + HC)
                        mm = pe.matmul(ps[bank][:, P * hd:P * hd + P], kTok[r, hd, t, :], vTok[r, hd, t, :],
                                       start=True, stop=True, skip_group_check=True)
                mm.then_inc(s["hg_ds"], 1)
            for hd in range(HG):
                pe.wait_ge(s["hg_st"], 60)
                for t in range(TT):
                    c = slice(P * t, P * t + P)
                    pe.matmul(ps[BA[hd]][:, c], vTok[:, hd, t, :], eC[:, hd, c], start=(t == 0), stop=False,
                              skip_group_check=True)
                for n in range(1, NCH):
                    c = slice(HC * n, HC * n + HC)
                    mm = pe.matmul(ps[BA[hd]][:, c], statesA[hd][:, n, :], qT[:, hd, c], start=False,
                                   stop=(n == NCH - 1), skip_group_check=True)
                mm.then_inc(s["hg_o"], 1)
            for hd in range(HG):
                pe.wait_ge(s["hg_sq"], hd + 1)
                pe.matmul(ps[3 + hd][:, :], mean_h[:, :], scr[:, hd, :], start=True, stop=True).then_inc(s["hg_sum"], 1)

            def peer(layer):
                norm_sum(2 * layer + 1)
                pe.wait_ge(s["hn_ready"], DC * (2 * layer + 2))
                c0 = STREAMS[f"wq{layer}"][0]

                def queries(g, par):
                    for c in range(2):
                        chunk(c0, g * 2 + c, 2 * par + c, lambda k: phn[:, k, :])
                    pe.wait_ge(s["acc_free"], g * 2 + (c0 + 2 + 2))
                    for b in range(2):
                        if layer or not (isinstance(g, int) and g == 0):
                            pe.wait_ge(s["sc_ready"], g * 2 + (2 * PH * layer + b - 1))
                        for k in range(4):
                            t = 2 * b + k // 2
                            mm = pe.matmul(ps[2 + b][:, P * k:P * k + P], pq[:, par, k % 2, P * t:P * t + P],
                                           keys[:, layer, k % 2, :], start=(k == 0), stop=(k == 3),
                                           skip_group_check=True)
                        mm.then_inc(s["sc_mm"], 1)

                queries(0, 0)
                for n in range(2 * TT):
                    t, half = n // 2, n % 2
                    if n >= 2 or layer:
                        pe.wait_ge(s["xt_copied"], 2 * TT * layer + n - 1)
                    for k in range(4):
                        mm = pe.transpose(ps[6 + n % 2][:, P * k:P * k + P], phn[:, 4 * half + k, P * t:P * t + P],
                                          ident[:, :])
                    mm.then_inc(s["xt_tr"], 1)
                pe.wait_ge(s["xt_copied"], 2 * TT * (layer + 1))

                def head(g, first):
                    for k in range(TOPK):
                        pe.wait_ge(s["diag_ready"], g * TOPK + (TOPK * HEADS * layer + k + 1))
                        pe.wait_ge(v_arrived[k % NV], (g * (TOPK // NV) + (HEADS * layer * (TOPK // NV) + k // NV + 1)) * 16)
                        for i in range(2):
                            mm = pe.matmul(ps[4 + i][:, :], diag[:, k, :], vring[:, k % NV, T * i:T * i + T],
                                           start=(first and k == 0), stop=False, skip_group_check=True)
                        mm.then_inc(s["v_free"], 1)

                def finish(t):
                    pe.wait_ge(s["y_copied"], t + (TT * layer + 1))
                    for k in range(DC):
                        o = ps[6 + k // 4][:, P * (k % 4):P * (k % 4) + P]
                        pe.matmul(o, ycur[:, P * k:P * k + P], ident[:, :], start=(k % 4 == 0), stop=False,
                                  skip_group_check=True)
                        mm = pe.matmul(o, ident[:, :], h[:, k, bass.ds(t * P, P)], start=False, stop=(k % 4 == 3),
                                       skip_group_check=True)
                    mm.then_inc(s["hy_ready"], 1)
                    pe.wait_ge(s["peer_done"], t + (TT * layer + 1))

                def pair(p):
                    for par in range(2):
                        g = p * 2 + par
                        if not (isinstance(g, int) and g == PH - 1):
                            queries(g + 1, 1 - par)
                        head(g, isinstance(g, int) and g == 0)

                pair(0)
                with pe.Fori(1, PH // 2 - 1) as p:
                    pair(p)
                pair(PH // 2 - 1)
                finish(0)
                with pe.Fori(1, TT) as t:
                    head(t * PH, True)
                    with pe.Fori(1, PH) as g:
                        head(t * PH + g, False)
                    finish(t)

            if stop_after == "mix0":
                return
            pe.wait_ge(s["mix_ready"], DC)
            stream("ev_out", lambda k: mix0[k])
            peer(0)
            if stop_after == "h1":
                return

            norm_sum(2)
            pe.wait_ge(s["hn_ready"], 3 * DC)
            for i, bank in enumerate((7, 2)):
                for k in range(DC):
                    mm = pe.matmul(ps[bank][0:GH, :], ba_w[:, k, GH * i:GH * i + GH], hn[:, k, :], start=(k == 0),
                                   stop=(k == DC - 1))
                mm.then_inc(s["ba_mm"], 1)
            c0, n = STREAMS["od_in"]

            def od_group(i, g):
                for j in range(NSLOT):
                    chunk(c0, i * NSLOT + j, j, lambda k: hn[:, k, :])
                    if g is not None and j == 1:
                        pe.wait_ge(s["l2_sq"], g + 1)
                        for e in range(4):
                            mm = pe.matmul(ps[3 + e][:, :], ones[:, :], scr[:, e, :], start=True, stop=True)
                        mm.then_inc(s["l2_sum"], 1)

            od_group(0, None)
            od_group(1, None)
            pe.wait_ge(s["beta_ready"], 1)
            pe.wait_ge(s["dec_ready"], 1)
            for i, r in enumerate((dec_r, beta_r)):
                for t in range(TT):
                    mm = pe.transpose(ps[7][:, 32 * i + GH * t:32 * i + GH * t + GH], r[:, P * t:P * t + P],
                                      ident[0:GH, 0:GH])
            mm.then_inc(s["col_tr"], 1)
            with pe.Fori(0, 4) as g:
                od_group(g + 2, g)
            with pe.Fori(6, 8) as i:
                od_group(i, None)
            pe.wait_ge(s["acc_free"], c0 + n + 2)

            def tile(t):
                return slice(P * t, P * t + P)

            for grp in range(2):
                hs = range(4 * grp, 4 * grp + 4)
                if grp:
                    pe.wait_ge(s["mix_ready"], 8 + 4 * grp)
                pe.wait_ge(s["cols_ready"], 1)
                pe.wait_ge(s["l2_done"], 5)
                for hh, hd in enumerate(hs):
                    pick = ident[0:GH, hd:hd + 1].to_broadcast([GH, P])
                    pe.matmul(ps[BA[hh]][:, :], pick, beta_r, start=True, stop=True)
                    pe.matmul(ps[3 + hh][:, :], pick, dec_r, start=True, stop=True).then_inc(s["bc_mm"], 1)
                for hh, hd in enumerate(hs):
                    pe.wait_ge(s["kb_ready"], 4 * grp + hh + 1)
                    for t in range(TT):
                        mm = pe.matmul(ps[BA[hh]][:, tile(t)], conv[:, GH + hd, tile(t)], kbT[:, hh, tile(t)],
                                       start=(t == 0), stop=(t == TT - 1), skip_group_check=True)
                    mm.then_inc(s["kk_mm"], 1)
                for hh, hd in enumerate(hs):
                    pe.wait_ge(s["lm_min"], 4 * grp + hh + 1)
                    pe.wait_ge(s["gq_exp"], 4 * grp + hh + 1)
                    for t in range(TT):
                        mm = pe.transpose(ps[3 + hh][:, tile(t)], conv[:, GH + hd, tile(t)], ident[:, :])
                    mm.then_inc(s["ktr_mm"], 1)
                pe.wait_ge(s["silu"], 2)
                for hh, hd in enumerate(hs):
                    pe.wait_ge(s["negA_ready"], 4 * grp + hh + 1)
                    for t in range(TT):
                        mm = pe.transpose(ps[BA[hh]][:, tile(t)], conv[:, 2 * GH + hd, tile(t)], ident[:, :])
                    mm.then_inc(s["vtr_mm"], 1)
                pe.wait_ge(s["vb_ready"], 4 * grp + 4)
                pe.wait_ge(s["kbe_ready"], 4 * grp + 4)
                pe.wait_ge(s["ktail_ready"], 4 * grp + 4)
                with pe.Fori(0, 7) as l:
                    for hh in range(4):
                        pe.wait_ge(s["wt_done"], l * 4 + (32 * grp + hh + 1))
                        for t in range(TT):
                            mm = pe.matmul(ps[BA[hh]][:, tile(t)], negA[:, hh, tile(t)], inv[:, hh, tile(t)],
                                           start=(t == 0), stop=(t == TT - 1), skip_group_check=True)
                        mm.then_inc(s["x_mm"], 1)
                    for hh in range(4):
                        pe.wait_ge(s["xs_copied"], l * 4 + (28 * grp + hh + 1))
                        if hh >= 2:
                            pe.wait_ge(s["wt_done"], l * 4 + (32 * grp + 4 + hh - 1))
                        for t in range(TT):
                            pe.matmul(ps[3 + hh % 2][:, tile(t)], invT[:, hh, tile(t)], xs[:, hh, tile(t)],
                                      start=(t == 0), stop=(t == TT - 1), skip_group_check=True)
                        for t in range(TT):
                            mm = pe.matmul(ps[5 + hh % 2][:, tile(t)], xs[:, hh, tile(t)], invT[:, hh, tile(t)],
                                           start=(t == 0), stop=(t == TT - 1), skip_group_check=True)
                        mm.then_inc(s["y_mm"], 1)
                pe.wait_ge(s["wt_done"], 32 * grp + 32)
                for hh in range(4):
                    for t in range(TT):
                        mm = pe.matmul(ps[BA[hh]][:, tile(t)], kbe[:, hh, t, :], invT[:, hh, tile(t)],
                                       start=(t == 0), stop=(t == TT - 1), skip_group_check=True)
                    mm.then_inc(s["kc_mm"], 1)
                for hh, hd in enumerate(hs):
                    for t in range(TT):
                        mm = pe.matmul(ps[3 + hh][:, tile(t)], conv[:, GH + hd, tile(t)], conv[:, hd, tile(t)],
                                       start=(t == 0), stop=(t == TT - 1), skip_group_check=True)
                    mm.then_inc(s["qk_mm"], 1)
                pe.wait_ge(s["kc_ready"], 4 * grp + 4)
                pe.wait_ge(s["att_ready"], 4 * grp + 4)
                for t in range(TT):
                    n = (grp * TT + t) * 4
                    for hh in range(4):
                        if t:
                            pe.wait_ge(s["gs_ready"], (grp * 3 + t - 1) * 4 + hh + 1)
                        mm = pe.matmul(ps[BA[hh]][:, 0:P], invT[:, hh, tile(t)], vb[:, hh, t, :], start=True,
                                       stop=(t == 0), skip_group_check=True)
                        if t:
                            mm = pe.matmul(ps[BA[hh]][:, 0:P], kbT[:, hh, tile(t)], gstate[:, hh, :], start=False,
                                           stop=True, skip_group_check=True)
                        mm.then_inc(s["vn_mm"], 1)
                    if t:
                        for hh in range(4):
                            pe.matmul(ps[3 + hh][:, tile(t)], gstate[:, hh, :], qdT[:, hh, tile(t)], start=False,
                                      stop=False, skip_group_check=True)
                    for hh in range(4):
                        pe.wait_ge(s["vn_ready"], n + hh + 1)
                        mm = pe.matmul(ps[3 + hh][:, tile(t)], vnew[:, hh, :], negA[:, hh, tile(t)], start=(t == 0),
                                       stop=(t == TT - 1), skip_group_check=True)
                        if t < TT - 1:
                            pe.matmul(ps[BA[hh]][:, P:2 * P], ktail[:, hh, t, :], vnew[:, hh, :], start=True,
                                      stop=True, skip_group_check=True).then_inc(s["gds_mm"], 1)
                        else:
                            mm.then_inc(s["go_done"], 1)
                for hh in range(4):
                    pe.wait_ge(s["g_sq"], 4 * grp + hh + 1)
                    pe.matmul(ps[BA[hh]][:, :], mean_h[:, :], scr[:, hh, :], start=True,
                              stop=True).then_inc(s["g_sum"], 1)
            if stop_after == "mix1":
                return
            pe.wait_ge(s["mix_ready"], 2 * DC)
            stream("od_out", lambda k: mix1[k])
            peer(1)
            norm_sum(4)

        @block.scalar
        def _(act):
            own = Chain(act, s["act_own"])

            def alone():
                act.sem_inc(s["act_passed"], 1)

            def norm_squares(n):
                for k in range(DC):
                    if n == 0 and k == 0:
                        act.wait_ge(s["x_loaded"], 16)
                        act.wait_ge(s["masks_built"], 1)
                    if n in (1, 3):
                        act.wait_ge(s["acc_free"], STREAMS["ev_out" if n == 1 else "od_out"][0] + 2 + k + 1)
                    if n in (2, 4) and k == 0:
                        act.wait_ge(s["peer_done"], TT * (n // 2))
                        act.wait_ge(s["ids_ready"], (HEADS + 1) * (n // 2))
                    if k >= 4:
                        act.wait_ge(s["sum_ready"], DC * n + k - 3)
                    act.activation(scr[:, k % 4, :], h[:, k, :], ACT.Square).then_inc(s["sq_ready"], 1)
                act.wait_ge(s["sum_ready"], DC * n + DC)
                own.link(act.activation(rt[:, :], ps[2][:, :], ACT.Ln, bias=eps_col))
                act.activation(rt[:, :], rt[:, :], ACT.Exp, scale=-0.5).then_inc(s["root_ready"], 1)

            norm_squares(0)
            act.wait_ge(s["small_loaded"], 16)
            act.activation(cols[:, 16:32], small_in("s5_ldt"), ACT.Exp).then_inc(s["s5_trig_exp"], 1)
            act.wait_ge(s["s5_theta"], 1)
            act.activation(cols[:, 32:48], cols[:, 32:48], ACT.Exp).then_inc(s["s5_trig_exp"], 1)
            act.wait_ge(s["lb_d"], 1)
            act.activation(cols[:, 4:12], cols[:, 4:12], ACT.Exp).then_inc(s["lb_e"], 1)
            act.wait_ge(s["s5_theta"], 2)
            act.activation(cols[:, 416:432], cols[:, 416:432], ACT.Sin)
            act.activation(cols[:, 432:448], cols[:, 432:448], ACT.Sin).then_inc(s["s5_trig"], 1)

            def evac(c0, c, dst, func):
                act.wait_ge(s["acc_ready"], c0 + c + 1)
                act.activation(dst, ps[c % 2][:, :], func).then_inc(s["acc_free"], 1)

            def s5_copy(st):
                act.wait_ge(s["s5_bu"], st + 1)
                if st >= 3:
                    act.wait_ge(s["s5_y"], st - 2)
                else:
                    act.wait_ge(s["s5_wc"], 1)
                    act.wait_ge(s["tab_pool"], 9)
                for i in range(2):
                    act.activation(s5w[st % 3][i], ps[3 + 2 * (st % 2) + i][:, :],
                                   ACT.Copy).then_inc(s["s5_bcopy"], 1)

            late = iter(range(EARLY, 20))
            for n in range(EARLY + ST):
                if n >= EARLY:
                    s5_copy(n - EARLY)
                c = n if n < EARLY else next(late, None)
                if c is None:
                    continue
                evac(0, c, proj[:, c, :], (ACT.Copy, ACT.Silu, ACT.Sigmoid, ACT.Copy, ACT.Silu)[c // 4])
            act.wait_ge(s["s5_ysum"], 4)
            act.activation(uT, uT, ACT.Gelu).then_inc(s["s5_gelu"], 1)
            act.wait_ge(s["hg_f"], 4)
            act.wait_ge(s["hg_k"], 1)
            act.activation(fT, fT, ACT.Ln).then_inc(s["hg_ln"], 1)
            act.wait_ge(s["hg_cum"], 1)
            act.activation(eC, fT, ACT.Exp).then_inc(s["hg_exp"], 1)
            act.activation(kE, fT, ACT.Exp, scale=-1.0).then_inc(s["hg_exp"], 1)
            act.wait_ge(s["hg_dif"], 1)
            act.activation(kD, kD, ACT.Exp).then_inc(s["hg_exp"], 1)
            act.activation(totH, fT.rearrange("p h (c l) -> p h c l", l=HC)[:, :, :, HC - 1],
                           ACT.Exp).then_inc(s["hg_exp"], 1)
            for n in range(4):
                act.wait_ge(s["s5_glu"], n + 1)
                act.activation(scr[:, n, :], ps[3 + n][:, :], ACT.Sigmoid).then_inc(s["s5_sig"], 1)
            for i in range(8):
                act.wait_ge(s["hg_tr"], i + 1)
                dst = (kTok if i < 4 else vTok)[:, i % 4]
                act.activation(dst, ps[3 + i % 4][:, :].rearrange("p (t d) -> p t d", t=TT),
                               ACT.Copy).then_inc(s["hg_trc"], 1)
            BA = (0, 1, 2, 7)
            act.wait_ge(s["mix_ready"], 4)
            for hd in range(HG):
                act.wait_ge(s["hg_o"], hd + 1)
                act.activation(scr[:, hd, :], ps[BA[hd]][:, :], ACT.Square).then_inc(s["hg_sq"], 1)
            for hd in range(HG):
                act.wait_ge(s["hg_sum"], hd + 1)
                own.link(act.activation(kE[:, hd, :], ps[3 + hd][:, :], ACT.Ln, bias=eps_col))
                act.activation(kE[:, hd, :], kE[:, hd, :], ACT.Exp, scale=-0.5).then_inc(s["hg_root"], 1)

            def peer(layer):
                norm_squares(2 * layer + 1)
                c0 = STREAMS[f"wq{layer}"][0]

                def queries(g, par):
                    for c in range(2):
                        act.wait_ge(s["acc_ready"], g * 2 + (c0 + c + 1))
                        act.activation(pq[:, par, c, :], ps[c][:, :], ACT.Copy).then_inc(s["acc_free"], 1)
                    for b in range(2):
                        act.wait_ge(s["sc_mm"], g * 2 + (2 * PH * layer + b + 1))
                        alone()
                        dst = sc[:, 0:HEADS, :].rearrange("p (t g) k -> p t g k", t=TT)[:, 2 * b:2 * b + 2, bass.ds(g, 1), :]
                        act.activation(dst.rearrange("p t g k -> p t (g k)"),
                                       ps[2 + b][:, :].rearrange("p (t k) -> p t k", t=2),
                                       ACT.Copy).then_inc(s["sc_ready"], 1)
                    act.wait_ge(s["sc_ready"], g * 2 + (2 * PH * layer + 2))

                queries(0, 0)
                own.link(act.activation(sc[:, HEADS, :], sc[:, 0, :], ACT.Copy))

                def stage(g, par):
                    if layer or not (isinstance(g, int) and g == 0):
                        act.wait_ge(s["ids_ready"], g + (HEADS + 1) * layer)
                    alone()
                    act.activation(sct[:, par, :, :].rearrange("p c k -> p (c k)"),
                                   sc[:, bass.ds(g, 1), :].rearrange("p a k -> p (a k)"),
                                   ACT.Copy).then_inc(s["sct_ready"], 1)

                def soft(g):
                    act.wait_ge(s["soft_in"], g + ((HEADS + 1) * layer + 1))
                    act.activation(soft_e, sel_v, ACT.Exp, bias=soft_m, accum_out=soft_s).then_inc(s["soft_exp"], 1)

                def head(g, par):
                    act.wait_ge(s["u_free"], g * TOPK + (TOPK * HEADS * layer + TOPK + NU))
                    act.activation(gelu[par], dots[par], ACT.Gelu).then_inc(s["gelu_ready"], 1)
                    act.wait_ge(s["w_ready"], g + (HEADS * layer + 1))
                    for k in range(TOPK):
                        act.wait_ge(s["v_free"], g * TOPK + (TOPK * HEADS * layer + k + 1))
                        act.activation(diag[:, k, :], ident[:, :], ACT.Copy,
                                       scale=wgt[par][:, k:k + 1]).then_inc(s["diag_ready"], 1)

                stage(0, 0)
                for n in range(2 * TT):
                    act.wait_ge(s["xt_tr"], 2 * TT * layer + n + 1)
                    act.activation(xtok[:, n // 2, T * (n % 2):T * (n % 2) + T], ps[6 + n % 2][:, :],
                                   ACT.Copy).then_inc(s["xt_copied"], 1)
                soft(0)

                def pair(g0, more):
                    for par in range(2):
                        g = g0 + par
                        if more and not (more == 1 and par == 1):
                            queries(g + 1, 1 - par)
                        stage(g + 1, 1 - par)
                        head(g, par)
                        soft(g + 1)

                def finish(t):
                    act.wait_ge(s["v_free"], t * (TOPK * PH) + (TOPK * HEADS * layer + TOPK * PH + TOPK))
                    for i in range(2):
                        m = act.activation(ycur[:, T * i:T * i + T], ps[4 + i][:, :], ACT.Copy)
                    m.then_inc(s["y_copied"], 1)
                    act.wait_ge(s["hy_ready"], t + (TT * layer + 1))
                    alone()
                    for i in range(2):
                        m = act.activation(h[:, 4 * i:4 * i + 4, bass.ds(t * P, P)],
                                           ps[6 + i][:, :].rearrange("p (k t) -> p k t", k=4), ACT.Copy)
                    m.then_inc(s["peer_done"], 1)

                with act.Fori(0, PH // 2 - 1) as p:
                    pair(p * 2, 2)
                pair(PH - 2, 1)
                finish(0)
                with act.Fori(1, TT) as t:
                    with act.Fori(0, PH // 2) as p:
                        pair(t * PH + p * 2, 0)
                    finish(t)

            if stop_after == "mix0":
                return
            peer(0)
            if stop_after == "h1":
                return

            norm_squares(2)
            c0 = STREAMS["od_in"][0]
            ab = small_in("ab")
            raw_z = region(4096, 32, T)

            def od_evac(i, j, func=ACT.Copy):
                act.wait_ge(s["acc_ready"], i * NSLOT + (c0 + j + 1))
                alone()
                act.activation(raw_z[:, bass.ds(i * NSLOT + j, 1), :].rearrange("p a t -> p (a t)"),
                               ps[j % 2][:, :], func).then_inc(s["acc_free"], 1)

            def od_silu(g):
                act.wait_ge(s["conv_done"], g + 1)
                alone()
                return act.activation(conv[:, bass.ds(g * 4, 4), :], conv[:, bass.ds(g * 4, 4), :], ACT.Silu)

            act.wait_ge(s["ba_mm"], 2)
            act.activation(beta_r, ps[7][0:GH, :], ACT.Sigmoid).then_inc(s["beta_ready"], 1)
            act.wait_ge(s["a_abs"], 1)
            act.activation(soft_r[1], soft_r[1], ACT.Exp, scale=-1.0)
            act.activation(cols[0:GH, 2:3], ab[0:GH, 0:1], ACT.Exp).then_inc(s["a_exp"], 1)
            od_evac(0, 0)
            act.wait_ge(s["a_one"], 1)
            act.activation(soft_r[1], soft_r[1], ACT.Ln).then_inc(s["a_ln"], 1)
            for j in range(1, NSLOT):
                od_evac(0, j)
            for j in range(NSLOT):
                od_evac(1, j)
            act.wait_ge(s["col_tr"], 1)
            act.activation(cols[:, 64:128], ps[7][:, 0:64], ACT.Copy).then_inc(s["cols_ready"], 1)
            start = own.base + own.k
            with act.Fori(0, 4) as g:
                own.base, own.k = g * 2 + start, 0
                od_evac(g + 2, 0)
                own.link(od_silu(g))
                act.wait_ge(s["l2_done"], g + 1)
                alone()
                act.activation(scr[:, :, :], conv[:, bass.ds(g * 4, 4), :], ACT.Square).then_inc(s["l2_sq"], 1)
                od_evac(g + 2, 1)
                od_evac(g + 2, 2)
                act.wait_ge(s["l2_sum"], g + 1)
                for e in range(4):
                    m = act.activation(scr[:, e, :], ps[3 + e][:, :], ACT.Ln, bias=eps_col)
                own.link(m)
                act.activation(scr[:, :, :], scr[:, :, :], ACT.Exp, scale=-0.5).then_inc(s["l2_root"], 1)
                od_evac(g + 2, 3)
            own.base, own.k = start + 8, 0
            with act.Fori(4, 6) as g:
                for j in range(NSLOT):
                    od_evac(g + 2, j, ACT.Silu)
                    if j == 1:
                        od_silu(g).then_inc(s["silu"], 1)
            BA = (0, 1, 2, 7)
            for grp in range(2):
                hs = range(4 * grp, 4 * grp + 4)
                for hh in range(4):
                    act.wait_ge(s["bc_mm"], 4 * grp + hh + 1)
                    act.activation(qdT[:, hh, :], ps[3 + hh][:, :], ACT.Exp).then_inc(s["gq_exp"], 1)
                for hh in range(4):
                    act.wait_ge(s["lm_min"], 4 * grp + hh + 1)
                    act.activation(lmT[:, hh, :], lmT[:, hh, :], ACT.Exp).then_inc(s["lm_exp"], 1)
                hsl = slice(4 * grp, 4 * grp + 4)
                act.wait_ge(s["last_ready"], grp + 1)
                act.activation(kbe_c[:, :, hsl], dec_c[:, :, hsl], ACT.Exp)
                act.activation(tail_c[:, :, hsl], tail_c[:, :, hsl], ACT.Exp)
                act.activation(tot_c[:, hsl, :], last_c[:, hsl, :], ACT.Exp).then_inc(s["small_exp"], 1)
                act.wait_ge(s["scale_cols"], grp + 1)
                for hh, hd in enumerate(hs):
                    act.wait_ge(s["ktr_mm"], 4 * grp + hh + 1)
                    for t in range(TT):
                        m = act.activation(kbe[:, hh, t, :], ps[3 + hh][:, P * t:P * t + P], ACT.Copy,
                                           scale=kbe_c[:, t, hd:hd + 1])
                    m.then_inc(s["kbe_ready"], 1)
                for hh, hd in enumerate(hs):
                    act.wait_ge(s["vtr_mm"], 4 * grp + hh + 1)
                    for t in range(TT):
                        m = act.activation(vb[:, hh, t, :], ps[BA[hh]][:, P * t:P * t + P], ACT.Copy,
                                           scale=beta_c[:, t, hd:hd + 1])
                    m.then_inc(s["vb_ready"], 1)
                with act.Fori(0, 7) as l:
                    for hh in range(4):
                        act.wait_ge(s["x_mm"], l * 4 + (28 * grp + hh + 1))
                        act.activation(xs[:, hh, :], ps[BA[hh]][:, :], ACT.Copy).then_inc(s["xs_copied"], 1)
                for hh in range(4):
                    act.wait_ge(s["kc_mm"], 4 * grp + hh + 1)
                    act.activation(kbT[:, hh, :], ps[BA[hh]][:, :], ACT.Copy, scale=-1.0).then_inc(s["kc_ready"], 1)
                for t in range(TT):
                    for hh in range(4):
                        act.wait_ge(s["vn_mm"], (grp * TT + t) * 4 + hh + 1)
                        act.activation(vnew[:, hh, :], ps[BA[hh]][:, 0:P], ACT.Copy).then_inc(s["vn_ready"], 1)
                for hh in range(4):
                    act.wait_ge(s["go_done"], 4 * grp + hh + 1)
                    act.activation(scr[:, hh, :], ps[3 + hh][:, :], ACT.Square).then_inc(s["g_sq"], 1)
                for hh in range(4):
                    act.wait_ge(s["g_sum"], 4 * grp + hh + 1)
                    own.link(act.activation(lmT[:, hh, :], ps[BA[hh]][:, :], ACT.Ln, bias=eps_col))
                    act.activation(lmT[:, hh, :], lmT[:, hh, :], ACT.Exp, scale=-0.5).then_inc(s["g_root"], 1)
            if stop_after == "mix1":
                return
            peer(1)
            norm_squares(4)

        @block.vector
        def _(dve):
            own = Chain(dve, s["dve_own"])
            link = own.link

            def alone():
                dve.sem_inc(s["dve_passed"], 1)

            tt, ts = dve.tensor_tensor, dve.tensor_scalar
            stt = dve.scalar_tensor_tensor

            dve.memset(eps_col, EPS).then_inc(s["acc_free"], 2)
            dve.wait_ge(s["const_pool"], 1)
            row = scr[:, 0, 0:P].bitcast(U32)
            col = scr[:, 0, P:2 * P].bitcast(U32)
            xr = scr[:, 0, 2 * P:3 * P].bitcast(U32)
            sh = scr[:, 0, 3 * P:4 * P].bitcast(U32)
            up = scr[:, 2, 0:P]
            dn = scr[:, 2, P:2 * P]
            tok = scr[:, 1, :].bitcast(U32)
            m32row = scr[:, 3, :]
            tt(xr, row, col, ALU.bitwise_xor)
            tt(up, row, col, ALU.is_lt)
            link(tt(dn, row, col, ALU.is_gt))
            link(ts(sh, xr, 5, None, ALU.logical_shift_right))
            link(ts(sh.bitcast(F32), sh, 0, None, ALU.is_equal))
            link(tt(mask32[:, :], sh.bitcast(F32), maskc[:, :], ALU.mult))
            dve.memset(rt[:, :], 0.0).then_inc(s["masks_built"], 1)
            dve.wait_ge(s["masks_built"], 1)

            def norm_apply(n, dst):
                dve.wait_ge(s["root_ready"], n + 1)
                for k in range(DC):
                    stt(dst[:, k, :], h[:, k, :], norm_w[:, n, k:k + 1], rt[:, :], ALU.mult,
                        ALU.mult).then_inc(s["hn_ready"], 1)

            dve.wait_ge(s["small_loaded"], 16)
            norm_apply(0, hn)
            lb = small_in("lb").rearrange("p (r c) -> p r c", r=2)
            le = cols[:, 4:12].rearrange("p (r c) -> p r c", r=2)
            lbm = cols[:, 544:548]
            lbv, oml = cols[:, 548:552], cols[:, 552:556]
            link(tt(lbm, lb[:, 0], lb[:, 1], ALU.max))
            tt(le[:, 0], lb[:, 0], lbm, ALU.subtract)
            link(tt(le[:, 1], lb[:, 1], lbm, ALU.subtract))
            dve.memset(cols[:, 1:2], 0.0).then_inc(s["lb_d"], 1)
            are, aim = small_in("s5_are"), small_in("s5_aim")
            dt_, mag, th = cols[:, 16:32], cols[:, 32:48], cols[:, 48:64]
            c1, s1 = cols[:, 128:144], cols[:, 144:160]
            sn_h, sn = cols[:, 416:432], cols[:, 432:448]
            t0, t1, t2, den = (cols[:, 448 + 16 * i:464 + 16 * i] for i in range(4))
            dve.wait_ge(s["s5_trig_exp"], 1)
            tt(mag, are, dt_, ALU.mult).then_inc(s["s5_theta"], 1)
            link(tt(th, aim, dt_, ALU.mult))
            link(ts(t0, th, 1.0 / 6.283185307179586, ROUND, ALU.mult, ALU.add))
            link(ts(t0, t0, -ROUND, None, ALU.add))
            link(stt(t1, t0, -TWO_PI_HI, th, ALU.mult, ALU.add))
            link(stt(t1, t0, -TWO_PI_LO, t1, ALU.mult, ALU.add))
            link(ts(t1, t1, -3.1415925, 3.1415925, ALU.max, ALU.min))
            ts(sn_h, t1, 0.5, None, ALU.mult)
            dve.tensor_copy(sn, t1).then_inc(s["s5_theta"], 1)
            dve.wait_ge(s["s5_trig"], 1)
            link(stt(t0, sn_h, -2.0, sn_h, ALU.mult, ALU.mult))
            dve.tensor_copy(s1, sn)
            link(ts(c1, t0, 1.0, None, ALU.add))
            for m in range(9):
                if m:
                    pc, psn = cols[:, 96 + 32 * m:112 + 32 * m], cols[:, 112 + 32 * m:128 + 32 * m]
                    nco, nsn = cols[:, 128 + 32 * m:144 + 32 * m], cols[:, 144 + 32 * m:160 + 32 * m]
                    tt(t0, pc, pc, ALU.mult)
                    tt(t1, psn, psn, ALU.mult)
                    link(stt(nsn, pc, 2.0, psn, ALU.mult, ALU.mult))
                    link(tt(nco, t0, t1, ALU.subtract))
                    tt(t0, nco, nco, ALU.mult)
                    link(tt(t1, nsn, nsn, ALU.mult))
                    link(tt(t0, t0, t1, ALU.add))
                    link(ts(t0, t0, -0.5, 1.5, ALU.mult, ALU.add))
                    tt(nco, nco, t0, ALU.mult)
                    link(tt(nsn, nsn, t0, ALU.mult))
            dve.memset(tab_c[:, :, 0:1], 1.0)
            link(dve.memset(tab_s[:, :, 0:1], 0.0))
            dve.memset(t2, 0.0).then_inc(s["s5_ctab"], 9)
            dve.wait_ge(s["s5_ctab"], 9)
            for m in range(9):
                w = 1 << m
                if m:
                    dve.wait_ge(s["tab_pool"], m)
                step = min(w, 128)
                cmb = cols[:, 128 + 32 * m:144 + 32 * m].unsqueeze(2).to_broadcast([P, ST, step])
                smb = cols[:, 144 + 32 * m:160 + 32 * m].unsqueeze(2).to_broadcast([P, ST, step])
                for a in range(0, w, step):
                    tmp = s5t(0, step)
                    tt(tab_c[:, :, w + a:w + a + step], tab_c[:, :, a:a + step], cmb, ALU.mult)
                    link(tt(tmp, tab_s[:, :, a:a + step], smb, ALU.mult))
                    last = tt(tab_c[:, :, w + a:w + a + step], tab_c[:, :, w + a:w + a + step], tmp, ALU.subtract)
                    if a + step < w:
                        link(last)
                last.then_inc(s["tab_dve"], 1)
                dve.wait_ge(s["tab_dve"], m + 1)
            dve.wait_ge(s["s5_trig_exp"], 2)
            cr, ci = cols[:, 512:528], cols[:, 528:544]
            tt(t0, mag, c1, ALU.mult)
            tt(t1, mag, s1, ALU.mult)
            tt(t2, are, are, ALU.mult)
            link(tt(den, aim, aim, ALU.mult))
            ts(t0, t0, -1.0, None, ALU.add)
            link(tt(den, den, t2, ALU.add))
            link(dve.reciprocal(den, den))
            tt(cr, t0, are, ALU.mult)
            link(tt(t2, t1, aim, ALU.mult))
            link(tt(cr, cr, t2, ALU.add))
            tt(cr, cr, den, ALU.mult)
            tt(ci, t1, are, ALU.mult)
            link(tt(t2, t0, aim, ALU.mult))
            link(tt(ci, ci, t2, ALU.subtract))
            link(tt(ci, ci, den, ALU.mult))
            dve.wait_ge(s["bc_loaded"], 32)
            dve.wait_ge(s["tab_pool"], 9)
            crb = cr.unsqueeze(2).to_broadcast([P, ST, 32])
            cib = ci.unsqueeze(2).to_broadcast([P, ST, 32])
            pr = [tab_t[:, 0, 512 * i:512 * i + 512].rearrange("p (a b) -> p a b", a=ST) for i in range(4)]
            tt(pr[0], cw[:, 0], crb, ALU.mult)
            tt(pr[1], cw[:, 1], cib, ALU.mult)
            tt(pr[2], cw[:, 0], cib, ALU.mult)
            link(tt(pr[3], cw[:, 1], crb, ALU.mult))
            tt(cw[:, 0], pr[0], pr[1], ALU.subtract)
            link(tt(cw[:, 1], pr[2], pr[3], ALU.add))
            link(ts(cw[:, 1], cw[:, 1], -1.0, None, ALU.mult))
            dve.memset(t0, 0.0).then_inc(s["s5_wc"], 1)

            dve.wait_ge(s["lb_e"], 1)
            link(tt(lbm, le[:, 0], le[:, 1], ALU.add))
            link(dve.reciprocal(lbm, lbm))
            link(tt(lbv, le[:, 0], lbm, ALU.mult))
            link(ts(oml, lbv, -1.0, 1.0, ALU.mult, ALU.add))
            dve.wait_ge(s["acc_free"], 12 + 2)
            for hd in range(HG):
                ts(fT[:, hd, :], fT[:, hd, :], oml[:, hd:hd + 1], lbv[:, hd:hd + 1], ALU.mult,
                   ALU.add).then_inc(s["hg_f"], 1)
            def s5_wr(st):
                W = s5w[st % 3]
                dve.wait_ge(s["s5_bcopy"], 2 * st + 2)
                if st >= 3:
                    dve.wait_ge(s["s5_y"], st - 2)
                tt(W[4], W[0], tab_c[:, st, :], ALU.mult)
                link(tt(W[2], W[1], tab_s[:, st, :], ALU.mult))
                tt(W[2], W[4], W[2], ALU.add).then_inc(s["s5_wr"], 1)

            def s5_sum(q):
                dve.wait_ge(s["s5_y"], 4 * q + 4)
                stt(uT[:, q, :], uT[:, q, :], small_in("s5_d")[:, q:q + 1], ps[7][:, :], ALU.mult,
                    ALU.add).then_inc(s["s5_ysum"], 1)

            s5_wr(0)
            for st in range(ST):
                W = s5w[st % 3]
                magb = mag[:, st:st + 1].to_broadcast([P, T])
                dve.wait_ge(s["s5_wr"], st + 1)
                dve.tensor_tensor_scan(W[2], magb, W[2], 0.0, ALU.mult, ALU.add).then_inc(s["s5_scan"], 1)
                dve.wait_ge(s["s5_wi"], st + 1)
                dve.tensor_tensor_scan(W[3], magb, W[3], 0.0, ALU.mult, ALU.add).then_inc(s["s5_scan"], 1)
                dve.wait_ge(s["s5_scan"], 2 * st + 2)
                tt(W[0], W[2], tab_c[:, st, :], ALU.mult)
                stt(W[4], W[3], -1.0, tab_s[:, st, :], ALU.mult, ALU.mult).then_inc(s["s5_pr"], 1)
                if st + 1 < ST:
                    s5_wr(st + 1)
                if st % 4 == 0 and st:
                    s5_sum(st // 4 - 1)
            s5_sum(3)
            m32 = rt[:, :]
            link(dve.memset(m32, 1.0))
            link(dve.memset(m32.rearrange("p (c l) -> p c l", l=HC)[:, :, 0:1], 0.0))
            dve.wait_ge(s["hg_ln"], 1)
            for hd in range(HG):
                link(dve.tensor_tensor_scan(fT[:, hd, :], m32, fT[:, hd, :], 0.0, ALU.mult, ALU.add))
            f4 = fT.rearrange("p h (c l) -> p (h c) l", l=HC)
            d4 = kD.rearrange("p h (c l) -> p (h c) l", l=HC)
            tt(d4, f4[:, :, HC - 1:HC].to_broadcast([P, HG * NCH, HC]), f4, ALU.subtract).then_inc(s["hg_dif"], 1)
            dve.memset(cols[:, 1:2], 0.0).then_inc(s["hg_cum"], 1)
            dve.wait_ge(s["hg_exp"], 1)
            stt(qT, qT, HGRN_SCALE, eC, ALU.mult, ALU.mult).then_inc(s["hg_ke"], 1)
            dve.wait_ge(s["hg_exp"], 2)
            dve.wait_ge(s["hg_k"], 1)
            tt(kE, kA, kE, ALU.mult).then_inc(s["hg_ke"], 1)
            dve.wait_ge(s["hg_ke"], 2)
            BA = (0, 1, 2, 7)
            for hd in range(HG):
                dve.wait_ge(s["hg_att"], hd + 1)
                tt(eC[:, hd, :].rearrange("p (t x) -> p t x", t=TT), ps[BA[hd]][:, :].rearrange("p (t x) -> p t x", t=TT),
                   mask32[:, :].unsqueeze(1).to_broadcast([P, TT, P]), ALU.mult).then_inc(s["hg_attm"], 1)
            dve.wait_ge(s["hg_exp"], 4)
            dve.wait_ge(s["s5_gelu"], 1)
            for n in range(4):
                dve.wait_ge(s["s5_sig"], n + 1)
                if n == 0:
                    dve.wait_ge(s["s5_glu"], 4)
                tt(uT[:, n, :], uT[:, n, :], scr[:, n, :], ALU.mult).then_inc(s["mix_ready"], 1)

            for n in range(NCH - 1):
                t, j = n // 4, n % 4
                dve.wait_ge(s["hg_ds"], t + 1)
                for hd in range(HG):
                    ds = ps[(BA if t % 2 else (3, 4, 5, 6))[j]][:, P * hd:P * hd + P]
                    if n == 0:
                        m = dve.tensor_copy(statesA[hd][:, 1, :], ds)
                    else:
                        m = stt(statesA[hd][:, n + 1, :], statesA[hd][:, n, :], totH[:, hd, n:n + 1], ds, ALU.mult,
                                ALU.add)
                    m.then_inc(s["hg_st"], 1)
                dve.wait_ge(s["hg_st"], 4 * n + 4)
            for hd in range(HG):
                dve.wait_ge(s["hg_root"], hd + 1)
                link(stt(kA[:, hd, :], ps[BA[hd]][:, :], gn_col[:, 0:1], kE[:, hd, :], ALU.mult, ALU.mult))
                tt(qT[:, hd, :], kA[:, hd, :], gT[:, hd, :], ALU.mult).then_inc(s["mix_ready"], 1)

            def add_stream(name):
                c0, n = STREAMS[name]
                with dve.Fori(0, n // NSLOT) as i:
                    for j in range(NSLOT):
                        dve.wait_ge(s["acc_ready"], i * NSLOT + (c0 + j + 1))
                        hc = h[:, bass.ds(i * NSLOT + j, 1), :].rearrange("p a t -> p (a t)")
                        tt(hc, hc, ps[j % 2][:, :], ALU.add).then_inc(s["acc_free"], 1)

            def peer(layer):
                norm_apply(2 * layer + 1, phn)

                def route(g, par):
                    dve.wait_ge(s["sct_ready"], g + ((HEADS + 1) * layer + 1))
                    alone()
                    for lo in (0, 8):
                        for c in range(2):
                            m = dve.max(top_v[:, c, lo:lo + 8], sct[:, par, c, :])
                        link(m)
                        alone()
                        for c in range(2):
                            m = dve.max_index(top_i[:, c, lo:lo + 8], top_v[:, c, lo:lo + 8], sct[:, par, c, :])
                        if lo == 0:
                            link(m)
                            alone()
                            for c in range(2):
                                m = dve.match_replace(sct[:, par, c, :], top_v[:, c, 0:8], sct[:, par, c, :], LOWEST)
                        link(m)
                        if lo == 0:
                            alone()
                    dve.tensor_copy(top_f, top_i)
                    link(tt(cand.rearrange("p (a b) -> p a b", a=TOPK),
                            top_v[:, 0, :].unsqueeze(2).to_broadcast([P, TOPK, TOPK]),
                            top_v[:, 1, :].unsqueeze(1).to_broadcast([P, TOPK, TOPK]), ALU.add))
                    alone()
                    link(dve.max(sel_v[:, 0:8], cand))
                    alone()
                    link(dve.max_index(sel_p[:, 0:8], sel_v[:, 0:8], cand))
                    ts(soft_m, sel_v[:, 0:1], -1.0, None, ALU.mult)
                    link(dve.match_replace(cand, sel_v[:, 0:8], cand, LOWEST))
                    alone()
                    dve.max(sel_v[:, 8:16], cand).then_inc(s["soft_in"], 1)
                    dve.wait_ge(s["soft_in"], g + ((HEADS + 1) * layer + 1))
                    alone()
                    link(dve.max_index(sel_p[:, 8:16], sel_v[:, 8:16], cand))
                    ts(sel_a, sel_p, 4, None, ALU.logical_shift_right)
                    link(ts(sel_b, sel_p, TOPK - 1, None, ALU.bitwise_and))
                    dve.tensor_copy(pos_a, sel_a)
                    link(dve.tensor_copy(pos_b, sel_b))
                    for pos, dst, c in ((pos_a, exp_a, 0), (pos_b, exp_b, 1)):
                        link(tt(hot, pos.unsqueeze(2).to_broadcast([P, TOPK, TOPK]),
                                iota16[:, :].unsqueeze(1).to_broadcast([P, TOPK, TOPK]), ALU.is_equal))
                        link(tt(hot, hot, top_f[:, c, :].unsqueeze(1).to_broadcast([P, TOPK, TOPK]), ALU.mult))
                        link(dve.tensor_reduce(dst, hot, AX.X, ALU.add))
                    link(stt(exp_a, exp_a, float(NK), exp_b, ALU.mult, ALU.add))
                    link(ts(ids[par], exp_a, float(layer * E), None, ALU.add))
                    dve.wait_ge(s["soft_exp"], g + ((HEADS + 1) * layer + 1))
                    link(dve.reciprocal(soft_s, soft_s))
                    ts(gate[par], soft_e, soft_s, None, ALU.mult).then_inc(s["ids_ready"], 1)

                def head(g, par):
                    for k in range(TOPK):
                        dve.wait_ge(u_arrived[k % NU],
                                    (g * (TOPK // NU) + (HEADS * layer * (TOPK // NU) + k // NU + 1)) * 16)
                        dve.tensor_tensor_reduce(uring[:, k % NU, :], uring[:, k % NU, :], xcur, 1.0, 0.0, ALU.mult,
                                                 ALU.add, dots[par][:, k:k + 1]).then_inc(s["u_free"], 1)
                    dve.wait_ge(s["gelu_ready"], g + (HEADS * layer + 1))
                    dve.wait_ge(s["ids_ready"], g + ((HEADS + 1) * layer + 1))
                    tt(wgt[par], gelu[par], gate[par], ALU.mult).then_inc(s["w_ready"], 1)

                route(0, 0)
                dve.wait_ge(s["xt_copied"], 2 * TT * (layer + 1))
                tile_links, pair_links = 1, 2 * ROUTE_LINKS
                per_tile = tile_links + (PH // 2) * pair_links
                start = own.base + own.k
                with dve.Fori(0, TT) as t:
                    own.base, own.k = t * per_tile + start, 0
                    link(dve.tensor_copy(xcur, xtok[:, bass.ds(t, 1), :].rearrange("p a d -> p (a d)")))
                    alone()
                    with dve.Fori(0, PH // 2) as p:
                        own.base, own.k = t * per_tile + p * pair_links + (start + tile_links), 0
                        for par in range(2):
                            g = t * PH + p * 2 + par
                            head(g, par)
                            route(g + 1, 1 - par)
                        assert own.k == pair_links, own.k
                own.base, own.k = start + TT * per_tile, 0

            if stop_after == "mix0":
                return
            dve.memset(cols[:, 1:2], 0.0).then_inc(s["u_free"], NU)
            dve.memset(cols[:, 2:3], 0.0).then_inc(s["v_free"], TOPK)
            add_stream("ev_out")
            peer(0)
            if stop_after == "h1":
                return

            norm_apply(2, hn)
            row = lmT[:, 0, 0:P].bitcast(U32)
            col = lmT[:, 0, P:2 * P].bitcast(U32)
            xr = lmT[:, 0, 2 * P:3 * P].bitcast(U32)
            sh = lmT[:, 0, 3 * P:4 * P].bitcast(U32)
            up, dn, shf = lmT[:, 1, 0:P], lmT[:, 1, P:2 * P], lmT[:, 1, 2 * P:3 * P]
            dve.wait_ge(s["lm_iota"], 1)
            tt(xr, row, col, ALU.bitwise_xor)
            tt(up, row, col, ALU.is_lt)
            link(tt(dn, row, col, ALU.is_gt))
            for l in range(7):
                link(ts(sh, xr, l, None, ALU.logical_shift_right))
                link(ts(shf, sh, 1, None, ALU.is_equal))
                tt(maskl[:, 0, l, :], shf, dn, ALU.mult)
                link(tt(maskl[:, 1, l, :], shf, up, ALU.mult))

            ab = small_in("ab")
            dve.wait_ge(s["ba_mm"], 2)
            link(ts(soft_r[0], ps[2][0:GH, :], ab[0:GH, 1:2], None, ALU.add))
            stt(soft_r[1], soft_r[0], -1.0, soft_r[0], ALU.mult, ALU.max).then_inc(s["a_abs"], 1)
            dve.memset(soft_r[3], 1.0)
            link(ts(soft_r[0], soft_r[0], 0.0, None, ALU.max))
            dve.memset(soft_r[3].rearrange("p (t x) -> p t x", t=TT)[:, :, 0:1], 0.0)
            dve.wait_ge(s["a_exp"], 1)
            ts(soft_r[1], soft_r[1], 1.0, None, ALU.add).then_inc(s["a_one"], 1)
            link(ts(cols[0:GH, 2:3], cols[0:GH, 2:3], -1.0, None, ALU.mult))
            dve.wait_ge(s["a_ln"], 1)
            link(tt(soft_r[0], soft_r[0], soft_r[1], ALU.add))
            link(ts(soft_r[0], soft_r[0], cols[0:GH, 2:3], None, ALU.mult))
            dve.tensor_tensor_scan(dec_r, soft_r[3], soft_r[0], 0.0, ALU.mult, ALU.add).then_inc(s["dec_ready"], 1)

            def conv_group(i):
                dve.wait_ge(s["acc_free"], i * 4 + (STREAMS["od_in"][0] + 4 + 2))
                for j in (3, 2, 1, 0):
                    d = 3 - j
                    for e in range(4):
                        c = bass.ds(i * 4 + e, 1)
                        w = conv_w[:, c, j:j + 1].rearrange("p a b -> p (a b)")
                        src = raw[:, c, 0:T - d].rearrange("p a t -> p (a t)")
                        dst = conv[:, c, d:T].rearrange("p a t -> p (a t)")
                        m = ts(dst, src, w, None, ALU.mult) if d == 0 else stt(dst, src, w, dst, ALU.mult, ALU.add)
                    if j:
                        link(m)
                m.then_inc(s["conv_done"], 1)

            conv_group(0)
            conv_group(1)
            dve.memset(cols[:, 1:2], 0.0).then_inc(s["l2_done"], 1)
            start = own.base + own.k
            for lo, scale in ((0, GDN_SCALE), (2, 1.0)):
                with dve.Fori(lo, lo + 2) as g:
                    own.base, own.k = g * 3 + start, 0
                    dve.wait_ge(s["l2_root"], g + 1)
                    qk = conv[:, bass.ds(g * 4, 4), :]
                    stt(qk, qk, scale, scr[:, :, :], ALU.mult, ALU.mult).then_inc(s["l2_done"], 1)
                    conv_group(g + 2)
            own.base, own.k = start + 12, 0

            for grp in range(2):
                hs = range(4 * grp, 4 * grp + 4)
                dve.wait_ge(s["cols_ready"], 1)
                dve.wait_ge(s["l2_done"], 5)
                for hh, hd in enumerate(hs):
                    dve.wait_ge(s["bc_mm"], 4 * grp + hh + 1)
                    tt(kbT[:, hh, :], conv[:, GH + hd, :], ps[BA[hh]][:, :], ALU.mult).then_inc(s["kb_ready"], 1)
                    dve.wait_ge(s["gq_exp"], 4 * grp + hh + 1)
                    dve.tensor_copy(last_c[:, hd, :], ps[3 + hh][:, :].rearrange("p (t x) -> p t x", t=TT)[:, :, P - 1])
                    for t in range(TT):
                        m = ts(lmT[:, hh, P * t:P * t + P], ps[3 + hh][:, P * t:P * t + P], dec_c[:, t, hd:hd + 1], 0.0,
                               ALU.subtract, ALU.min)
                    m.then_inc(s["lm_min"], 1)
                dve.wait_ge(s["lm_min"], 4 * grp + 4)
                hsl = slice(4 * grp, 4 * grp + 4)
                tt(tail_c[:, :, hsl], last_c[:, hsl, :].rearrange("p h t -> p t h"), dec_c[:, :, hsl],
                   ALU.subtract).then_inc(s["last_ready"], 1)
                dve.wait_ge(s["small_exp"], grp + 1)
                tt(kbe_c[:, :, hsl], kbe_c[:, :, hsl], beta_c[:, :, hsl], ALU.mult).then_inc(s["scale_cols"], 1)
                for hh, hd in enumerate(hs):
                    dve.wait_ge(s["gq_exp"], 4 * grp + hh + 1)
                    tt(qdT[:, hh, :], conv[:, hd, :], qdT[:, hh, :], ALU.mult).then_inc(s["qd_ready"], 1)
                for hh in range(4):
                    dve.wait_ge(s["kk_mm"], 4 * grp + hh + 1)
                    dve.wait_ge(s["lm_exp"], 4 * grp + hh + 1)
                    stt(negA[:, hh, :], ps[BA[hh]][:, :], -1.0, lmT[:, hh, :], ALU.mult,
                        ALU.mult).then_inc(s["negA_ready"], 1)
                for hh, hd in enumerate(hs):
                    dve.wait_ge(s["kbe_ready"], 4 * grp + hh + 1)
                    for t in range(TT):
                        m = ts(ktail[:, hh, t, :], ps[3 + hh][:, P * t:P * t + P], tail_c[:, t, hd:hd + 1], None,
                               ALU.mult)
                    m.then_inc(s["ktail_ready"], 1)
                eye = ident[:, :].unsqueeze(1).to_broadcast([P, TT, P])
                for hh in range(4):
                    dve.tensor_copy(inv[:, hh, :].rearrange("p (t x) -> p t x", t=TT), eye)
                    dve.tensor_copy(invT[:, hh, :].rearrange("p (t x) -> p t x", t=TT), eye).then_inc(s["wt_done"], 1)
                dve.wait_ge(s["wt_done"], 32 * grp + 4)
                start = own.base + own.k
                with dve.Fori(0, 7) as l:
                    own.base, own.k = l + start, 0
                    link(dve.tensor_copy(mcur, maskl[:, :, bass.ds(l, 1), :].rearrange("p a b x -> p a (b x)")))
                    for hh in range(4):
                        dve.wait_ge(s["y_mm"], l * 4 + (28 * grp + hh + 1))
                        alone()
                        for m, (dst, bank) in enumerate(((inv, 3), (invT, 5))):
                            q = dve.copy_predicated(dst[:, hh, :].rearrange("p (t x) -> p t x", t=TT),
                                                    mcur[:, m, :].bitcast(U32).unsqueeze(1).to_broadcast([P, TT, P]),
                                                    ps[bank + hh % 2][:, :].rearrange("p (t x) -> p t x", t=TT))
                        q.then_inc(s["wt_done"], 1)
                    dve.wait_ge(s["wt_done"], l * 4 + (32 * grp + 8))
                    alone()
                own.base, own.k = start + 7, 0
                for hh in range(4):
                    dve.wait_ge(s["qk_mm"], 4 * grp + hh + 1)
                    tt(negA[:, hh, :], ps[3 + hh][:, :], lmT[:, hh, :], ALU.mult).then_inc(s["att_raw"], 1)
                for t in range(TT - 1):
                    for hh, hd in enumerate(hs):
                        n = (grp * 3 + t) * 4 + hh + 1
                        dve.wait_ge(s["gds_mm"], n)
                        ds = ps[BA[hh]][:, P:2 * P]
                        if t:
                            m = stt(gstate[:, hh, :], gstate[:, hh, :], tot_c[:, hd, t:t + 1], ds, ALU.mult, ALU.add)
                        else:
                            m = dve.tensor_copy(gstate[:, hh, :], ds)
                        m.then_inc(s["gs_ready"], 1)
                    dve.wait_ge(s["gs_ready"], (grp * 3 + t) * 4 + 4)
                for hh, hd in enumerate(hs):
                    dve.wait_ge(s["g_root"], 4 * grp + hh + 1)
                    link(stt(xs[:, 2, :], ps[3 + hh][:, :], gn_col[:, 1:2], lmT[:, hh, :], ALU.mult, ALU.mult))
                    tt(zT[:, hd, :], xs[:, 2, :], zT[:, hd, :], ALU.mult).then_inc(s["mix_ready"], 1)
                    dve.wait_ge(s["mix_ready"], 8 + 4 * grp + hh + 1)
            if stop_after == "mix1":
                return
            add_stream("od_out")
            peer(1)
            norm_apply(4, hn)


def host_layout(i):
    import numpy as np
    f = {k: np.asarray(v) for k, v in i.items()}

    def chunks(w):
        k, n = w.shape
        return w.reshape(k // P, P, n // P, P).transpose(2, 1, 0, 3)

    def rows(w, c):
        return np.moveaxis(w.reshape((c, P) + w.shape[1:]), 0, 1)

    ev = f["ev_in_w"][0]
    ev = np.concatenate([ev[:, 2048:2560], ev[:, 0:2048]], axis=1)
    od = f["od_in_w"][0]
    wall = np.concatenate([chunks(w) for w in (ev, f["ev_out_w"][0], f["peer_wq"][0], od[:, 0:4096],
                                               f["od_out_w"][0], f["peer_wq"][1])])
    norm = np.concatenate([f["norm_mix_w"][0:1], f["norm_ffn_w"][0:1], f["norm_mix_w"][1:2],
                           f["norm_ffn_w"][1:2], f["norm_out_w"][None]])
    b = np.zeros((4, 2, 16, 2, 4, 2, 64), np.float32)
    c = np.zeros((2, 64, 2, ST, 2, 16), np.float32)
    for n, (bn, cn) in enumerate((("s5_b_re", "s5_c_re"), ("s5_b_im", "s5_c_im"))):
        bb = f[bn][0].reshape(4, 4, 2, 64, 16)
        cc = f[cn][0].reshape(ST, 2, 16, 64)
        for g in range(2):
            b[:, g, :, n, :, g, :] = bb[:, :, g].transpose(1, 3, 0, 2)
            c[g, :, n, :, g, :] = cc[:, g].transpose(2, 0, 1)
    ab = np.zeros((P, 2), np.float32)
    ab[0:GH, 0], ab[0:GH, 1] = f["gdn_a_log"][0], f["gdn_dt_bias"][0]
    parts = {
        "norm_w": norm.reshape(5, DC, P).transpose(2, 0, 1),
        "s5_are": f["s5_a_re"][0].reshape(ST, P).T,
        "s5_aim": f["s5_a_im"][0].reshape(ST, P).T,
        "s5_ldt": np.repeat(f["s5_log_dt"][0], 64).reshape(ST, P).T,
        "s5_d": f["s5_d"][0].reshape(4, P).T,
        "lb": f["hgrn_lb"].reshape(2, 4, P).transpose(2, 0, 1),
        "gn": np.stack([f["hgrn_gn_w"][0], f["gdn_gn_w"][0]], axis=1),
        "conv": f["gdn_conv_w"][0].reshape(4, 24, P).transpose(2, 1, 0),
        "ab": ab,
        "ba_w": rows(od[:, 4096:4112], DC),
        "keys": f["peer_sub_keys"].transpose(3, 0, 1, 2),
    }
    small = np.concatenate([parts[n].reshape(P, w) for n, w in SMALL], axis=1)
    return {
        "xT": rows(f["x"][0].T, DC), "wall": wall, "glu_w": rows(f["s5_glu_w"][0], 4),
        "s5_b": b.reshape(P, 2, 4, P), "s5_c": c.reshape(P, 2, ST, 32), "small": small,
        "u_tab": f["peer_u"].reshape(2 * E, D), "v_tab": f["peer_v"].reshape(2 * E, D),
    }


def kernel(**inputs):
    import numpy as np
    import concourse.bacc as bacc
    from concourse.bass_utils import run_bass_kernel_spmd

    nc = bacc.Bacc("TRN2", target_bir_lowering=False, num_devices=1)
    arrays = {n: np.ascontiguousarray(a) for n, a in host_layout(inputs).items()}
    args = [nc.dram_tensor(n, a.shape, mybir.dt.from_np(a.dtype), kind="ExternalInput").ap()
            for n, a in arrays.items()]
    out = nc.dram_tensor("out", (P, DC, T), F32, kind="ExternalOutput").ap()
    trunk(nc, *args, out)
    r = run_bass_kernel_spmd(nc, [arrays], core_ids=[0])
    got = r.results[0]["out"]
    return got.transpose(2, 1, 0).reshape(1, T, D)
```

```python
from contextlib import ExitStack

import concourse.bass as bass
from concourse import mybir

F32 = mybir.dt.float32
I32 = mybir.dt.int32
U32 = mybir.dt.uint32
ALU = mybir.AluOpType
ACT = mybir.ActivationFunctionType
AX = mybir.AxisListType

P = 128
D = 1024
T = 512
DC = D // P
TT = T // P
HG = 4
HC = 32
NCH = T // HC
ST = 16
GH = 8
PH = 8
NK = 128
TOPK = 16
E = NK * NK
EPS = 1e-6
HGRN_SCALE = 128 ** -0.5
GDN_SCALE = 128 ** -0.5
TWO_PI_HI = 6.28125
TWO_PI_LO = 6.283185307179586 - 6.28125
ROUND = 12582912.0
LOWEST = -3.0e38
NU = 8
NV = 8
ROUTE_LINKS = 21
HEADS = PH * TT

STREAMS = {"ev_in": (0, 20, 0), "ev_out": (20, 8, 20), "wq0": (28, 16, 28), "od_pre": (44, 24, 44),
           "od_in": (68, 32, 44), "od_out": (100, 8, 76), "wq1": (108, 16, 84)}
PRE = T - P
EARLY = 8
NSLOT = 4

SMALL = [("norm_w", 5 * DC), ("s5_are", ST), ("s5_aim", ST), ("s5_ldt", ST), ("s5_d", 4),
         ("lb", 8), ("gn", 2), ("conv", 96), ("ab", 2), ("ba_w", DC * 16), ("keys", 4 * NK)]
SMALL_AT = {}
_at = 0
for _n, _w in SMALL:
    SMALL_AT[_n] = (_at, _w)
    _at += _w
NSMALL = _at

ARENA = 40064


class Chain:

    def __init__(self, eng, sem):
        self.eng, self.sem, self.base, self.k = eng, sem, 0, 0

    def link(self, ins):
        self.k += 1
        ins.then_inc(self.sem, 1)
        self.eng.wait_ge(self.sem, self.base + self.k)


def trunk(nc, xT, wall, glu_w, s5_b, s5_c, small, u_tab, v_tab, out):
    ctx = ExitStack()
    with ctx:
        def sb(name, shape, dt=F32):
            return ctx.enter_context(nc.sbuf_tensor(name, shape, dt))

        def sem(name):
            return ctx.enter_context(nc.semaphore(name))

        h = sb("h", [P, DC, T])
        wring = sb("wring", [P, NSLOT, DC, P])
        scr = sb("scr", [P, 4, T])
        consts = sb("consts", [P, NSMALL])
        ident = sb("ident", [P, P])
        mean_d = sb("mean_d", [P, P])
        mean_h = sb("mean_h", [P, P])
        ones = sb("ones", [P, P])
        maskc = sb("maskc", [P, P])
        mask32 = sb("mask32", [P, P])
        iota16 = sb("iota16", [P, TOPK])
        cols = sb("cols", [P, 640])
        rt = sb("rt", [P, T])
        arena = sb("arena", [P, ARENA])
        ps = [ctx.enter_context(nc.psum_tensor(f"ps{i}", [P, T], F32)) for i in range(8)]

        def region(at, *shape):
            n = 1
            for x in shape:
                n *= x
            assert at + n <= ARENA, (at, n)
            v = arena[:, at:at + n]
            if len(shape) == 2:
                return v.rearrange("p (a b) -> p a b", a=shape[0])
            if len(shape) == 3:
                return v.rearrange("p (a b c) -> p a b c", a=shape[0], b=shape[1])
            return v

        def small_in(name):
            a, w = SMALL_AT[name]
            return consts[:, a:a + w]

        norm_w = small_in("norm_w").rearrange("p (n k) -> p n k", k=DC)
        conv_w = small_in("conv").rearrange("p (c j) -> p c j", j=4)
        ba_w = small_in("ba_w").rearrange("p (k m) -> p k m", m=16)
        keys = small_in("keys").rearrange("p (l c k) -> p l c k", l=2, c=2)
        gn_col = small_in("gn")
        eps_col = cols[:, 0:1]

        maskl = region(12544, 2, 7, P)

        hn = region(0, DC, T)
        proj = region(4096, 20, T)
        uT, qT, fT, vT0, gT = (proj[:, 4 * i:4 * i + 4, :] for i in range(5))
        tab_c = region(14336, ST, T)
        tab_s = region(22528, ST, T)
        bw = region(30720, 2, 4, P)
        cw = region(31744, 2, ST, 32)
        s5w = [[region(32768 + T * i, T) for i in range(6)], [region(35840 + T * i, T) for i in range(6)],
               [scr[:, 0, :], scr[:, 1, :], scr[:, 2, :], scr[:, 3, :], rt[:, :], region(38912, T)]]
        tab_t = region(32768, 2, 2048)
        kA = region(14336, HG, T)
        eC = region(16384, HG, T)
        kE = region(18432, HG, T)
        kD = region(20480, HG, T)
        kTok = region(22528, HG, TT, P)
        vTok = region(24576, HG, TT, P)
        glu_sb = region(36864, 4, T)
        totH = cols[:, 64:128].rearrange("p (h c) -> p h c", h=HG)
        mix0 = [qT[:, j, :] for j in range(4)] + [uT[:, j, :] for j in range(4)]
        statesA = [region(26624, NCH, P), region(28672, NCH, P), region(32768, NCH, P), region(34816, NCH, P)]

        raw_q = region(0, 8, T)
        raw_k = region(8448, 8, T)
        raw_v = region(35072, 8, T)
        zT = region(14592, GH, T)
        conv = region(18688, 24, T)
        mask_w = region(6144, 2, T)
        soft_r = [region(4096 + T * i, T)[0:GH] for i in range(4)]
        beta_r = region(39168, T)[0:GH]
        dec_r = rt[0:GH, :]
        dec_c = cols[:, 64:96].rearrange("p (t h) -> p t h", h=GH)
        beta_c = cols[:, 96:128].rearrange("p (t h) -> p t h", h=GH)
        last_c = cols[:, 128:160].rearrange("p (h t) -> p h t", t=TT)
        kbe_c = cols[:, 160:192].rearrange("p (t h) -> p t h", h=GH)
        tail_c = cols[:, 192:224].rearrange("p (t h) -> p t h", h=GH)
        tot_c = cols[:, 224:256].rearrange("p (h t) -> p h t", t=TT)
        kbT = region(0, 4, T)
        qdT = region(2048, 4, T)
        vb = region(4096, 4, TT, P)
        kbe = region(6144, 4, TT, P)
        ktail = region(8192, 4, TT, P)
        invT = region(10240, 4, T)
        negA = region(30976, 4, T)
        inv = region(33024, 4, T)
        lmT = region(35072, 4, T)
        xs = region(37120, 4, T)
        gstate = region(37120, 4, P)
        vnew = region(37632, 4, P)
        mcur = region(12288, 2, P)
        mix1 = [zT[:, j, :] for j in range(GH)]

        sc = region(0, HEADS + 1, 2 * NK)
        xtok = region(8448, TT, D)
        xcur = region(12544, D)
        ycur = region(13568, D)
        uring = region(14592, NU, D)
        vring = region(22784, NV, D)
        sct = region(39168, 2, 2, NK)
        phn = region(30976, DC, T)
        ysq = ycur.rearrange("p (k t) -> p k t", k=DC)
        trt = cols[:, 480:608]
        pq = region(35072, 2, 2, T)
        cand = rt[:, 0:TOPK * TOPK]
        hot = rt[:, TOPK * TOPK:2 * TOPK * TOPK].rearrange("p (a b) -> p a b", a=TOPK)
        diag = scr[:, :, :].rearrange("p a (b c) -> p (a b) c", c=P)

        def rcol(i, n, dt=F32):
            return cols[:, i:i + n].bitcast(dt) if dt is not F32 else cols[:, i:i + n]

        top_v = rcol(64, 32).rearrange("p (c k) -> p c k", c=2)
        top_i = rcol(96, 32, U32).rearrange("p (c k) -> p c k", c=2)
        top_f = rcol(128, 32).rearrange("p (c k) -> p c k", c=2)
        sel_v, sel_p = rcol(160, TOPK), rcol(176, TOPK, U32)
        sel_a, sel_b = rcol(192, TOPK, U32), rcol(208, TOPK, U32)
        pos_a, pos_b = rcol(224, TOPK), rcol(240, TOPK)
        exp_a, exp_b = rcol(256, TOPK), rcol(272, TOPK)
        soft_e, soft_m, soft_s = rcol(288, TOPK), rcol(304, 1), rcol(305, 1)
        ids = [rcol(320 + 16 * i, TOPK, U32) for i in range(2)]
        gate = [rcol(352 + 16 * i, TOPK) for i in range(2)]
        dots = [rcol(384 + 16 * i, TOPK) for i in range(2)]
        gelu = [rcol(416 + 16 * i, TOPK) for i in range(2)]
        wgt = [rcol(448 + 16 * i, TOPK) for i in range(2)]

        s = {n: sem(n) for n in (
            "lm_iota", "conv_done", "silu", "l2_sq", "l2_sum", "l2_root", "l2_done", "ba_mm", "a_abs",
            "a_exp", "a_one", "a_ln", "beta_ready", "dec_ready", "col_tr", "cols_ready", "bc_mm",
            "last_ready", "kb_ready", "lm_min", "gq_exp", "lm_exp", "small_exp", "scale_cols",
            "kk_mm", "negA_ready", "ktr_mm", "kbe_ready", "ktail_ready", "vtr_mm",
            "vb_ready", "eye_ready", "wt_done", "x_mm", "xs_copied", "y_mm", "kc_mm", "kc_ready",
            "qk_mm", "att_raw", "att_ready", "vn_mm", "vn_ready", "gds_mm", "gs_ready", "go_done",
            "g_sq", "g_sum", "g_root", "xt_tr", "xt_copied", "sc_mm", "sc_ready", "sct_ready",
            "soft_in", "soft_exp", "ids_ready", "u_free", "v_free", "gelu_ready", "w_ready",
            "diag_ready", "y_copied", "hy_ready", "peer_done", "tile_sq", "tile_sum", "tile_root",
            "tile_normed", "x_loaded", "small_loaded", "bc_loaded", "glu_loaded", "out_stored",
            "const_pool", "masks_built", "sq_ready", "sum_ready", "root_ready", "hn_ready", "hn_first",
            "q_first", "q_first_copied", "sc_first", "acc_ready", "acc_free", "dve_own", "act_own",
            "pool_own", "dve_passed", "act_passed", "pool_passed", "s5_theta", "s5_trig",
            "s5_trig_exp", "s5_wc", "tab_dve", "tab_pool", "s5_ctab", "s5_bu", "s5_bcopy", "s5_wr",
            "s5_wi", "s5_scan", "s5_pr", "s5_pi", "s5_y", "s5_ysum", "s5_gelu", "s5_glu", "s5_sig",
            "lb_e", "lb_d", "hg_f", "hg_ln", "hg_k", "hg_cum", "hg_dif", "hg_exp", "hg_ke", "hg_kd",
            "hg_att", "hg_attm", "hg_tr", "hg_trc", "hg_ds", "hg_st", "hg_o", "hg_sq", "hg_sum",
            "hg_root", "mix_ready")}
        u_arrived = [sem(f"u_arrived{i}") for i in range(NU)]
        v_arrived = [sem(f"v_arrived{i}") for i in range(NV)]
        w_arrived = [sem(f"w_arrived{i}") for i in range(NSLOT)]

        block = ctx.enter_context(nc.Block())

        def s5t(i, w):
            return tab_t[:, i, 0:ST * w].rearrange("p (a b) -> p a b", a=ST)

        @block.sync
        def _(sp):
            sp.dma_start(h[:, :, :], xT).then_inc(s["x_loaded"], 16)
            sp.dma_start(consts[:, :], small).then_inc(s["small_loaded"], 16)
            sp.dma_start(bw, s5_b).then_inc(s["bc_loaded"], 16)
            sp.dma_start(cw, s5_c).then_inc(s["bc_loaded"], 16)

            def load_stream(name, first=False):
                c0, n, at = STREAMS[name]
                start = 0
                if first:
                    for j in range(NSLOT):
                        sp.dma_start(wring[:, j, :, :], wall[at + j]).then_inc(w_arrived[j], 16)
                    start = NSLOT
                with sp.Fori(start // NSLOT, n // NSLOT) as i:
                    for j in range(NSLOT):
                        sp.wait_ge(s["acc_ready"], i * NSLOT + (c0 + j - NSLOT + 1))
                        sp.dma_start(wring[:, j, :, :],
                                     wall[bass.ds(i * NSLOT + (at + j), 1)].rearrange("a p k n -> (a p) k n")
                                     ).then_inc(w_arrived[j], 16)

            load_stream("ev_in", first=True)
            sp.wait_ge(s["s5_y"], ST)
            sp.dma_start(glu_sb, glu_w).then_inc(s["glu_loaded"], 16)
            load_stream("ev_out")
            load_stream("wq0")
            load_stream("od_pre")
            load_stream("od_in")
            load_stream("od_out")
            load_stream("wq1")
            for t in range(TT):
                sp.wait_ge(s["tile_normed"], TT + t + 1)
                sp.dma_start(out[:, :, P * t:P * t + P], phn[:, :, P * t:P * t + P]).then_inc(s["out_stored"], 16)
            sp.wait_ge(s["out_stored"], 16 * TT)

        @block.gpsimd
        def _(pool):
            own = Chain(pool, s["pool_own"])
            pool.memset(ident[:, :], 0.0)
            pool.memset(mean_d[:, :], 1.0 / D)
            pool.memset(mean_h[:, :], 1.0 / P)
            pool.memset(maskc[:, :], 1.0)
            own.link(pool.memset(ones[:, :], 1.0))
            pool.affine_select(out=ident[:, :], in_=ident[:, :], compare_op=ALU.not_equal, fill=1.0, base=0,
                               pattern=[[-1, P]], channel_multiplier=1)
            pool.affine_select(out=maskc[:, :], in_=maskc[:, :], compare_op=ALU.is_ge, fill=0.0, base=0,
                               pattern=[[1, P]], channel_multiplier=-1)
            pool.iota(iota16[:, :], [[1, TOPK]], base=0, channel_multiplier=0,
                      allow_small_or_imprecise_dtypes=True)
            row = scr[:, 0, 0:P].bitcast(I32)
            col = scr[:, 0, P:2 * P].bitcast(I32)
            pool.iota(row, [[0, P]], base=0, channel_multiplier=1)
            pool.iota(col, [[1, P]], base=0, channel_multiplier=0).then_inc(s["const_pool"], 1)

            for m in range(9):
                w = 1 << m
                pool.wait_ge(s["s5_ctab"], m + 1)
                if m:
                    pool.wait_ge(s["tab_dve"], m)
                step = min(w, 128)
                for a in range(0, w, step):
                    tmp = s5t(1, step)
                    cmb = cols[:, 128 + 32 * m:144 + 32 * m].unsqueeze(2).to_broadcast([P, ST, step])
                    smb = cols[:, 144 + 32 * m:160 + 32 * m].unsqueeze(2).to_broadcast([P, ST, step])
                    pool.tensor_tensor(tab_s[:, :, w + a:w + a + step], tab_s[:, :, a:a + step], cmb, ALU.mult)
                    own.link(pool.tensor_tensor(tmp, tab_c[:, :, a:a + step], smb, ALU.mult))
                    last = pool.tensor_tensor(tab_s[:, :, w + a:w + a + step], tab_s[:, :, w + a:w + a + step], tmp,
                                              ALU.add)
                    if a + step < w:
                        own.link(last)
                last.then_inc(s["tab_pool"], 1)
                pool.wait_ge(s["tab_pool"], m + 1)

            def s5_wi(st):
                W = s5w[st % 3]
                pool.wait_ge(s["s5_bcopy"], 2 * st + 2)
                if st == 0:
                    pool.wait_ge(s["tab_dve"], 9)
                if st >= 3:
                    pool.wait_ge(s["s5_y"], st - 2)
                pool.tensor_tensor(W[5], W[1], tab_c[:, st, :], ALU.mult)
                own.link(pool.tensor_tensor(W[3], W[0], tab_s[:, st, :], ALU.mult))
                pool.tensor_tensor(W[3], W[5], W[3], ALU.subtract).then_inc(s["s5_wi"], 1)

            s5_wi(0)
            for st in range(ST):
                if st + 1 < ST:
                    s5_wi(st + 1)
                W = s5w[st % 3]
                pool.wait_ge(s["s5_scan"], 2 * st + 2)
                pool.tensor_tensor(W[1], W[2], tab_s[:, st, :], ALU.mult)
                pool.tensor_tensor(W[5], W[3], tab_c[:, st, :], ALU.mult).then_inc(s["s5_pi"], 1)

            pool.wait_ge(s["hg_f"], 4)
            pool.wait_ge(s["s5_y"], ST)
            pool.tensor_scalar(kA, fT, -1.0, 1.0, ALU.mult, ALU.add).then_inc(s["hg_k"], 1)
            pool.wait_ge(s["hg_exp"], 3)
            pool.tensor_tensor(kD, kA, kD, ALU.mult).then_inc(s["hg_kd"], 1)

            def peer(layer):
                def head(g, par):
                    pool.wait_ge(s["ids_ready"], g + ((HEADS + 1) * layer + 1))
                    for ring, tab, n, free, extra, arrived in ((uring, u_tab, NU, "u_free", 0, u_arrived),
                                                               (vring, v_tab, NV, "v_free", TOPK - NV, v_arrived)):
                        for k in range(TOPK):
                            pool.wait_ge(s[free], g * TOPK + (TOPK * HEADS * layer + extra + k + 1))
                            pool.sem_inc(s["pool_passed"], 1)
                            pool.indirect_dma_start(
                                out=ring[:, k % n, :], out_offset=None, in_=tab,
                                in_offset=bass.IndirectOffsetOnAxis(ap=ids[par][:, k:k + 1], axis=0)
                            ).then_inc(arrived[k % n], 16)

                with pool.Fori(0, HEADS // 2) as p:
                    for par in range(2):
                        head(p * 2 + par, par)

            peer(0)

            pool.wait_ge(s["peer_done"], TT)
            row = mask_w[:, 0, 0:P].bitcast(I32)
            col = mask_w[:, 0, P:2 * P].bitcast(I32)
            pool.iota(row, [[0, P]], base=0, channel_multiplier=1)
            pool.iota(col, [[1, P]], base=0, channel_multiplier=0).then_inc(s["lm_iota"], 1)

            for grp in range(2):
                if grp:
                    pool.wait_ge(s["go_done"], 4)
                else:
                    pool.wait_ge(s["bc_mm"], 1)
                for x in (inv, invT):
                    m = pool.tensor_copy(x.rearrange("p h (t x) -> p (h t) x", t=TT),
                                         ident[:, :].unsqueeze(1).to_broadcast([P, 4 * TT, P]))
                m.then_inc(s["eye_ready"], 1)
                for hh in range(4):
                    pool.wait_ge(s["att_raw"], 4 * grp + hh + 1)
                    pool.tensor_tensor(negA[:, hh, :].rearrange("p (t x) -> p t x", t=TT),
                                       negA[:, hh, :].rearrange("p (t x) -> p t x", t=TT),
                                       maskc[:, :].unsqueeze(1).to_broadcast([P, TT, P]),
                                       ALU.mult).then_inc(s["att_ready"], 1)
            peer(1)

        @block.tensor
        def _(pe):
            def norm_sum(n):
                for k in range(DC):
                    pe.wait_ge(s["sq_ready"], DC * n + k + 1)
                    mm = pe.matmul(ps[2][:, :], mean_d[:, :], scr[:, k % 4, :], start=(k == 0), stop=(k == DC - 1))
                    mm.then_inc(s["sum_ready"], 1)

            def stream(name, rhs, upto):
                c0 = STREAMS[name][0]
                with pe.Fori(0, upto // NSLOT) as i:
                    for j in range(NSLOT):
                        chunk(c0, i * NSLOT + j, j, rhs)

            def out_stream(name, mix, order, base):
                c0, n, _ = STREAMS[name]
                for j in range(NSLOT):
                    if j:
                        chunk(c0, j, j, lambda k: mix[k])
                    else:
                        chunk(c0, j, j, lambda k: mix[k], order=order, base=base)
                with pe.Fori(1, n // NSLOT) as i:
                    for j in range(NSLOT):
                        chunk(c0, i * NSLOT + j, j, lambda k: mix[k])

            def chunk(c0, c, j, rhs, width=T, order=range(DC), base=None):
                pe.wait_ge(w_arrived[j], (c - j) * 4 + (4 * c0 + 16))
                pe.wait_ge(s["acc_free"], c + (c0 + 1))
                for n, k in enumerate(order):
                    if base is not None and n >= 4:
                        pe.wait_ge(s["mix_ready"], base + n + 1)
                    mm = pe.matmul(ps[j % 2][:, 0:width], wring[:, j, k, :], rhs(k), start=(n == 0), stop=(n == DC - 1))
                mm.then_inc(s["acc_ready"], 1)

            pe.wait_ge(s["const_pool"], 1)
            norm_sum(0)
            pe.wait_ge(s["hn_ready"], DC)

            def s5_in(st):
                q, jj = st // 4, st % 4
                if st >= 2:
                    pe.wait_ge(s["s5_bcopy"], 2 * (st - 2) + 2)
                for i in range(2):
                    mm = pe.matmul(ps[3 + 2 * (st % 2) + i][:, :], bw[32 * jj:32 * jj + 32, i, q, :],
                                   uT[32 * jj:32 * jj + 32, q, :], start=True, stop=True)
                mm.then_inc(s["s5_bu"], 1)

            def s5_out(st):
                q, jj = st // 4, st % 4
                W = s5w[st % 3]
                pe.wait_ge(s["s5_pr"], st + 1)
                pe.wait_ge(s["s5_pi"], st + 1)
                if jj == 0 and q:
                    pe.wait_ge(s["s5_ysum"], q)
                o = ps[7][32 * jj:32 * jj + 32, :]
                for n, (w, x) in enumerate(((0, 0), (0, 4), (1, 1), (1, 5))):
                    mm = pe.matmul(o, cw[:, w, st, :], W[x], start=(n == 0), stop=(n == 3))
                mm.then_inc(s["s5_y"], 1)

            stream("ev_in", lambda k: hn[:, k, :], upto=EARLY)
            pe.wait_ge(s["bc_loaded"], 32)
            late = iter(range(EARLY, 20))
            s5_in(0)
            for st in range(ST + 1):
                if st + 1 < ST:
                    s5_in(st + 1)
                c = next(late, None)
                if c is not None:
                    chunk(0, c, c % 4, lambda k: hn[:, k, :])
                if st:
                    s5_out(st - 1)

            pe.wait_ge(s["s5_gelu"], 1)
            pe.wait_ge(s["glu_loaded"], 16)
            for n in range(4):
                for k in range(4):
                    mm = pe.matmul(ps[3 + n][:, :], glu_sb[:, k, P * n:P * n + P], uT[:, k, :],
                                   start=(k == 0), stop=(k == 3))
                mm.then_inc(s["s5_glu"], 1)

            BA = (0, 1, 2, 7)
            pe.wait_ge(s["hg_ke"], 2)
            for hd in range(HG):
                for t in range(TT):
                    c = slice(P * t, P * t + P)
                    mm = pe.matmul(ps[BA[hd]][:, c], kE[:, hd, c], qT[:, hd, c], start=(t == 0), stop=(t == TT - 1),
                                   skip_group_check=True)
                mm.then_inc(s["hg_att"], 1)
            pe.wait_ge(s["s5_sig"], 4)
            pe.wait_ge(s["hg_kd"], 1)
            for i in range(8):
                hd = i % 4
                src = kD if i < 4 else vT0
                if i >= 4:
                    pe.wait_ge(s["hg_trc"], i - 3)
                for t in range(TT):
                    c = slice(P * t, P * t + P)
                    mm = pe.transpose(ps[3 + hd][:, c], src[:, hd, c], ident[:, :])
                mm.then_inc(s["hg_tr"], 1)
            pe.wait_ge(s["hg_trc"], 8)
            pe.wait_ge(s["hg_attm"], 4)
            for t in range(TT):
                if t >= 2:
                    pe.wait_ge(s["hg_st"], 16 * (t - 1))
                for j in range(4):
                    bank = (BA if t % 2 else (3, 4, 5, 6))[j]
                    for hd in range(HG):
                        r = slice(HC * j, HC * j + HC)
                        mm = pe.matmul(ps[bank][:, P * hd:P * hd + P], kTok[r, hd, t, :], vTok[r, hd, t, :],
                                       start=True, stop=True, skip_group_check=True)
                mm.then_inc(s["hg_ds"], 1)

            def head_sum(hd):
                pe.wait_ge(s["hg_sq"], hd + 1)
                pe.matmul(ps[3 + hd][:, :], mean_h[:, :], scr[:, hd, :], start=True, stop=True).then_inc(s["hg_sum"], 1)

            for hd in range(HG):
                pe.wait_ge(s["hg_st"], 60)
                for t in range(TT):
                    c = slice(P * t, P * t + P)
                    pe.matmul(ps[BA[hd]][:, c], vTok[:, hd, t, :], eC[:, hd, c], start=(t == 0), stop=False,
                              skip_group_check=True)
                for n in range(1, NCH):
                    c = slice(HC * n, HC * n + HC)
                    mm = pe.matmul(ps[BA[hd]][:, c], statesA[hd][:, n, :], qT[:, hd, c], start=False,
                                   stop=(n == NCH - 1), skip_group_check=True)
                mm.then_inc(s["hg_o"], 1)
                if hd:
                    head_sum(hd - 1)
            head_sum(HG - 1)

            def peer(layer):
                norm_sum(layer + 1)
                c0 = STREAMS[f"wq{layer}"][0]
                pe.wait_ge(s["hn_first"], layer + 1)
                for c in range(2):
                    pe.wait_ge(w_arrived[c], 4 * c0 + 16)
                    for k in range(DC):
                        mm = pe.matmul(ps[4 + c][:, 0:P], wring[:, c, k, :], phn[:, k, 0:P], start=(k == 0),
                                       stop=(k == DC - 1))
                    mm.then_inc(s["q_first"], 1)
                pe.wait_ge(s["q_first_copied"], 2 * layer + 2)
                for c in range(2):
                    mm = pe.matmul(ps[6][:, P * c:P * c + P], pq[:, 0, c, 0:P], keys[:, layer, c, :], start=(c == 0),
                                   stop=(c == 1), skip_group_check=True)
                mm.then_inc(s["sc_first"], 1)
                pe.wait_ge(s["hn_ready"], DC * (layer + 2))

                def queries(g, par):
                    first = isinstance(g, int) and g == 0
                    lo = P if first else 0
                    for c in range(2):
                        chunk(c0, g * 2 + c, 2 * par + c, lambda k: phn[:, k, lo:T], T - lo)
                    pe.wait_ge(s["acc_free"], g * 2 + (c0 + 2 + 2))
                    for b in range(2):
                        if layer or not first:
                            pe.wait_ge(s["sc_ready"], g * 2 + (2 * PH * layer + b - 1))
                        ks = range(2 if first and b == 0 else 0, 4)
                        for k in ks:
                            t = 2 * b + k // 2
                            mm = pe.matmul(ps[2 + b][:, P * k:P * k + P], pq[:, par, k % 2, P * t:P * t + P],
                                           keys[:, layer, k % 2, :], start=(k == ks[0]), stop=(k == 3),
                                           skip_group_check=True)
                        mm.then_inc(s["sc_mm"], 1)

                queries(0, 0)
                pe.wait_ge(s["sct_ready"], (HEADS + 1) * layer + 1)
                for n in range(2 * TT):
                    t, half = n // 2, n % 2
                    if n >= 2 or layer:
                        pe.wait_ge(s["xt_copied"], 2 * TT * layer + n - 1)
                    for k in range(4):
                        mm = pe.transpose(ps[6 + n % 2][:, P * k:P * k + P], phn[:, 4 * half + k, P * t:P * t + P],
                                          ident[:, :])
                    mm.then_inc(s["xt_tr"], 1)
                pe.wait_ge(s["xt_copied"], 2 * TT * (layer + 1))

                def head(g, first):
                    for k in range(TOPK):
                        pe.wait_ge(s["diag_ready"], g * TOPK + (TOPK * HEADS * layer + k + 1))
                        pe.wait_ge(v_arrived[k % NV],
                                   (g * (TOPK // NV) + (HEADS * layer * (TOPK // NV) + k // NV + 1)) * 16)
                        for i in range(2):
                            mm = pe.matmul(ps[4 + i][:, :], diag[:, k, :], vring[:, k % NV, T * i:T * i + T],
                                           start=(first and k == 0), stop=False, skip_group_check=True)
                        mm.then_inc(s["v_free"], 1)

                def finish(t):
                    pe.wait_ge(s["y_copied"], t + (TT * layer + 1))
                    for k in range(DC):
                        o = ps[6 + k // 4][:, P * (k % 4):P * (k % 4) + P]
                        pe.matmul(o, ycur[:, P * k:P * k + P], ident[:, :], start=(k % 4 == 0), stop=False,
                                  skip_group_check=True)
                        mm = pe.matmul(o, ident[:, :], h[:, k, bass.ds(t * P, P)], start=False, stop=(k % 4 == 3),
                                       skip_group_check=True)
                    mm.then_inc(s["hy_ready"], 1)
                    pe.wait_ge(s["tile_sq"], t + (TT * layer + 1))
                    for k in range(DC):
                        mm = pe.matmul(ps[3][:, 0:P], mean_d[:, :], ysq[:, k, :], start=(k == 0), stop=(k == DC - 1))
                    mm.then_inc(s["tile_sum"], 1)

                def pair(p):
                    for par in range(2):
                        g = p * 2 + par
                        if not (isinstance(g, int) and g == PH - 1):
                            queries(g + 1, 1 - par)
                        head(g, isinstance(g, int) and g == 0)

                pair(0)
                with pe.Fori(1, PH // 2 - 1) as p:
                    pair(p)
                pair(PH // 2 - 1)
                finish(0)
                with pe.Fori(1, TT if layer else TT - 1) as t:
                    head(t * PH, True)
                    with pe.Fori(1, PH) as g:
                        head(t * PH + g, False)
                    finish(t)
                if layer == 0:
                    g0, c_pre = (TT - 1) * PH, STREAMS["od_pre"][0]

                    def pre(e):
                        for j in range(NSLOT):
                            chunk(c_pre, e * NSLOT + j, j, lambda k: phn[:, k, 0:PRE], PRE)

                    head(g0, True)
                    pe.wait_ge(s["tile_normed"], TT - 1)
                    pre(0)
                    head(g0 + 1, False)
                    with pe.Fori(1, PH // 2 - 1) as p:
                        for par in range(2):
                            pre(p * 2 + (par - 1))
                            head(p * 2 + (g0 + par), False)
                    pre(5)
                    head(g0 + PH - 2, False)
                    head(g0 + PH - 1, False)
                    finish(TT - 1)

            pe.wait_ge(s["mix_ready"], 5)
            out_stream("ev_out", mix0, (4, 5, 6, 7, 0, 1, 2, 3), 0)
            peer(0)

            c0 = STREAMS["od_in"][0]
            pe.wait_ge(s["tile_normed"], TT)
            with pe.Fori(0, 6) as i:
                for j in range(NSLOT):
                    chunk(c0, i * NSLOT + j, j, lambda k: phn[:, k, PRE:T], P)
            for i, bank in enumerate((7, 2)):
                for k in range(DC):
                    mm = pe.matmul(ps[bank][0:GH, :], ba_w[:, k, GH * i:GH * i + GH], phn[:, k, :], start=(k == 0),
                                   stop=(k == DC - 1))
                mm.then_inc(s["ba_mm"], 1)
            with pe.Fori(0, 2) as p:
                for par in range(2):
                    pe.wait_ge(s["l2_sq"], p * 2 + (par + 1))
                    for e in range(4):
                        mm = pe.matmul(ps[3 + e][:, :], ones[:, :], scr[:, e, :], start=True, stop=True)
                    mm.then_inc(s["l2_sum"], 1)
                    for e in range(2):
                        chunk(c0, p * 4 + (24 + 2 * par + e), 2 * par + e, lambda k: phn[:, k, :])
            pe.wait_ge(s["beta_ready"], 1)
            pe.wait_ge(s["dec_ready"], 1)
            for i, r in enumerate((dec_r, beta_r)):
                for t in range(TT):
                    mm = pe.transpose(ps[7][:, 32 * i + GH * t:32 * i + GH * t + GH], r[:, P * t:P * t + P],
                                      ident[0:GH, 0:GH])
            mm.then_inc(s["col_tr"], 1)
            pe.wait_ge(s["acc_free"], c0 + 32 + 2)

            def tile(t):
                return slice(P * t, P * t + P)

            for grp in range(2):
                hs = range(4 * grp, 4 * grp + 4)
                pe.wait_ge(s["cols_ready"], 1)
                pe.wait_ge(s["l2_done"], 4)
                for hh, hd in enumerate(hs):
                    if grp:
                        pe.wait_ge(s["mix_ready"], 8 + hh + 1)
                    pick = ident[0:GH, hd:hd + 1].to_broadcast([GH, P])
                    pe.matmul(ps[BA[hh]][:, :], pick, beta_r, start=True, stop=True)
                    pe.matmul(ps[3 + hh][:, :], pick, dec_r, start=True, stop=True).then_inc(s["bc_mm"], 1)
                for hh, hd in enumerate(hs):
                    pe.wait_ge(s["kb_ready"], 4 * grp + hh + 1)
                    for t in range(TT):
                        mm = pe.matmul(ps[BA[hh]][:, tile(t)], conv[:, GH + hd, tile(t)], kbT[:, hh, tile(t)],
                                       start=(t == 0), stop=(t == TT - 1), skip_group_check=True)
                    mm.then_inc(s["kk_mm"], 1)
                for hh, hd in enumerate(hs):
                    pe.wait_ge(s["lm_min"], 4 * grp + hh + 1)
                    pe.wait_ge(s["gq_exp"], 4 * grp + hh + 1)
                    for t in range(TT):
                        mm = pe.transpose(ps[3 + hh][:, tile(t)], conv[:, GH + hd, tile(t)], ident[:, :])
                    mm.then_inc(s["ktr_mm"], 1)
                pe.wait_ge(s["silu"], 2)
                for hh, hd in enumerate(hs):
                    pe.wait_ge(s["negA_ready"], 4 * grp + hh + 1)
                    for t in range(TT):
                        mm = pe.transpose(ps[BA[hh]][:, tile(t)], conv[:, 2 * GH + hd, tile(t)], ident[:, :])
                    mm.then_inc(s["vtr_mm"], 1)
                pe.wait_ge(s["vb_ready"], 4 * grp + 4)
                pe.wait_ge(s["kbe_ready"], 4 * grp + 4)
                pe.wait_ge(s["ktail_ready"], 4 * grp + 4)
                def level(l):
                    first, last = (isinstance(l, int) and l == x for x in (0, 6))
                    for hh in range(4):
                        if first:
                            pe.wait_ge(s["eye_ready"], grp + 1)
                        else:
                            pe.wait_ge(s["wt_done"], l * 4 + (28 * grp + hh - 3))
                        for t in range(TT):
                            mm = pe.matmul(ps[BA[hh]][:, tile(t)], negA[:, hh, tile(t)], inv[:, hh, tile(t)],
                                           start=(t == 0), stop=(t == TT - 1), skip_group_check=True)
                        mm.then_inc(s["x_mm"], 1)
                    if first:
                        return
                    for hh in range(4):
                        pe.wait_ge(s["xs_copied"], l * 4 + (24 * grp + hh - 3))
                        if hh >= 2:
                            pe.wait_ge(s["wt_done"], l * 4 + (28 * grp + hh - 1))
                        if not last:
                            for t in range(TT):
                                pe.matmul(ps[3 + hh % 2][:, tile(t)], invT[:, hh, tile(t)], xs[:, hh, tile(t)],
                                          start=(t == 0), stop=(t == TT - 1), skip_group_check=True)
                        for t in range(TT):
                            mm = pe.matmul(ps[5 + hh % 2][:, tile(t)], xs[:, hh, tile(t)], invT[:, hh, tile(t)],
                                           start=(t == 0), stop=(t == TT - 1), skip_group_check=True)
                        mm.then_inc(s["y_mm"], 1)

                level(0)
                with pe.Fori(1, 6) as l:
                    level(l)
                level(6)
                pe.wait_ge(s["wt_done"], 28 * grp + 28)
                for hh in range(4):
                    for t in range(TT):
                        mm = pe.matmul(ps[BA[hh]][:, tile(t)], kbe[:, hh, t, :], invT[:, hh, tile(t)],
                                       start=(t == 0), stop=(t == TT - 1), skip_group_check=True)
                    mm.then_inc(s["kc_mm"], 1)
                for hh, hd in enumerate(hs):
                    for t in range(TT):
                        mm = pe.matmul(ps[3 + hh][:, tile(t)], conv[:, GH + hd, tile(t)], conv[:, hd, tile(t)],
                                       start=(t == 0), stop=(t == TT - 1), skip_group_check=True)
                    mm.then_inc(s["qk_mm"], 1)
                pe.wait_ge(s["kc_ready"], 4 * grp + 4)
                pe.wait_ge(s["att_ready"], 4 * grp + 4)
                for t in range(TT):
                    n = (grp * TT + t) * 4
                    for hh in range(4):
                        if t:
                            pe.wait_ge(s["gs_ready"], (grp * 3 + t - 1) * 4 + hh + 1)
                        mm = pe.matmul(ps[BA[hh]][:, 0:P], invT[:, hh, tile(t)], vb[:, hh, t, :], start=True,
                                       stop=(t == 0), skip_group_check=True)
                        if t:
                            mm = pe.matmul(ps[BA[hh]][:, 0:P], kbT[:, hh, tile(t)], gstate[:, hh, :], start=False,
                                           stop=True, skip_group_check=True)
                        mm.then_inc(s["vn_mm"], 1)
                    if t:
                        for hh in range(4):
                            pe.matmul(ps[3 + hh][:, tile(t)], gstate[:, hh, :], qdT[:, hh, tile(t)], start=False,
                                      stop=False, skip_group_check=True)
                    for hh in range(4):
                        pe.wait_ge(s["vn_ready"], n + hh + 1)
                        mm = pe.matmul(ps[3 + hh][:, tile(t)], vnew[:, hh, :], negA[:, hh, tile(t)], start=(t == 0),
                                       stop=(t == TT - 1), skip_group_check=True)
                        if t < TT - 1:
                            pe.matmul(ps[BA[hh]][:, P:2 * P], ktail[:, hh, t, :], vnew[:, hh, :], start=True,
                                      stop=True, skip_group_check=True).then_inc(s["gds_mm"], 1)
                        else:
                            mm.then_inc(s["go_done"], 1)
                for hh in range(4):
                    pe.wait_ge(s["g_sq"], 4 * grp + hh + 1)
                    pe.matmul(ps[BA[hh]][:, :], mean_h[:, :], scr[:, hh, :], start=True,
                              stop=True).then_inc(s["g_sum"], 1)
            pe.wait_ge(s["mix_ready"], DC + 5)
            out_stream("od_out", mix1, range(DC), DC)
            peer(1)

        @block.scalar
        def _(act):
            own = Chain(act, s["act_own"])

            def alone():
                act.sem_inc(s["act_passed"], 1)

            def norm_squares(n):
                for k in range(DC):
                    if n == 0 and k == 0:
                        act.wait_ge(s["x_loaded"], 16)
                        act.wait_ge(s["masks_built"], 1)
                    if n:
                        act.wait_ge(s["acc_free"], STREAMS["ev_out" if n == 1 else "od_out"][0] + 2 + k + 1)
                    if k >= 4:
                        act.wait_ge(s["sum_ready"], DC * n + k - 3)
                    act.activation(scr[:, k % 4, :], h[:, k, :], ACT.Square).then_inc(s["sq_ready"], 1)
                act.wait_ge(s["sum_ready"], DC * n + DC)
                own.link(act.activation(rt[:, :], ps[2][:, :], ACT.Ln, bias=eps_col))
                act.activation(rt[:, :], rt[:, :], ACT.Exp, scale=-0.5).then_inc(s["root_ready"], 1)

            norm_squares(0)
            act.wait_ge(s["small_loaded"], 16)
            act.activation(cols[:, 16:32], small_in("s5_ldt"), ACT.Exp).then_inc(s["s5_trig_exp"], 1)
            act.wait_ge(s["s5_theta"], 1)
            act.activation(cols[:, 32:48], cols[:, 32:48], ACT.Exp).then_inc(s["s5_trig_exp"], 1)
            act.wait_ge(s["lb_d"], 1)
            act.activation(cols[:, 4:12], cols[:, 4:12], ACT.Exp).then_inc(s["lb_e"], 1)
            act.wait_ge(s["s5_theta"], 2)
            act.activation(cols[:, 416:432], cols[:, 416:432], ACT.Sin)
            act.activation(cols[:, 432:448], cols[:, 432:448], ACT.Sin).then_inc(s["s5_trig"], 1)

            def evac(c0, c, dst, func):
                act.wait_ge(s["acc_ready"], c0 + c + 1)
                act.activation(dst, ps[c % 2][:, :], func).then_inc(s["acc_free"], 1)

            def s5_copy(st):
                act.wait_ge(s["s5_bu"], st + 1)
                if st >= 3:
                    act.wait_ge(s["s5_y"], st - 2)
                else:
                    act.wait_ge(s["s5_wc"], 1)
                    act.wait_ge(s["tab_pool"], 9)
                for i in range(2):
                    act.activation(s5w[st % 3][i], ps[3 + 2 * (st % 2) + i][:, :],
                                   ACT.Copy).then_inc(s["s5_bcopy"], 1)

            late = iter(range(EARLY, 20))
            for n in range(EARLY + ST):
                if n >= EARLY:
                    s5_copy(n - EARLY)
                c = n if n < EARLY else next(late, None)
                if c is None:
                    continue
                evac(0, c, proj[:, c, :], (ACT.Copy, ACT.Silu, ACT.Sigmoid, ACT.Copy, ACT.Silu)[c // 4])
            act.wait_ge(s["s5_ysum"], 4)
            act.activation(uT, uT, ACT.Gelu).then_inc(s["s5_gelu"], 1)
            act.wait_ge(s["hg_f"], 4)
            act.wait_ge(s["hg_k"], 1)
            act.activation(fT, fT, ACT.Ln).then_inc(s["hg_ln"], 1)
            act.wait_ge(s["hg_cum"], 1)
            act.activation(eC, fT, ACT.Exp).then_inc(s["hg_exp"], 1)
            act.activation(kE, fT, ACT.Exp, scale=-1.0).then_inc(s["hg_exp"], 1)
            act.wait_ge(s["hg_dif"], 1)
            act.activation(kD, kD, ACT.Exp).then_inc(s["hg_exp"], 1)
            act.activation(totH, fT.rearrange("p h (c l) -> p h c l", l=HC)[:, :, :, HC - 1],
                           ACT.Exp).then_inc(s["hg_exp"], 1)
            for n in range(4):
                act.wait_ge(s["s5_glu"], n + 1)
                act.activation(scr[:, n, :], ps[3 + n][:, :], ACT.Sigmoid).then_inc(s["s5_sig"], 1)
            for i in range(8):
                act.wait_ge(s["hg_tr"], i + 1)
                dst = (kTok if i < 4 else vTok)[:, i % 4]
                act.activation(dst, ps[3 + i % 4][:, :].rearrange("p (t d) -> p t d", t=TT),
                               ACT.Copy).then_inc(s["hg_trc"], 1)
            BA = (0, 1, 2, 7)
            act.wait_ge(s["mix_ready"], 4)
            for n in range(HG + 1):
                if n < HG:
                    act.wait_ge(s["hg_o"], n + 1)
                    act.activation(scr[:, n, :], ps[BA[n]][:, :], ACT.Square).then_inc(s["hg_sq"], 1)
                if n:
                    hd = n - 1
                    act.wait_ge(s["hg_sum"], hd + 1)
                    own.link(act.activation(kE[:, hd, :], ps[3 + hd][:, :], ACT.Ln, bias=eps_col))
                    act.activation(kE[:, hd, :], kE[:, hd, :], ACT.Exp, scale=-0.5).then_inc(s["hg_root"], 1)

            def peer(layer):
                norm_squares(layer + 1)
                c0 = STREAMS[f"wq{layer}"][0]

                def queries(g, par):
                    first = isinstance(g, int) and g == 0
                    lo = P if first else 0
                    for c in range(2):
                        act.wait_ge(s["acc_ready"], g * 2 + (c0 + c + 1))
                        act.activation(pq[:, par, c, lo:T], ps[c][:, 0:T - lo], ACT.Copy).then_inc(s["acc_free"], 1)
                    for b in range(2):
                        act.wait_ge(s["sc_mm"], g * 2 + (2 * PH * layer + b + 1))
                        alone()
                        t0 = 1 if first and b == 0 else 2 * b
                        dst = sc[:, 0:HEADS, :].rearrange("p (t g) k -> p t g k", t=TT)
                        dst = dst[:, t0:2 * b + 2, bass.ds(g, 1), :]
                        act.activation(dst.rearrange("p t g k -> p t (g k)"),
                                       ps[2 + b][:, 2 * NK * (t0 - 2 * b):].rearrange("p (t k) -> p t k", k=2 * NK),
                                       ACT.Copy).then_inc(s["sc_ready"], 1)
                    act.wait_ge(s["sc_ready"], g * 2 + (2 * PH * layer + 2))

                def stage(g, par):
                    if layer or not (isinstance(g, int) and g == 0):
                        act.wait_ge(s["ids_ready"], g + (HEADS + 1) * layer)
                    alone()
                    act.activation(sct[:, par, :, :].rearrange("p c k -> p (c k)"),
                                   sc[:, bass.ds(g, 1), :].rearrange("p a k -> p (a k)"),
                                   ACT.Copy).then_inc(s["sct_ready"], 1)

                def soft(g):
                    act.wait_ge(s["soft_in"], g + ((HEADS + 1) * layer + 1))
                    act.activation(soft_e, sel_v, ACT.Exp, bias=soft_m, accum_out=soft_s).then_inc(s["soft_exp"], 1)

                def head(g, par):
                    act.wait_ge(s["u_free"], g * TOPK + (TOPK * HEADS * layer + TOPK + NU))
                    act.activation(gelu[par], dots[par], ACT.Gelu).then_inc(s["gelu_ready"], 1)
                    act.wait_ge(s["w_ready"], g + (HEADS * layer + 1))
                    for k in range(TOPK):
                        act.wait_ge(s["v_free"], g * TOPK + (TOPK * HEADS * layer + k + 1))
                        act.activation(diag[:, k, :], ident[:, :], ACT.Copy,
                                       scale=wgt[par][:, k:k + 1]).then_inc(s["diag_ready"], 1)

                for c in range(2):
                    act.wait_ge(s["q_first"], 2 * layer + c + 1)
                    act.activation(pq[:, 0, c, 0:P], ps[4 + c][:, 0:P], ACT.Copy).then_inc(s["q_first_copied"], 1)
                act.wait_ge(s["sc_first"], layer + 1)
                own.link(act.activation(sc[:, 0, :], ps[6][:, 0:2 * NK], ACT.Copy))
                stage(0, 0)
                own.link(act.activation(sc[:, HEADS, :], sc[:, 0, :], ACT.Copy))
                queries(0, 0)
                for n in range(2 * TT):
                    act.wait_ge(s["xt_tr"], 2 * TT * layer + n + 1)
                    act.activation(xtok[:, n // 2, T * (n % 2):T * (n % 2) + T], ps[6 + n % 2][:, :],
                                   ACT.Copy).then_inc(s["xt_copied"], 1)
                soft(0)

                def pair(g0, more=0, pre=(None, None)):
                    for par in range(2):
                        g = g0 + par
                        if more and not (more == 1 and par == 1):
                            queries(g + 1, 1 - par)
                        stage(g + 1, 1 - par)
                        if pre[par] is not None:
                            for j in range(NSLOT):
                                pre_evac(j, *pre[par])
                        head(g, par)
                        soft(g + 1)

                def pre_evac(j, e, raw, at):
                    act.wait_ge(s["acc_ready"], e * NSLOT + (STREAMS["od_pre"][0] + j + 1))
                    alone()
                    act.activation(raw[:, bass.ds(at + j, 1), 0:PRE].rearrange("p a t -> p (a t)"), ps[j % 2][:, 0:PRE],
                                   ACT.Copy).then_inc(s["acc_free"], 1)

                def finish(t):
                    act.wait_ge(s["v_free"], t * (TOPK * PH) + (TOPK * HEADS * layer + TOPK * PH + TOPK))
                    for i in range(2):
                        m = act.activation(ycur[:, T * i:T * i + T], ps[4 + i][:, :], ACT.Copy)
                    m.then_inc(s["y_copied"], 1)
                    act.wait_ge(s["hy_ready"], t + (TT * layer + 1))
                    alone()
                    for i in range(2):
                        m = act.activation(h[:, 4 * i:4 * i + 4, bass.ds(t * P, P)],
                                           ps[6 + i][:, :].rearrange("p (k t) -> p k t", k=4), ACT.Copy)
                    m.then_inc(s["peer_done"], 1)
                    for i in range(2):
                        m = act.activation(ysq[:, 4 * i:4 * i + 4, :],
                                           ps[6 + i][:, :].rearrange("p (k t) -> p k t", k=4), ACT.Square)
                    m.then_inc(s["tile_sq"], 1)
                    act.wait_ge(s["tile_sum"], t + (TT * layer + 1))
                    if not (isinstance(t, int) and t == 0):
                        act.wait_ge(s["tile_normed"], t + TT * layer)
                    own.link(act.activation(trt, ps[3][:, 0:P], ACT.Ln, bias=eps_col))
                    act.activation(trt, trt, ACT.Exp, scale=-0.5).then_inc(s["tile_root"], 1)

                with act.Fori(0, PH // 2 - 1) as p:
                    pair(p * 2, 2)
                pair(PH - 2, 1)
                finish(0)
                start = own.base + own.k
                with act.Fori(1, TT if layer else TT - 1) as t:
                    own.base, own.k = t + (start - 1), 0
                    with act.Fori(0, PH // 2) as p:
                        pair(t * PH + p * 2)
                    finish(t)
                own.base, own.k = start + (TT - 1 if layer else TT - 2), 0
                if layer == 0:
                    g0 = (TT - 1) * PH
                    pair(g0, pre=(None, (0, raw_v, 0)))
                    with act.Fori(1, PH // 2 - 1) as p:
                        pair(p * 2 + g0, pre=((p * 2 - 1, raw_q, (p - 1) * 4), (p * 2, raw_k, (p - 1) * 4)))
                    pair(g0 + PH - 2, pre=((5, raw_v, 4), None))
                    finish(TT - 1)

            peer(0)

            c0 = STREAMS["od_in"][0]
            ab = small_in("ab")

            def od_evac(i, j, raw, a):
                act.wait_ge(s["acc_ready"], i * NSLOT + (c0 + j + 1))
                alone()
                act.activation(raw[:, bass.ds(a * 4 + j, 1), PRE:T].rearrange("p a t -> p (a t)"), ps[j % 2][:, 0:P],
                               ACT.Copy).then_inc(s["acc_free"], 1)

            def od_silu(g):
                act.wait_ge(s["conv_done"], g + 1)
                return act.activation(conv[:, g * 4:g * 4 + 4, :], conv[:, g * 4:g * 4 + 4, :], ACT.Silu)

            act.wait_ge(s["ids_ready"], HEADS + 1)
            for j in range(NSLOT):
                od_evac(0, j, raw_v, 0)
            with act.Fori(0, 2) as a:
                for j in range(NSLOT):
                    od_evac(a * 2 + 1, j, raw_q, a)
                for j in range(NSLOT):
                    od_evac(a * 2 + 2, j, raw_k, a)
            for j in range(NSLOT):
                od_evac(5, j, raw_v, 1)
            own.link(od_silu(0))
            act.activation(scr[:, :, :], conv[:, 0:4, :], ACT.Square).then_inc(s["l2_sq"], 1)
            act.wait_ge(s["ba_mm"], 2)
            act.activation(beta_r, ps[7][0:GH, :], ACT.Sigmoid).then_inc(s["beta_ready"], 1)
            act.wait_ge(s["a_abs"], 1)
            act.activation(soft_r[1], soft_r[1], ACT.Exp, scale=-1.0)
            act.activation(cols[0:GH, 2:3], ab[0:GH, 0:1], ACT.Exp).then_inc(s["a_exp"], 1)
            act.wait_ge(s["a_one"], 1)
            act.activation(soft_r[1], soft_r[1], ACT.Ln).then_inc(s["a_ln"], 1)
            for g in range(4):
                act.wait_ge(s["l2_sum"], g + 1)
                for e in range(4):
                    m = act.activation(scr[:, e, :], ps[3 + e][:, :], ACT.Ln, bias=eps_col)
                own.link(m)
                act.activation(scr[:, :, :], scr[:, :, :], ACT.Exp, scale=-0.5).then_inc(s["l2_root"], 1)
                for e in range(2):
                    c = 2 * g + e
                    if g == 3:
                        od_silu(4 + e).then_inc(s["silu"], 1)
                    elif e == 0:
                        own.link(od_silu(g + 1))
                    else:
                        act.wait_ge(s["l2_done"], g + 1)
                        act.activation(scr[:, :, :], conv[:, g * 4 + 4:g * 4 + 8, :],
                                       ACT.Square).then_inc(s["l2_sq"], 1)
                    act.wait_ge(s["acc_ready"], c0 + 24 + c + 1)
                    act.activation(zT[:, c, :], ps[c % 2][:, :], ACT.Silu).then_inc(s["acc_free"], 1)
            act.wait_ge(s["col_tr"], 1)
            act.activation(cols[:, 64:128], ps[7][:, 0:64], ACT.Copy).then_inc(s["cols_ready"], 1)
            BA = (0, 1, 2, 7)
            for grp in range(2):
                hs = range(4 * grp, 4 * grp + 4)
                for hh in range(4):
                    act.wait_ge(s["bc_mm"], 4 * grp + hh + 1)
                    act.activation(qdT[:, hh, :], ps[3 + hh][:, :], ACT.Exp).then_inc(s["gq_exp"], 1)
                for hh in range(4):
                    act.wait_ge(s["lm_min"], 4 * grp + hh + 1)
                    act.activation(lmT[:, hh, :], lmT[:, hh, :], ACT.Exp).then_inc(s["lm_exp"], 1)
                hsl = slice(4 * grp, 4 * grp + 4)
                act.wait_ge(s["last_ready"], grp + 1)
                act.activation(kbe_c[:, :, hsl], dec_c[:, :, hsl], ACT.Exp)
                act.activation(tail_c[:, :, hsl], tail_c[:, :, hsl], ACT.Exp)
                act.activation(tot_c[:, hsl, :], last_c[:, hsl, :], ACT.Exp).then_inc(s["small_exp"], 1)
                act.wait_ge(s["scale_cols"], grp + 1)
                for hh, hd in enumerate(hs):
                    act.wait_ge(s["ktr_mm"], 4 * grp + hh + 1)
                    for t in range(TT):
                        m = act.activation(kbe[:, hh, t, :], ps[3 + hh][:, P * t:P * t + P], ACT.Copy,
                                           scale=kbe_c[:, t, hd:hd + 1])
                    m.then_inc(s["kbe_ready"], 1)
                for hh, hd in enumerate(hs):
                    act.wait_ge(s["vtr_mm"], 4 * grp + hh + 1)
                    for t in range(TT):
                        m = act.activation(vb[:, hh, t, :], ps[BA[hh]][:, P * t:P * t + P], ACT.Copy,
                                           scale=beta_c[:, t, hd:hd + 1])
                    m.then_inc(s["vb_ready"], 1)
                with act.Fori(1, 7) as l:
                    for hh in range(4):
                        act.wait_ge(s["x_mm"], l * 4 + (28 * grp + hh + 1))
                        act.activation(xs[:, hh, :], ps[BA[hh]][:, :], ACT.Copy).then_inc(s["xs_copied"], 1)
                for hh in range(4):
                    act.wait_ge(s["kc_mm"], 4 * grp + hh + 1)
                    act.activation(kbT[:, hh, :], ps[BA[hh]][:, :], ACT.Copy, scale=-1.0).then_inc(s["kc_ready"], 1)
                for t in range(TT):
                    for hh in range(4):
                        act.wait_ge(s["vn_mm"], (grp * TT + t) * 4 + hh + 1)
                        act.activation(vnew[:, hh, :], ps[BA[hh]][:, 0:P], ACT.Copy).then_inc(s["vn_ready"], 1)
                for hh in range(4):
                    act.wait_ge(s["go_done"], 4 * grp + hh + 1)
                    act.activation(scr[:, hh, :], ps[3 + hh][:, :], ACT.Square).then_inc(s["g_sq"], 1)
                for hh in range(4):
                    act.wait_ge(s["g_sum"], 4 * grp + hh + 1)
                    own.link(act.activation(lmT[:, hh, :], ps[BA[hh]][:, :], ACT.Ln, bias=eps_col))
                    act.activation(lmT[:, hh, :], lmT[:, hh, :], ACT.Exp, scale=-0.5).then_inc(s["g_root"], 1)
            peer(1)

        @block.vector
        def _(dve):
            own = Chain(dve, s["dve_own"])
            link = own.link

            def alone():
                dve.sem_inc(s["dve_passed"], 1)

            tt, ts = dve.tensor_tensor, dve.tensor_scalar
            stt = dve.scalar_tensor_tensor

            dve.memset(eps_col, EPS).then_inc(s["acc_free"], 2)
            dve.wait_ge(s["const_pool"], 1)
            row = scr[:, 0, 0:P].bitcast(U32)
            col = scr[:, 0, P:2 * P].bitcast(U32)
            xr = scr[:, 0, 2 * P:3 * P].bitcast(U32)
            sh = scr[:, 0, 3 * P:4 * P].bitcast(U32)
            link(tt(xr, row, col, ALU.bitwise_xor))
            link(ts(sh, xr, 5, None, ALU.logical_shift_right))
            link(ts(sh.bitcast(F32), sh, 0, None, ALU.is_equal))
            link(tt(mask32[:, :], sh.bitcast(F32), maskc[:, :], ALU.mult))
            dve.memset(rt[:, :], 0.0).then_inc(s["masks_built"], 1)
            dve.wait_ge(s["masks_built"], 1)

            def norm_apply(n, m, dst):
                dve.wait_ge(s["root_ready"], m + 1)
                lo = P if m else 0
                if m:
                    for k in range(DC):
                        q = stt(dst[:, k, 0:P], h[:, k, 0:P], norm_w[:, n, k:k + 1], rt[:, 0:P], ALU.mult, ALU.mult)
                    q.then_inc(s["hn_first"], 1)
                for k in range(DC):
                    stt(dst[:, k, lo:T], h[:, k, lo:T], norm_w[:, n, k:k + 1], rt[:, lo:T], ALU.mult,
                        ALU.mult).then_inc(s["hn_ready"], 1)

            dve.wait_ge(s["small_loaded"], 16)
            norm_apply(0, 0, hn)
            lb = small_in("lb").rearrange("p (r c) -> p r c", r=2)
            le = cols[:, 4:12].rearrange("p (r c) -> p r c", r=2)
            lbm = cols[:, 544:548]
            lbv, oml = cols[:, 548:552], cols[:, 552:556]
            link(tt(lbm, lb[:, 0], lb[:, 1], ALU.max))
            tt(le[:, 0], lb[:, 0], lbm, ALU.subtract)
            link(tt(le[:, 1], lb[:, 1], lbm, ALU.subtract))
            dve.memset(cols[:, 1:2], 0.0).then_inc(s["lb_d"], 1)
            are, aim = small_in("s5_are"), small_in("s5_aim")
            dt_, mag, th = cols[:, 16:32], cols[:, 32:48], cols[:, 48:64]
            c1, s1 = cols[:, 128:144], cols[:, 144:160]
            sn_h, sn = cols[:, 416:432], cols[:, 432:448]
            t0, t1, t2, den = (cols[:, 448 + 16 * i:464 + 16 * i] for i in range(4))
            dve.wait_ge(s["s5_trig_exp"], 1)
            tt(mag, are, dt_, ALU.mult).then_inc(s["s5_theta"], 1)
            link(tt(th, aim, dt_, ALU.mult))
            link(ts(t0, th, 1.0 / 6.283185307179586, ROUND, ALU.mult, ALU.add))
            link(ts(t0, t0, -ROUND, None, ALU.add))
            link(stt(t1, t0, -TWO_PI_HI, th, ALU.mult, ALU.add))
            link(stt(t1, t0, -TWO_PI_LO, t1, ALU.mult, ALU.add))
            link(ts(t1, t1, -3.1415925, 3.1415925, ALU.max, ALU.min))
            ts(sn_h, t1, 0.5, None, ALU.mult)
            dve.tensor_copy(sn, t1).then_inc(s["s5_theta"], 1)
            dve.wait_ge(s["s5_trig"], 1)
            link(stt(t0, sn_h, -2.0, sn_h, ALU.mult, ALU.mult))
            dve.tensor_copy(s1, sn)
            link(ts(c1, t0, 1.0, None, ALU.add))
            for m in range(9):
                if m:
                    pc, psn = cols[:, 96 + 32 * m:112 + 32 * m], cols[:, 112 + 32 * m:128 + 32 * m]
                    nco, nsn = cols[:, 128 + 32 * m:144 + 32 * m], cols[:, 144 + 32 * m:160 + 32 * m]
                    tt(t0, pc, pc, ALU.mult)
                    tt(t1, psn, psn, ALU.mult)
                    link(stt(nsn, pc, 2.0, psn, ALU.mult, ALU.mult))
                    link(tt(nco, t0, t1, ALU.subtract))
                    tt(t0, nco, nco, ALU.mult)
                    link(tt(t1, nsn, nsn, ALU.mult))
                    link(tt(t0, t0, t1, ALU.add))
                    link(ts(t0, t0, -0.5, 1.5, ALU.mult, ALU.add))
                    tt(nco, nco, t0, ALU.mult)
                    link(tt(nsn, nsn, t0, ALU.mult))
            dve.memset(tab_c[:, :, 0:1], 1.0)
            link(dve.memset(tab_s[:, :, 0:1], 0.0))
            dve.memset(t2, 0.0).then_inc(s["s5_ctab"], 9)
            dve.wait_ge(s["s5_ctab"], 9)
            for m in range(9):
                w = 1 << m
                if m:
                    dve.wait_ge(s["tab_pool"], m)
                step = min(w, 128)
                cmb = cols[:, 128 + 32 * m:144 + 32 * m].unsqueeze(2).to_broadcast([P, ST, step])
                smb = cols[:, 144 + 32 * m:160 + 32 * m].unsqueeze(2).to_broadcast([P, ST, step])
                for a in range(0, w, step):
                    tmp = s5t(0, step)
                    tt(tab_c[:, :, w + a:w + a + step], tab_c[:, :, a:a + step], cmb, ALU.mult)
                    link(tt(tmp, tab_s[:, :, a:a + step], smb, ALU.mult))
                    last = tt(tab_c[:, :, w + a:w + a + step], tab_c[:, :, w + a:w + a + step], tmp, ALU.subtract)
                    if a + step < w:
                        link(last)
                last.then_inc(s["tab_dve"], 1)
                dve.wait_ge(s["tab_dve"], m + 1)
            dve.wait_ge(s["s5_trig_exp"], 2)
            cr, ci = cols[:, 512:528], cols[:, 528:544]
            tt(t0, mag, c1, ALU.mult)
            tt(t1, mag, s1, ALU.mult)
            tt(t2, are, are, ALU.mult)
            link(tt(den, aim, aim, ALU.mult))
            ts(t0, t0, -1.0, None, ALU.add)
            link(tt(den, den, t2, ALU.add))
            link(dve.reciprocal(den, den))
            tt(cr, t0, are, ALU.mult)
            link(tt(t2, t1, aim, ALU.mult))
            link(tt(cr, cr, t2, ALU.add))
            tt(cr, cr, den, ALU.mult)
            tt(ci, t1, are, ALU.mult)
            link(tt(t2, t0, aim, ALU.mult))
            link(tt(ci, ci, t2, ALU.subtract))
            link(tt(ci, ci, den, ALU.mult))
            dve.wait_ge(s["bc_loaded"], 32)
            dve.wait_ge(s["tab_pool"], 9)
            crb = cr.unsqueeze(2).to_broadcast([P, ST, 32])
            cib = ci.unsqueeze(2).to_broadcast([P, ST, 32])
            pr = [tab_t[:, 0, 512 * i:512 * i + 512].rearrange("p (a b) -> p a b", a=ST) for i in range(4)]
            tt(pr[0], cw[:, 0], crb, ALU.mult)
            tt(pr[1], cw[:, 1], cib, ALU.mult)
            tt(pr[2], cw[:, 0], cib, ALU.mult)
            link(tt(pr[3], cw[:, 1], crb, ALU.mult))
            tt(cw[:, 0], pr[0], pr[1], ALU.subtract)
            link(tt(cw[:, 1], pr[2], pr[3], ALU.add))
            link(ts(cw[:, 1], cw[:, 1], -1.0, None, ALU.mult))
            dve.memset(t0, 0.0).then_inc(s["s5_wc"], 1)

            dve.wait_ge(s["lb_e"], 1)
            link(tt(lbm, le[:, 0], le[:, 1], ALU.add))
            link(dve.reciprocal(lbm, lbm))
            link(tt(lbv, le[:, 0], lbm, ALU.mult))
            link(ts(oml, lbv, -1.0, 1.0, ALU.mult, ALU.add))

            def s5_wr(st):
                W = s5w[st % 3]
                dve.wait_ge(s["s5_bcopy"], 2 * st + 2)
                if st >= 3:
                    dve.wait_ge(s["s5_y"], st - 2)
                tt(W[4], W[0], tab_c[:, st, :], ALU.mult)
                link(tt(W[2], W[1], tab_s[:, st, :], ALU.mult))
                tt(W[2], W[4], W[2], ALU.add).then_inc(s["s5_wr"], 1)

            def s5_sum(q):
                dve.wait_ge(s["s5_y"], 4 * q + 4)
                stt(uT[:, q, :], uT[:, q, :], small_in("s5_d")[:, q:q + 1], ps[7][:, :], ALU.mult,
                    ALU.add).then_inc(s["s5_ysum"], 1)

            s5_wr(0)
            for st in range(ST):
                W = s5w[st % 3]
                magb = mag[:, st:st + 1].to_broadcast([P, T])
                dve.wait_ge(s["s5_wr"], st + 1)
                dve.tensor_tensor_scan(W[2], magb, W[2], 0.0, ALU.mult, ALU.add).then_inc(s["s5_scan"], 1)
                dve.wait_ge(s["s5_wi"], st + 1)
                dve.tensor_tensor_scan(W[3], magb, W[3], 0.0, ALU.mult, ALU.add).then_inc(s["s5_scan"], 1)
                dve.wait_ge(s["s5_scan"], 2 * st + 2)
                tt(W[0], W[2], tab_c[:, st, :], ALU.mult)
                stt(W[4], W[3], -1.0, tab_s[:, st, :], ALU.mult, ALU.mult).then_inc(s["s5_pr"], 1)
                if st + 1 < ST:
                    s5_wr(st + 1)
                if st % 4 == 0 and st:
                    s5_sum(st // 4 - 1)
                if st == 6:
                    dve.wait_ge(s["acc_free"], 12 + 2)
                    for hd in range(HG):
                        ts(fT[:, hd, :], fT[:, hd, :], oml[:, hd:hd + 1], lbv[:, hd:hd + 1], ALU.mult,
                           ALU.add).then_inc(s["hg_f"], 1)
            s5_sum(3)
            m32 = rt[:, :]
            link(dve.memset(m32, 1.0))
            link(dve.memset(m32.rearrange("p (c l) -> p c l", l=HC)[:, :, 0:1], 0.0))
            dve.wait_ge(s["hg_ln"], 1)
            for hd in range(HG):
                link(dve.tensor_tensor_scan(fT[:, hd, :], m32, fT[:, hd, :], 0.0, ALU.mult, ALU.add))
            f4 = fT.rearrange("p h (c l) -> p (h c) l", l=HC)
            d4 = kD.rearrange("p h (c l) -> p (h c) l", l=HC)
            tt(d4, f4[:, :, HC - 1:HC].to_broadcast([P, HG * NCH, HC]), f4, ALU.subtract).then_inc(s["hg_dif"], 1)
            dve.memset(cols[:, 1:2], 0.0).then_inc(s["hg_cum"], 1)
            dve.wait_ge(s["hg_exp"], 1)
            stt(qT, qT, HGRN_SCALE, eC, ALU.mult, ALU.mult).then_inc(s["hg_ke"], 1)
            dve.wait_ge(s["hg_exp"], 2)
            dve.wait_ge(s["hg_k"], 1)
            tt(kE, kA, kE, ALU.mult).then_inc(s["hg_ke"], 1)
            dve.wait_ge(s["hg_ke"], 2)
            BA = (0, 1, 2, 7)
            for hd in range(HG):
                dve.wait_ge(s["hg_att"], hd + 1)
                tt(eC[:, hd, :].rearrange("p (t x) -> p t x", t=TT),
                   ps[BA[hd]][:, :].rearrange("p (t x) -> p t x", t=TT),
                   mask32[:, :].unsqueeze(1).to_broadcast([P, TT, P]), ALU.mult).then_inc(s["hg_attm"], 1)
            dve.wait_ge(s["hg_exp"], 4)
            dve.wait_ge(s["s5_gelu"], 1)
            for n in range(4):
                dve.wait_ge(s["s5_sig"], n + 1)
                if n == 0:
                    dve.wait_ge(s["s5_glu"], 4)
                tt(uT[:, n, :], uT[:, n, :], scr[:, n, :], ALU.mult).then_inc(s["mix_ready"], 1)

            for n in range(NCH - 1):
                t, j = n // 4, n % 4
                dve.wait_ge(s["hg_ds"], t + 1)
                for hd in range(HG):
                    ds = ps[(BA if t % 2 else (3, 4, 5, 6))[j]][:, P * hd:P * hd + P]
                    if n == 0:
                        m = dve.tensor_copy(statesA[hd][:, 1, :], ds)
                    else:
                        m = stt(statesA[hd][:, n + 1, :], statesA[hd][:, n, :], totH[:, hd, n:n + 1], ds, ALU.mult,
                                ALU.add)
                    m.then_inc(s["hg_st"], 1)
                dve.wait_ge(s["hg_st"], 4 * n + 4)
            for hd in range(HG):
                dve.wait_ge(s["hg_root"], hd + 1)
                link(stt(kA[:, hd, :], ps[BA[hd]][:, :], gn_col[:, 0:1], kE[:, hd, :], ALU.mult, ALU.mult))
                tt(qT[:, hd, :], kA[:, hd, :], gT[:, hd, :], ALU.mult).then_inc(s["mix_ready"], 1)

            def add_stream(name):
                c0, n, _ = STREAMS[name]
                with dve.Fori(0, n // NSLOT) as i:
                    for j in range(NSLOT):
                        dve.wait_ge(s["acc_ready"], i * NSLOT + (c0 + j + 1))
                        hc = h[:, bass.ds(i * NSLOT + j, 1), :].rearrange("p a t -> p (a t)")
                        tt(hc, hc, ps[j % 2][:, :], ALU.add).then_inc(s["acc_free"], 1)

            def peer(layer):
                norm_apply(2 * layer + 1, layer + 1, phn)

                def route(g, par):
                    dve.wait_ge(s["sct_ready"], g + ((HEADS + 1) * layer + 1))
                    alone()
                    for lo in (0, 8):
                        for c in range(2):
                            m = dve.max(top_v[:, c, lo:lo + 8], sct[:, par, c, :])
                        link(m)
                        alone()
                        for c in range(2):
                            m = dve.max_index(top_i[:, c, lo:lo + 8], top_v[:, c, lo:lo + 8], sct[:, par, c, :])
                        if lo == 0:
                            link(m)
                            alone()
                            for c in range(2):
                                m = dve.match_replace(sct[:, par, c, :], top_v[:, c, 0:8], sct[:, par, c, :], LOWEST)
                        link(m)
                        if lo == 0:
                            alone()
                    dve.tensor_copy(top_f, top_i)
                    link(tt(cand.rearrange("p (a b) -> p a b", a=TOPK),
                            top_v[:, 0, :].unsqueeze(2).to_broadcast([P, TOPK, TOPK]),
                            top_v[:, 1, :].unsqueeze(1).to_broadcast([P, TOPK, TOPK]), ALU.add))
                    alone()
                    link(dve.max(sel_v[:, 0:8], cand))
                    alone()
                    link(dve.max_index(sel_p[:, 0:8], sel_v[:, 0:8], cand))
                    ts(soft_m, sel_v[:, 0:1], -1.0, None, ALU.mult)
                    link(dve.match_replace(cand, sel_v[:, 0:8], cand, LOWEST))
                    alone()
                    dve.max(sel_v[:, 8:16], cand).then_inc(s["soft_in"], 1)
                    dve.wait_ge(s["soft_in"], g + ((HEADS + 1) * layer + 1))
                    alone()
                    link(dve.max_index(sel_p[:, 8:16], sel_v[:, 8:16], cand))
                    ts(sel_a, sel_p, 4, None, ALU.logical_shift_right)
                    link(ts(sel_b, sel_p, TOPK - 1, None, ALU.bitwise_and))
                    dve.tensor_copy(pos_a, sel_a)
                    link(dve.tensor_copy(pos_b, sel_b))
                    for pos, dst, c in ((pos_a, exp_a, 0), (pos_b, exp_b, 1)):
                        link(tt(hot, pos.unsqueeze(2).to_broadcast([P, TOPK, TOPK]),
                                iota16[:, :].unsqueeze(1).to_broadcast([P, TOPK, TOPK]), ALU.is_equal))
                        link(tt(hot, hot, top_f[:, c, :].unsqueeze(1).to_broadcast([P, TOPK, TOPK]), ALU.mult))
                        link(dve.tensor_reduce(dst, hot, AX.X, ALU.add))
                    link(stt(exp_a, exp_a, float(NK), exp_b, ALU.mult, ALU.add))
                    link(ts(ids[par], exp_a, float(layer * E), None, ALU.add))
                    dve.wait_ge(s["soft_exp"], g + ((HEADS + 1) * layer + 1))
                    link(dve.reciprocal(soft_s, soft_s))
                    ts(gate[par], soft_e, soft_s, None, ALU.mult).then_inc(s["ids_ready"], 1)

                def head(g, par):
                    for k in range(TOPK):
                        dve.wait_ge(u_arrived[k % NU],
                                    (g * (TOPK // NU) + (HEADS * layer * (TOPK // NU) + k // NU + 1)) * 16)
                        dve.tensor_tensor_reduce(uring[:, k % NU, :], uring[:, k % NU, :], xcur, 1.0, 0.0, ALU.mult,
                                                 ALU.add, dots[par][:, k:k + 1]).then_inc(s["u_free"], 1)
                    dve.wait_ge(s["gelu_ready"], g + (HEADS * layer + 1))
                    dve.wait_ge(s["ids_ready"], g + ((HEADS + 1) * layer + 1))
                    tt(wgt[par], gelu[par], gate[par], ALU.mult).then_inc(s["w_ready"], 1)

                route(0, 0)
                dve.wait_ge(s["xt_copied"], 2 * TT * (layer + 1))
                tile_links, pair_links = 1, 2 * ROUTE_LINKS
                per_tile = tile_links + (PH // 2) * pair_links
                start = own.base + own.k

                def apply(t):
                    dve.wait_ge(s["tile_root"], t + (TT * layer + 1))
                    alone()
                    for k in range(DC):
                        m = stt(phn[:, k, bass.ds(t * P, P)], h[:, k, bass.ds(t * P, P)],
                                norm_w[:, 2 * layer + 2, k:k + 1], trt, ALU.mult, ALU.mult)
                    m.then_inc(s["tile_normed"], 1)

                def pair(t, p):
                    own.base, own.k = t * per_tile + p * pair_links + (start + tile_links), 0
                    for par in range(2):
                        g = t * PH + p * 2 + par
                        head(g, par)
                        route(g + 1, 1 - par)
                        if isinstance(p, int) and par == 0:
                            apply(t - 1)
                    assert own.k == pair_links, own.k

                def tile_input(t):
                    own.base, own.k = t * per_tile + start, 0
                    link(dve.tensor_copy(xcur, xtok[:, bass.ds(t, 1), :].rearrange("p a d -> p (a d)")))
                    alone()

                tile_input(0)
                with dve.Fori(0, PH // 2) as p:
                    pair(0, p)
                with dve.Fori(1, TT) as t:
                    tile_input(t)
                    pair(t, 0)
                    with dve.Fori(1, PH // 2) as p:
                        pair(t, p)
                own.base, own.k = start + TT * per_tile, 0
                apply(TT - 1)

            dve.memset(cols[:, 1:2], 0.0).then_inc(s["u_free"], NU)
            dve.memset(cols[:, 2:3], 0.0).then_inc(s["v_free"], TOPK)
            add_stream("ev_out")
            peer(0)

            row = mask_w[:, 0, 0:P].bitcast(U32)
            col = mask_w[:, 0, P:2 * P].bitcast(U32)
            xr = mask_w[:, 0, 2 * P:3 * P].bitcast(U32)
            sh = mask_w[:, 0, 3 * P:4 * P].bitcast(U32)
            up, dn, shf = mask_w[:, 1, 0:P], mask_w[:, 1, P:2 * P], mask_w[:, 1, 2 * P:3 * P]
            dve.wait_ge(s["lm_iota"], 1)
            tt(xr, row, col, ALU.bitwise_xor)
            tt(up, row, col, ALU.is_lt)
            link(tt(dn, row, col, ALU.is_gt))
            for l in range(7):
                link(ts(sh, xr, l, None, ALU.logical_shift_right))
                link(ts(shf, sh, 1, None, ALU.is_equal))
                tt(maskl[:, 0, l, :], shf, dn, ALU.mult)
                link(tt(maskl[:, 1, l, :], shf, up, ALU.mult))

            def conv_group(raw, part, a, need):
                dve.wait_ge(s["acc_free"], need)
                for j in (3, 2, 1, 0):
                    d = 3 - j
                    for e in range(4):
                        c = bass.ds(a * 4 + (8 * part + e), 1)
                        w = conv_w[:, c, j:j + 1].rearrange("p a b -> p (a b)")
                        src = raw[:, bass.ds(a * 4 + e, 1), 0:T - d].rearrange("p a t -> p (a t)")
                        dst = conv[:, c, d:T].rearrange("p a t -> p (a t)")
                        m = ts(dst, src, w, None, ALU.mult) if d == 0 else stt(dst, src, w, dst, ALU.mult, ALU.add)
                    if j:
                        link(m)
                m.then_inc(s["conv_done"], 1)

            def unit_length(g, scale):
                dve.wait_ge(s["l2_root"], g + 1)
                qk = conv[:, bass.ds(g * 4, 4), :]
                stt(qk, qk, scale, scr[:, :, :], ALU.mult, ALU.mult).then_inc(s["l2_done"], 1)

            done = STREAMS["od_in"][0] + 2
            start = own.base + own.k
            with dve.Fori(0, 2) as a:
                own.base, own.k = a * 3 + start, 0
                conv_group(raw_q, 0, a, a * 8 + (done + 8))
            with dve.Fori(0, 2) as a:
                own.base, own.k = a * 3 + (start + 6), 0
                conv_group(raw_k, 1, a, a * 8 + (done + 12))
            own.base, own.k = start + 12, 0

            ab = small_in("ab")
            dve.wait_ge(s["ba_mm"], 2)
            link(ts(soft_r[0], ps[2][0:GH, :], ab[0:GH, 1:2], None, ALU.add))
            stt(soft_r[1], soft_r[0], -1.0, soft_r[0], ALU.mult, ALU.max).then_inc(s["a_abs"], 1)
            dve.memset(soft_r[3], 1.0)
            link(ts(soft_r[0], soft_r[0], 0.0, None, ALU.max))
            dve.memset(soft_r[3].rearrange("p (t x) -> p t x", t=TT)[:, :, 0:1], 0.0)
            dve.wait_ge(s["a_exp"], 1)
            ts(soft_r[1], soft_r[1], 1.0, None, ALU.add).then_inc(s["a_one"], 1)
            link(ts(cols[0:GH, 2:3], cols[0:GH, 2:3], -1.0, None, ALU.mult))
            dve.wait_ge(s["a_ln"], 1)
            link(tt(soft_r[0], soft_r[0], soft_r[1], ALU.add))
            link(ts(soft_r[0], soft_r[0], cols[0:GH, 2:3], None, ALU.mult))
            dve.tensor_tensor_scan(dec_r, soft_r[3], soft_r[0], 0.0, ALU.mult, ALU.add).then_inc(s["dec_ready"], 1)

            start = own.base + own.k
            with dve.Fori(0, 2) as a:
                own.base, own.k = a * 3 + start, 0
                unit_length(a, GDN_SCALE)
                conv_group(raw_v, 2, a, done + 24)
            own.base, own.k = start + 6, 0
            with dve.Fori(2, 4) as g:
                unit_length(g, 1.0)

            for grp in range(2):
                hs = range(4 * grp, 4 * grp + 4)
                dve.wait_ge(s["cols_ready"], 1)
                dve.wait_ge(s["l2_done"], 4)
                for hh, hd in enumerate(hs):
                    dve.wait_ge(s["bc_mm"], 4 * grp + hh + 1)
                    tt(kbT[:, hh, :], conv[:, GH + hd, :], ps[BA[hh]][:, :], ALU.mult).then_inc(s["kb_ready"], 1)
                    dve.wait_ge(s["gq_exp"], 4 * grp + hh + 1)
                    dve.tensor_copy(last_c[:, hd, :], ps[3 + hh][:, :].rearrange("p (t x) -> p t x", t=TT)[:, :, P - 1])
                    for t in range(TT):
                        m = ts(lmT[:, hh, P * t:P * t + P], ps[3 + hh][:, P * t:P * t + P], dec_c[:, t, hd:hd + 1], 0.0,
                               ALU.subtract, ALU.min)
                    m.then_inc(s["lm_min"], 1)
                dve.wait_ge(s["lm_min"], 4 * grp + 4)
                hsl = slice(4 * grp, 4 * grp + 4)
                tt(tail_c[:, :, hsl], last_c[:, hsl, :].rearrange("p h t -> p t h"), dec_c[:, :, hsl],
                   ALU.subtract).then_inc(s["last_ready"], 1)
                dve.wait_ge(s["small_exp"], grp + 1)
                tt(kbe_c[:, :, hsl], kbe_c[:, :, hsl], beta_c[:, :, hsl], ALU.mult).then_inc(s["scale_cols"], 1)
                for hh, hd in enumerate(hs):
                    dve.wait_ge(s["gq_exp"], 4 * grp + hh + 1)
                    tt(qdT[:, hh, :], conv[:, hd, :], qdT[:, hh, :], ALU.mult)
                for hh in range(4):
                    dve.wait_ge(s["kk_mm"], 4 * grp + hh + 1)
                    dve.wait_ge(s["lm_exp"], 4 * grp + hh + 1)
                    stt(negA[:, hh, :], ps[BA[hh]][:, :], -1.0, lmT[:, hh, :], ALU.mult,
                        ALU.mult).then_inc(s["negA_ready"], 1)
                for hh, hd in enumerate(hs):
                    dve.wait_ge(s["kbe_ready"], 4 * grp + hh + 1)
                    for t in range(TT):
                        m = ts(ktail[:, hh, t, :], ps[3 + hh][:, P * t:P * t + P], tail_c[:, t, hd:hd + 1], None,
                               ALU.mult)
                    m.then_inc(s["ktail_ready"], 1)
                def update(dst, hh, mask, src):
                    return dve.copy_predicated(dst[:, hh, :].rearrange("p (t x) -> p t x", t=TT),
                                               mask.bitcast(U32).unsqueeze(1).to_broadcast([P, TT, P]),
                                               src.rearrange("p (t x) -> p t x", t=TT))

                dve.wait_ge(s["eye_ready"], grp + 1)
                for hh in range(4):
                    dve.wait_ge(s["x_mm"], 28 * grp + hh + 1)
                    update(inv, hh, maskl[:, 0, 0, :], ps[BA[hh]][:, :])
                    update(invT, hh, maskl[:, 1, 0, :], negA[:, hh, :]).then_inc(s["wt_done"], 1)
                dve.wait_ge(s["wt_done"], 28 * grp + 4)
                start = own.base + own.k
                with dve.Fori(1, 6) as l:
                    own.base, own.k = l + (start - 1), 0
                    link(dve.tensor_copy(mcur, maskl[:, :, bass.ds(l, 1), :].rearrange("p a b x -> p a (b x)")))
                    for hh in range(4):
                        dve.wait_ge(s["y_mm"], l * 4 + (24 * grp + hh - 3))
                        alone()
                        update(inv, hh, mcur[:, 0, :], ps[3 + hh % 2][:, :])
                        update(invT, hh, mcur[:, 1, :], ps[5 + hh % 2][:, :]).then_inc(s["wt_done"], 1)
                    dve.wait_ge(s["wt_done"], l * 4 + (28 * grp + 4))
                    alone()
                own.base, own.k = start + 5, 0
                for hh in range(4):
                    dve.wait_ge(s["y_mm"], 24 * grp + 20 + hh + 1)
                    update(invT, hh, maskl[:, 1, 6, :], ps[5 + hh % 2][:, :]).then_inc(s["wt_done"], 1)
                dve.wait_ge(s["wt_done"], 28 * grp + 28)
                for hh in range(4):
                    dve.wait_ge(s["qk_mm"], 4 * grp + hh + 1)
                    tt(negA[:, hh, :], ps[3 + hh][:, :], lmT[:, hh, :], ALU.mult).then_inc(s["att_raw"], 1)
                for t in range(TT - 1):
                    for hh, hd in enumerate(hs):
                        n = (grp * 3 + t) * 4 + hh + 1
                        dve.wait_ge(s["gds_mm"], n)
                        ds = ps[BA[hh]][:, P:2 * P]
                        if t:
                            m = stt(gstate[:, hh, :], gstate[:, hh, :], tot_c[:, hd, t:t + 1], ds, ALU.mult, ALU.add)
                        else:
                            m = dve.tensor_copy(gstate[:, hh, :], ds)
                        m.then_inc(s["gs_ready"], 1)
                    dve.wait_ge(s["gs_ready"], (grp * 3 + t) * 4 + 4)
                for hh, hd in enumerate(hs):
                    dve.wait_ge(s["g_root"], 4 * grp + hh + 1)
                    link(stt(xs[:, 2, :], ps[3 + hh][:, :], gn_col[:, 1:2], lmT[:, hh, :], ALU.mult, ALU.mult))
                    tt(zT[:, hd, :], xs[:, 2, :], zT[:, hd, :], ALU.mult).then_inc(s["mix_ready"], 1)
                    dve.wait_ge(s["mix_ready"], 8 + 4 * grp + hh + 1)
            add_stream("od_out")
            peer(1)


def host_layout(i):
    import numpy as np
    f = {k: np.asarray(v) for k, v in i.items()}

    def chunks(w):
        k, n = w.shape
        return w.reshape(k // P, P, n // P, P).transpose(2, 1, 0, 3)

    def rows(w, c):
        return np.moveaxis(w.reshape((c, P) + w.shape[1:]), 0, 1)

    ev = f["ev_in_w"][0]
    ev = np.concatenate([ev[:, 2048:2560], ev[:, 0:2048]], axis=1)
    od = f["od_in_w"][0]
    halves = [od[:, 512 * i:512 * i + 512] for i in (4, 0, 2, 1, 3, 5, 6, 7)]
    wall = np.concatenate([chunks(w) for w in (ev, f["ev_out_w"][0], f["peer_wq"][0], *halves,
                                               f["od_out_w"][0], f["peer_wq"][1])])
    norm = np.concatenate([f["norm_mix_w"][0:1], f["norm_ffn_w"][0:1], f["norm_mix_w"][1:2],
                           f["norm_ffn_w"][1:2], f["norm_out_w"][None]])
    b = np.zeros((4, 2, 16, 2, 4, 2, 64), np.float32)
    c = np.zeros((2, 64, 2, ST, 2, 16), np.float32)
    for n, (bn, cn) in enumerate((("s5_b_re", "s5_c_re"), ("s5_b_im", "s5_c_im"))):
        bb = f[bn][0].reshape(4, 4, 2, 64, 16)
        cc = f[cn][0].reshape(ST, 2, 16, 64)
        for g in range(2):
            b[:, g, :, n, :, g, :] = bb[:, :, g].transpose(1, 3, 0, 2)
            c[g, :, n, :, g, :] = cc[:, g].transpose(2, 0, 1)
    ab = np.zeros((P, 2), np.float32)
    ab[0:GH, 0], ab[0:GH, 1] = f["gdn_a_log"][0], f["gdn_dt_bias"][0]
    parts = {
        "norm_w": norm.reshape(5, DC, P).transpose(2, 0, 1),
        "s5_are": f["s5_a_re"][0].reshape(ST, P).T,
        "s5_aim": f["s5_a_im"][0].reshape(ST, P).T,
        "s5_ldt": np.repeat(f["s5_log_dt"][0], 64).reshape(ST, P).T,
        "s5_d": f["s5_d"][0].reshape(4, P).T,
        "lb": f["hgrn_lb"].reshape(2, 4, P).transpose(2, 0, 1),
        "gn": np.stack([f["hgrn_gn_w"][0], f["gdn_gn_w"][0]], axis=1),
        "conv": f["gdn_conv_w"][0].reshape(4, 24, P).transpose(2, 1, 0),
        "ab": ab,
        "ba_w": rows(od[:, 4096:4112], DC),
        "keys": f["peer_sub_keys"].transpose(3, 0, 1, 2),
    }
    small = np.concatenate([parts[n].reshape(P, w) for n, w in SMALL], axis=1)
    return {
        "xT": rows(f["x"][0].T, DC), "wall": wall, "glu_w": rows(f["s5_glu_w"][0], 4),
        "s5_b": b.reshape(P, 2, 4, P), "s5_c": c.reshape(P, 2, ST, 32), "small": small,
        "u_tab": f["peer_u"].reshape(2 * E, D), "v_tab": f["peer_v"].reshape(2 * E, D),
    }


def kernel(**inputs):
    import numpy as np
    import concourse.bacc as bacc
    from concourse.bass_utils import run_bass_kernel_spmd

    nc = bacc.Bacc("TRN2", target_bir_lowering=False, num_devices=1)
    arrays = {n: np.ascontiguousarray(a) for n, a in host_layout(inputs).items()}
    args = [nc.dram_tensor(n, a.shape, mybir.dt.from_np(a.dtype), kind="ExternalInput").ap()
            for n, a in arrays.items()]
    out = nc.dram_tensor("out", (P, DC, T), F32, kind="ExternalOutput").ap()
    trunk(nc, *args, out)
    r = run_bass_kernel_spmd(nc, [arrays], core_ids=[0])
    got = r.results[0]["out"]
    return got.transpose(2, 1, 0).reshape(1, T, D)
```
